# Optimizing a Trainium2 kernel written in Bass

```python
import math
import jax
import jax.numpy as jnp
from jax import lax
import numpy as np

D_MODEL = 1024
BATCH = 1
SEQ = 256
DEPTH = 2

GRID_W = 64
CTX_LEN = 256
EPS = 1e-6
N_MOD = 6

MLA_HEADS = 4
Q_LORA = 256
KV_LORA = 128
QK_NOPE = 64
QK_ROPE = 32
V_HEAD = 64
MLA_WIDTH = MLA_HEADS * V_HEAD
MLA_SCALE = (QK_NOPE + QK_ROPE) ** -0.5
ROPE_THETA = 10000.0
Q_BLOCK = 128

SC_WIDTH = 256
SC_KERNEL = 3

SSD_HEADS = 8
SSD_HEAD_DIM = 64
SSD_WIDTH = SSD_HEADS * SSD_HEAD_DIM
SSD_GROUPS = 2
SSD_STATE = 64
SSD_CONV = 3
SSD_CHUNK = 128
SSD_GN = SSD_GROUPS * SSD_STATE
SSD_XBC = SSD_WIDTH + 2 * SSD_GN

D_MIX = MLA_WIDTH + SC_WIDTH + SSD_WIDTH
IN_MLA = Q_LORA + KV_LORA + QK_ROPE
IN_SC = 3 * SC_WIDTH
IN_SSD = SSD_WIDTH + SSD_XBC + 2 * SSD_HEADS
D_IN = IN_MLA + IN_SC + IN_SSD
D_FF = 4 * D_MODEL


def _rms_norm(x, g):
    xf = x.astype(jnp.float32)
    y = xf * lax.rsqrt(jnp.mean(xf * xf, axis=-1, keepdims=True) + EPS)
    return (y * g.astype(jnp.float32)).astype(x.dtype)

def _modulate(h, shift, scale):
    return h * (1 + scale) + shift

def _dwconv(x, w):
    k = w.shape[0]
    return lax.conv_general_dilated(
        x, w[:, None, :].astype(x.dtype), window_strides=(1,),
        padding=[(k // 2, k // 2)], dimension_numbers=('NWC', 'WIO', 'NWC'),
        feature_group_count=x.shape[-1])

def _axial_rope_tables(rows):
    half = QK_ROPE // 2
    inv_freq = ROPE_THETA ** (-jnp.arange(0, half, 2, dtype=jnp.float32) / half)
    row = jnp.repeat(jnp.arange(rows, dtype=jnp.float32), GRID_W)
    col = jnp.tile(jnp.arange(GRID_W, dtype=jnp.float32), rows)
    ang_r = row[:, None] * inv_freq
    ang_c = col[:, None] * inv_freq
    ang = jnp.concatenate([ang_r, ang_r, ang_c, ang_c], axis=-1)
    return jnp.cos(ang), jnp.sin(ang)

def _apply_rope(x, cos, sin):
    xf = x.astype(jnp.float32)
    a, b, c, d = jnp.split(xf, 4, axis=-1)
    rot = jnp.concatenate([-b, a, -d, c], axis=-1)
    return (xf * cos + rot * sin).astype(x.dtype)

def _split_in(u):
    return u[..., :IN_MLA], u[..., IN_MLA:IN_MLA + IN_SC], u[..., IN_MLA + IN_SC:]

def _mla_kv(u, kv_g, w_ukv, rope):
    b, l, _ = u.shape
    ckv = _rms_norm(u[..., Q_LORA:Q_LORA + KV_LORA], kv_g)
    kv = (ckv @ w_ukv).reshape(b, l, MLA_HEADS, QK_NOPE + V_HEAD)
    k_nope, v = kv[..., :QK_NOPE], kv[..., QK_NOPE:]
    k_rope = u[..., Q_LORA + KV_LORA:]
    if rope is not None:
        k_rope = _apply_rope(k_rope, rope[0], rope[1])
    k_rope = jnp.broadcast_to(k_rope[:, :, None, :], (b, l, MLA_HEADS, QK_ROPE))
    return jnp.concatenate([k_nope, k_rope], axis=-1), v

def _mla_q(u, q_g, w_uq, rope):
    b, l, _ = u.shape
    cq = _rms_norm(u[..., :Q_LORA], q_g)
    q = (cq @ w_uq).reshape(b, l, MLA_HEADS, QK_NOPE + QK_ROPE)
    if rope is not None:
        q_rope = _apply_rope(q[..., QK_NOPE:], rope[0][:, None, :], rope[1][:, None, :])
        q = jnp.concatenate([q[..., :QK_NOPE], q_rope], axis=-1)
    return q

def _softmax_attend(q, k, v):
    s = jnp.einsum('bqhd,bkhd->bhqk', q, k).astype(jnp.float32) * MLA_SCALE
    p = jax.nn.softmax(s, axis=-1).astype(v.dtype)
    return jnp.einsum('bhqk,bkhd->bqhd', p, v)

def _blocked_attention(q, k, v):
    b, l, h, d = q.shape
    nb = l // Q_BLOCK
    qb = q.reshape(b, nb, Q_BLOCK, h, d).transpose(1, 0, 2, 3, 4)
    o = lax.map(lambda qi: _softmax_attend(qi, k, v), qb)
    return o.transpose(1, 0, 2, 3, 4).reshape(b, l, h * V_HEAD)

def _short_conv(u, w):
    gate_b, gate_c, val = jnp.split(u, 3, axis=-1)
    return gate_b * _dwconv(gate_c * val, w)

def _segsum_exp(cs):
    t = cs.shape[-1]
    diff = cs[..., :, None] - cs[..., None, :]
    mask = jnp.tril(jnp.ones((t, t), dtype=bool))
    return jnp.exp(jnp.where(mask, diff, -jnp.inf))

def _ssd_chunked(xs, dt, a, bm, cm, h0):
    b, l, h, p = xs.shape
    nc = l // SSD_CHUNK
    rep = h // SSD_GROUPS
    f32 = jnp.float32
    xdt = (xs.astype(f32) * dt[..., None]).reshape(b, nc, SSD_CHUNK, h, p)
    bc = jnp.repeat(bm.astype(f32), rep, axis=2).reshape(b, nc, SSD_CHUNK, h, SSD_STATE)
    cc = jnp.repeat(cm.astype(f32), rep, axis=2).reshape(b, nc, SSD_CHUNK, h, SSD_STATE)
    la = (dt * a).reshape(b, nc, SSD_CHUNK, h).transpose(0, 3, 1, 2)
    cs = jnp.cumsum(la, axis=-1)
    scores = jnp.einsum('bclhn,bcshn->bhcls', cc, bc) * _segsum_exp(cs)
    y_diag = jnp.einsum('bhcls,bcshp->bclhp', scores, xdt)
    decay_states = jnp.exp(cs[..., -1:] - cs).transpose(0, 2, 3, 1)
    states = jnp.einsum('bclhn,bclhp->bchpn', bc, xdt * decay_states[..., None])
    states = jnp.concatenate([h0[:, None], states], axis=1)
    chunk_tot = jnp.pad(cs[..., -1], ((0, 0), (0, 0), (1, 0)))
    decay_chunk = _segsum_exp(jnp.cumsum(chunk_tot, axis=-1))
    new_states = jnp.einsum('bhzc,bchpn->bzhpn', decay_chunk, states)
    state_decay = jnp.exp(cs).transpose(0, 2, 3, 1)[..., None]
    y_off = jnp.einsum('bclhn,bchpn->bclhp', cc, new_states[:, :-1]) * state_decay
    y = (y_diag + y_off).reshape(b, l, h, p)
    return y, new_states[:, -1]

def _ssd_prepare(u, conv_w, conv_b, dt_bias):
    b, l, _ = u.shape
    z = u[..., :SSD_WIDTH]
    xbc = jax.nn.silu(_dwconv(u[..., SSD_WIDTH:SSD_WIDTH + SSD_XBC], conv_w) + conv_b)
    xs = xbc[..., :SSD_WIDTH].reshape(b, l, SSD_HEADS, SSD_HEAD_DIM)
    bm = xbc[..., SSD_WIDTH:SSD_WIDTH + SSD_GN].reshape(b, l, SSD_GROUPS, SSD_STATE)
    cm = xbc[..., SSD_WIDTH + SSD_GN:].reshape(b, l, SSD_GROUPS, SSD_STATE)
    dt_raw = u[..., SSD_WIDTH + SSD_XBC:].reshape(b, l, 2, SSD_HEADS).astype(jnp.float32)
    dt = jax.nn.softplus(dt_raw + dt_bias.astype(jnp.float32))
    return z, xs, bm, cm, dt

def _bidir_ssd(xs, bm, cm, dt, a, h0):
    flip = lambda t: jnp.flip(t, axis=1)
    xs2 = jnp.stack([xs, flip(xs)])
    bm2 = jnp.stack([bm, flip(bm)])
    cm2 = jnp.stack([cm, flip(cm)])
    dt2 = jnp.stack([dt[:, :, 0], flip(dt[:, :, 1])])
    y2, h_final = jax.vmap(_ssd_chunked)(xs2, dt2, a, bm2, cm2, h0)
    return y2[0] + flip(y2[1]), h_final

def _ssd_output(y, xs, z, d_skip, norm_g):
    b, l = z.shape[0], z.shape[1]
    y = (y + d_skip.astype(jnp.float32)[:, None] * xs.astype(jnp.float32)).reshape(b, l, SSD_WIDTH)
    g = (y * jax.nn.silu(z.astype(jnp.float32))).reshape(b, l, SSD_GROUPS, SSD_WIDTH // SSD_GROUPS)
    g = g * lax.rsqrt(jnp.mean(g * g, axis=-1, keepdims=True) + EPS)
    return (g.reshape(b, l, SSD_WIDTH) * norm_g.astype(jnp.float32)).astype(z.dtype)

def _ffn_sublayer(x, shift, scale, gate, p):
    h = _modulate(_rms_norm(x, p['g_pre_ffn']), shift, scale)
    f = jnp.square(jax.nn.relu(h @ p['w_ff1'])) @ p['w_ff2']
    return x + gate * _rms_norm(f, p['g_post_ffn'])

def _layer(x, xc, mod, mod_c, rope, need_ctx, p):
    sh1, sc1, g1, sh2, sc2, g2 = jnp.split(mod[:, None, :], N_MOD, axis=-1)
    csh1, csc1, cg1, csh2, csc2, cg2 = jnp.split(mod_c, N_MOD, axis=-1)
    bsz, lc = xc.shape[0], xc.shape[1]

    h = _modulate(_rms_norm(x, p['g_pre_mix']), sh1, sc1)
    hc = _modulate(_rms_norm(xc, p['g_pre_mix']), csh1, csc1)
    ua, us, um = _split_in(h @ p['w_in'])
    uca, ucs, ucm = _split_in(hc @ p['w_in'])

    k, v = _mla_kv(ua, p['mla_kv_norm'], p['w_ukv'], rope)
    kc, vc = _mla_kv(uca, p['mla_kv_norm'], p['w_ukv'], None)
    q = _mla_q(ua, p['mla_q_norm'], p['w_uq'], rope)
    y_att = _blocked_attention(q, jnp.concatenate([kc, k], axis=1), jnp.concatenate([vc, v], axis=1))

    y_sc = _short_conv(us, p['sc_conv_w'])

    a = -jnp.exp(p['ssd_a_log'].astype(jnp.float32))
    zc, xsc, bmc, cmc, dtc = _ssd_prepare(ucm, p['ssd_conv_w'], p['ssd_conv_b'], p['ssd_dt_bias'])
    z, xs, bm, cm, dt = _ssd_prepare(um, p['ssd_conv_w'], p['ssd_conv_b'], p['ssd_dt_bias'])
    h0 = jnp.zeros((2, bsz, SSD_HEADS, SSD_HEAD_DIM, SSD_STATE), jnp.float32)
    yc_scan, h_ctx = _bidir_ssd(xsc, bmc, cmc, dtc, a, h0)
    y_scan, _ = _bidir_ssd(xs, bm, cm, dt, a, h_ctx)
    y_ssd = _ssd_output(y_scan, xs, z, p['ssd_d'], p['ssd_norm'])

    y = jnp.concatenate([y_att, y_sc, y_ssd], axis=-1) @ p['w_out']
    x = x + g1 * _rms_norm(y, p['g_post_mix'])
    x = _ffn_sublayer(x, sh2, sc2, g2, p)

    if need_ctx:
        qc = _mla_q(uca, p['mla_q_norm'], p['w_uq'], None)
        yc_att = _softmax_attend(qc, kc, vc).reshape(bsz, lc, MLA_WIDTH)
        yc_sc = _short_conv(ucs, p['sc_conv_w'])
        yc_ssd = _ssd_output(yc_scan, xsc, zc, p['ssd_d'], p['ssd_norm'])
        yc = jnp.concatenate([yc_att, yc_sc, yc_ssd], axis=-1) @ p['w_out']
        xc = xc + cg1 * _rms_norm(yc, p['g_post_mix'])
        xc = _ffn_sublayer(xc, csh2, csc2, cg2, p)
    return x, xc

def first_inputs(seed: int = 0) -> dict:
    key = jax.random.key(seed)
    k = jax.random.split(key, 25)
    f32 = jnp.float32
    L = DEPTH

    def nrm(i, shape, scale):
        return jax.random.normal(k[i], shape, f32) * scale

    def gain(i, shape):
        return 1.0 + 0.1 * jax.random.normal(k[i], shape, f32)

    dt0 = jnp.exp(jax.random.uniform(k[16], (L, 2, SSD_HEADS), f32, math.log(1e-3), math.log(1e-1)))
    return {
        'x': nrm(0, (BATCH, SEQ, D_MODEL), 1.0),
        'c': nrm(1, (BATCH, D_MODEL), 1.0),
        'ctx': nrm(2, (BATCH, CTX_LEN, D_MODEL), 1.0),
        'c_ctx': nrm(3, (D_MODEL,), 1.0),
        'w_mod': nrm(4, (L, D_MODEL, N_MOD * D_MODEL), 0.5 * D_MODEL ** -0.5),
        'b_mod': nrm(5, (L, N_MOD * D_MODEL), 0.02),
        'g_pre_mix': gain(6, (L, D_MODEL)),
        'w_in': nrm(7, (L, D_MODEL, D_IN), D_MODEL ** -0.5),
        'mla_q_norm': gain(8, (L, Q_LORA)),
        'w_uq': nrm(9, (L, Q_LORA, MLA_HEADS * (QK_NOPE + QK_ROPE)), Q_LORA ** -0.5),
        'mla_kv_norm': gain(10, (L, KV_LORA)),
        'w_ukv': nrm(11, (L, KV_LORA, MLA_HEADS * (QK_NOPE + V_HEAD)), KV_LORA ** -0.5),
        'sc_conv_w': nrm(12, (L, SC_KERNEL, SC_WIDTH), SC_KERNEL ** -0.5),
        'ssd_conv_w': nrm(13, (L, SSD_CONV, SSD_XBC), SSD_CONV ** -0.5),
        'ssd_conv_b': nrm(14, (L, SSD_XBC), 0.02),
        'ssd_a_log': jnp.log(jax.random.uniform(k[15], (L, 2, SSD_HEADS), f32, 1.0, 16.0)),
        'ssd_dt_bias': dt0 + jnp.log(-jnp.expm1(-dt0)),
        'ssd_d': gain(17, (L, SSD_HEADS)),
        'ssd_norm': gain(18, (L, SSD_WIDTH)),
        'w_out': nrm(19, (L, D_MIX, D_MODEL), D_MIX ** -0.5),
        'g_post_mix': gain(20, (L, D_MODEL)),
        'g_pre_ffn': gain(21, (L, D_MODEL)),
        'w_ff1': nrm(22, (L, D_MODEL, D_FF), D_MODEL ** -0.5),
        'w_ff2': nrm(23, (L, D_FF, D_MODEL), D_FF ** -0.5),
        'g_post_ffn': gain(24, (L, D_MODEL)),
    }

def first_block(x, c, ctx, c_ctx, w_mod, b_mod, g_pre_mix, w_in, mla_q_norm, w_uq, mla_kv_norm, w_ukv,
              sc_conv_w, ssd_conv_w, ssd_conv_b, ssd_a_log, ssd_dt_bias, ssd_d, ssd_norm, w_out,
              g_post_mix, g_pre_ffn, w_ff1, w_ff2, g_post_ffn):
    rows = x.shape[1] // GRID_W
    rope = _axial_rope_tables(rows)
    xc = ctx
    s_lat = jax.nn.silu(c)
    s_ctx = jax.nn.silu(c_ctx)
    for i in range(DEPTH):
        p = {
            'g_pre_mix': g_pre_mix[i], 'w_in': w_in[i],
            'mla_q_norm': mla_q_norm[i], 'w_uq': w_uq[i],
            'mla_kv_norm': mla_kv_norm[i], 'w_ukv': w_ukv[i],
            'sc_conv_w': sc_conv_w[i],
            'ssd_conv_w': ssd_conv_w[i], 'ssd_conv_b': ssd_conv_b[i],
            'ssd_a_log': ssd_a_log[i], 'ssd_dt_bias': ssd_dt_bias[i],
            'ssd_d': ssd_d[i], 'ssd_norm': ssd_norm[i],
            'w_out': w_out[i], 'g_post_mix': g_post_mix[i],
            'g_pre_ffn': g_pre_ffn[i], 'w_ff1': w_ff1[i], 'w_ff2': w_ff2[i],
            'g_post_ffn': g_post_ffn[i],
        }
        mod = s_lat @ w_mod[i] + b_mod[i]
        mod_c = s_ctx @ w_mod[i] + b_mod[i]
        x, xc = _layer(x, xc, mod, mod_c, rope, i < DEPTH - 1, p)
    return x


HEAD_DIM = 64
PLE_DIM = 256
BLOCK = 128
N_MIXERS = 3
LN_EPS = 1e-5
DEEPNORM_ALPHA = (2 * DEPTH) ** 0.25
DEEPNORM_BETA = (8 * DEPTH) ** -0.25

A_GROUPS = ((128, 1), (512, 4), (2048, 16))
A_HEADS = D_MODEL // HEAD_DIM
A_WIDTH = A_HEADS * HEAD_DIM
A_IN = 3 * len(A_GROUPS) * A_WIDTH + A_WIDTH

B_HEADS = D_MODEL // HEAD_DIM
B_KV_HEADS = 2
B_WINDOW = 128
B_WIDTH = B_HEADS * HEAD_DIM
B_KV = B_KV_HEADS * HEAD_DIM
B_IN = 2 * B_WIDTH + 2 * B_KV

C_HEADS = D_MODEL // HEAD_DIM
C_KV_HEADS = 4
C_WIDTH = C_HEADS * HEAD_DIM
C_KV = C_KV_HEADS * HEAD_DIM
C_CMP_LEN = 32
C_CMP_STRIDE = 16
C_SEL_LEN = 64
C_N_SEL = 16
C_WINDOW = 512
C_SEL_OVERLAP = (1.0, 2.0, 2.0, 2.0, 1.0)
C_IN = 2 * C_WIDTH + 6 * C_KV + 3 * C_HEADS

N_A_LAYERS = len(range(0, DEPTH, N_MIXERS))
N_B_LAYERS = len(range(1, DEPTH, N_MIXERS))
N_C_LAYERS = len(range(2, DEPTH, N_MIXERS))


def split_cols(h, sizes):
    out, start = [], 0
    for s in sizes:
        out.append(h[..., start:start + s])
        start += s
    return out

def rope_tables(seq_len):
    inv = 1.0 / (ROPE_THETA ** (jnp.arange(0, HEAD_DIM, 2, dtype=jnp.float32) / HEAD_DIM))
    ang = jnp.arange(seq_len, dtype=jnp.float32)[:, None] * inv[None, :]
    return jnp.cos(ang), jnp.sin(ang)

def apply_rope(t, cos, sin):
    tf = t.astype(jnp.float32)
    half = HEAD_DIM // 2
    t1, t2 = tf[..., :half], tf[..., half:]
    c, s = cos[None, :, None, :], sin[None, :, None, :]
    return jnp.concatenate([t1 * c - t2 * s, t2 * c + t1 * s], axis=-1).astype(t.dtype)

def layer_norm(x, g, b):
    xf = x.astype(jnp.float32)
    mu = jnp.mean(xf, axis=-1, keepdims=True)
    var = jnp.mean(jnp.square(xf - mu), axis=-1, keepdims=True)
    y = (xf - mu) * lax.rsqrt(var + LN_EPS) * g.astype(jnp.float32) + b.astype(jnp.float32)
    return y.astype(x.dtype)

def banded_attention(q, k, v, max_dist, sinks=None):
    B_, L, Hk, G, dh = q.shape
    nb = -(-L // BLOCK)
    pad = nb * BLOCK - L
    npv = -(-max_dist // BLOCK)
    W = (npv + 1) * BLOCK
    qb = jnp.pad(q, ((0, 0), (0, pad), (0, 0), (0, 0), (0, 0))).reshape(B_, nb, BLOCK, Hk, G, dh)

    def windows(t):
        tp = jnp.pad(t, ((0, 0), (npv * BLOCK, pad), (0, 0), (0, 0))).reshape(B_, nb + npv, BLOCK, Hk, dh)
        return jnp.concatenate([tp[:, j:j + nb] for j in range(npv + 1)], axis=2)

    kw, vw = windows(k), windows(v)
    s = jnp.einsum('bnqhgd,bnkhd->bnhgqk', qb, kw).astype(jnp.float32) * (dh ** -0.5)
    dist = np.arange(BLOCK)[:, None] + npv * BLOCK - np.arange(W)[None, :]
    band = (dist >= 0) & (dist <= max_dist)
    kpos = np.arange(nb)[:, None] * BLOCK - npv * BLOCK + np.arange(W)[None, :]
    mask = band[None, :, :] & (kpos >= 0)[:, None, :]
    s = jnp.where(mask[None, :, None, None, :, :], s, -jnp.inf)
    m = jnp.max(s, axis=-1, keepdims=True)
    if sinks is not None:
        sk = sinks.astype(jnp.float32).reshape(1, 1, Hk, G, 1, 1)
        m = jnp.maximum(m, sk)
    e = jnp.exp(s - m)
    l = jnp.sum(e, axis=-1, keepdims=True)
    if sinks is not None:
        l = l + jnp.exp(sk - m)
    o = jnp.einsum('bnhgqk,bnkhd->bnqhgd', e, vw.astype(jnp.float32))
    o = o / jnp.transpose(l, (0, 1, 4, 2, 3, 5))
    lse = jnp.transpose((m + jnp.log(l))[..., 0], (0, 1, 4, 2, 3))
    o = o.reshape(B_, nb * BLOCK, Hk, G, dh)[:, :L]
    lse = lse.reshape(B_, nb * BLOCK, Hk, G)[:, :L]
    return o, lse

def mixer_a(x, w_in, w_out, cos, sin):
    B_, S, _ = x.shape
    h = x @ w_in
    outs, lses = [], []
    for gi, (window, dil) in enumerate(A_GROUPS):
        base = 3 * gi * A_WIDTH
        q, k, v = split_cols(h[..., base:base + 3 * A_WIDTH], [A_WIDTH] * 3)
        q = apply_rope(q.reshape(B_, S, A_HEADS, HEAD_DIM), cos, sin)
        k = apply_rope(k.reshape(B_, S, A_HEADS, HEAD_DIM), cos, sin)
        v = v.reshape(B_, S, A_HEADS, HEAD_DIM)
        Ls = S // dil

        def strided(t):
            return jnp.transpose(t.reshape(B_, Ls, dil, A_HEADS, HEAD_DIM), (0, 2, 1, 3, 4)).reshape(B_ * dil, Ls, A_HEADS, HEAD_DIM)

        o, lse = banded_attention(strided(q)[:, :, :, None, :], strided(k), strided(v), window // dil)
        o = jnp.transpose(o.reshape(B_, dil, Ls, A_HEADS, HEAD_DIM), (0, 2, 1, 3, 4)).reshape(B_, S, A_HEADS, HEAD_DIM)
        lse = jnp.transpose(lse.reshape(B_, dil, Ls, A_HEADS), (0, 2, 1, 3)).reshape(B_, S, A_HEADS)
        outs.append(o)
        lses.append(lse)
    wts = jax.nn.softmax(jnp.stack(lses, axis=0), axis=0)
    o = jnp.einsum('gbsh,gbshd->bshd', wts, jnp.stack(outs, axis=0))
    z = h[..., -A_WIDTH:]
    o = o.reshape(B_, S, A_WIDTH).astype(x.dtype)
    return (o * jax.nn.silu(z)) @ w_out

def mixer_b(x, w_in, sinks, w_out, cos, sin):
    B_, S, _ = x.shape
    G = B_HEADS // B_KV_HEADS
    q, k, v, z = split_cols(x @ w_in, [B_WIDTH, B_KV, B_KV, B_WIDTH])
    q = apply_rope(q.reshape(B_, S, B_HEADS, HEAD_DIM), cos, sin).reshape(B_, S, B_KV_HEADS, G, HEAD_DIM)
    k = apply_rope(k.reshape(B_, S, B_KV_HEADS, HEAD_DIM), cos, sin)
    v = v.reshape(B_, S, B_KV_HEADS, HEAD_DIM)
    o, _ = banded_attention(q, k, v, B_WINDOW - 1, sinks)
    o = o.reshape(B_, S, B_WIDTH).astype(x.dtype)
    return (o * jax.nn.silu(z)) @ w_out

def mixer_c(x, w_in, w_ck, w_cv, pos_cmp, w_out, cos, sin):
    B_, S, _ = x.shape
    Hk, G, dh = C_KV_HEADS, C_HEADS // C_KV_HEADS, HEAD_DIM
    scale = dh ** -0.5
    q, kc, vc, ks, vs, kw, vw, gl, z = split_cols(x @ w_in, [C_WIDTH] + [C_KV] * 6 + [3 * C_HEADS, C_WIDTH])
    q = apply_rope(q.reshape(B_, S, C_HEADS, dh), cos, sin).reshape(B_, S, Hk, G, dh)
    kv_shape = (B_, S, Hk, dh)
    kc = apply_rope(kc.reshape(kv_shape), cos, sin)
    ks = apply_rope(ks.reshape(kv_shape), cos, sin)
    kw = apply_rope(kw.reshape(kv_shape), cos, sin)
    vc, vs, vw = vc.reshape(kv_shape), vs.reshape(kv_shape), vw.reshape(kv_shape)

    n_c = S // C_CMP_STRIDE - 1

    def compress(t, w):
        tr = t.reshape(B_, S // C_CMP_STRIDE, C_CMP_STRIDE, Hk, dh)
        blk = jnp.concatenate([tr[:, :-1], tr[:, 1:]], axis=2)
        return jnp.einsum('bnjhd,jde->bnhe', blk + pos_cmp[None, None, :, None, :], w)

    k_cmp, v_cmp = compress(kc, w_ck), compress(vc, w_cv)
    cmp_end = jnp.arange(n_c) * C_CMP_STRIDE + C_CMP_LEN - 1

    n_s = S // C_SEL_LEN
    n_sel = min(C_N_SEL, n_s)
    ks_blocks = jnp.transpose(ks.reshape(B_, n_s, C_SEL_LEN, Hk, dh), (0, 3, 1, 2, 4))
    vs_blocks = jnp.transpose(vs.reshape(B_, n_s, C_SEL_LEN, Hk, dh), (0, 3, 1, 2, 4))
    bi = jnp.arange(B_)[:, None, None, None]
    hi = jnp.arange(Hk)[None, None, :, None]
    blk_ids = jnp.arange(n_s)

    def query_block(args):
        qb, t0 = args
        tq = t0 + jnp.arange(BLOCK)
        s = jnp.einsum('bqhgd,bnhd->bqhgn', qb, k_cmp).astype(jnp.float32) * scale
        cvalid = cmp_end[None, :] <= tq[:, None]
        s = jnp.where(cvalid[None, :, None, None, :], s, -jnp.inf)
        m = jnp.max(s, axis=-1, keepdims=True)
        m = jnp.where(jnp.isfinite(m), m, 0.0)
        e = jnp.exp(s - m)
        pc = e / jnp.maximum(jnp.sum(e, axis=-1, keepdims=True), 1e-30)
        o_cmp = jnp.einsum('bqhgn,bnhd->bqhgd', pc, v_cmp.astype(jnp.float32))
        imp = jnp.pad(jnp.sum(pc, axis=3), ((0, 0), (0, 0), (0, 0), (1, 1)))
        imp_s = C_SEL_OVERLAP[0] * imp[..., 0::4][..., :n_s]
        for o_off in range(1, len(C_SEL_OVERLAP)):
            imp_s = imp_s + C_SEL_OVERLAP[o_off] * imp[..., o_off::4][..., :n_s]
        cur = tq // C_SEL_LEN
        forced = (blk_ids[None, :] == 0) | (blk_ids[None, :] == cur[:, None]) | (blk_ids[None, :] == cur[:, None] - 1)
        bvalid = blk_ids[None, :] * C_SEL_LEN <= tq[:, None]
        score = jnp.where(forced[None, :, None, :], 1e4, jnp.where(bvalid[None, :, None, :], imp_s, -1.0))
        _, idx = lax.top_k(score, n_sel)
        ksel = ks_blocks[bi, hi, idx]
        vsel = vs_blocks[bi, hi, idx]
        kpos = idx[..., None] * C_SEL_LEN + jnp.arange(C_SEL_LEN)
        smask = kpos <= tq[None, :, None, None, None]
        ss = jnp.einsum('bqhgd,bqhnkd->bqhgnk', qb, ksel).astype(jnp.float32) * scale
        ss = jnp.where(smask[:, :, :, None], ss, -jnp.inf)
        ps = jax.nn.softmax(ss.reshape(ss.shape[:4] + (n_sel * C_SEL_LEN,)), axis=-1).reshape(ss.shape)
        o_slc = jnp.einsum('bqhgnk,bqhnkd->bqhgd', ps, vsel.astype(jnp.float32))
        return o_cmp, o_slc

    nqb = S // BLOCK
    q_blocks = jnp.transpose(q.reshape(B_, nqb, BLOCK, Hk, G, dh), (1, 0, 2, 3, 4, 5))
    t0s = jnp.arange(nqb, dtype=jnp.int32) * BLOCK
    o_cmp, o_slc = lax.map(query_block, (q_blocks, t0s))
    o_cmp = jnp.transpose(o_cmp, (1, 0, 2, 3, 4, 5)).reshape(B_, S, Hk, G, dh)
    o_slc = jnp.transpose(o_slc, (1, 0, 2, 3, 4, 5)).reshape(B_, S, Hk, G, dh)
    o_win, _ = banded_attention(q, kw, vw, C_WINDOW - 1)
    g = jax.nn.sigmoid(gl.astype(jnp.float32)).reshape(B_, S, 3, Hk, G, 1)
    o = g[:, :, 0] * o_cmp + g[:, :, 1] * o_slc + g[:, :, 2] * o_win
    o = o.reshape(B_, S, C_WIDTH).astype(x.dtype)
    return (o * jax.nn.silu(z)) @ w_out

def second_inputs(seed: int = 0) -> dict:
    key = jax.random.key(seed)
    ks = jax.random.split(key, 16)

    def nrm(k, shape, scale):
        return jax.random.normal(k, shape, jnp.float32) * scale

    return {
        'x': nrm(ks[0], (BATCH, SEQ, D_MODEL), 1.0),
        'p': nrm(ks[1], (DEPTH, BATCH, SEQ, PLE_DIM), 1.0),
        'a_w_in': nrm(ks[2], (N_A_LAYERS, D_MODEL, A_IN), D_MODEL ** -0.5),
        'a_w_out': nrm(ks[3], (N_A_LAYERS, A_WIDTH, D_MODEL), A_WIDTH ** -0.5 * DEEPNORM_BETA),
        'b_w_in': nrm(ks[4], (N_B_LAYERS, D_MODEL, B_IN), D_MODEL ** -0.5),
        'b_sinks': nrm(ks[5], (N_B_LAYERS, B_HEADS), 1.0),
        'b_w_out': nrm(ks[6], (N_B_LAYERS, B_WIDTH, D_MODEL), B_WIDTH ** -0.5 * DEEPNORM_BETA),
        'c_w_in': nrm(ks[7], (N_C_LAYERS, D_MODEL, C_IN), D_MODEL ** -0.5),
        'c_w_ck': nrm(ks[8], (N_C_LAYERS, C_CMP_LEN, HEAD_DIM, HEAD_DIM), (C_CMP_LEN * HEAD_DIM) ** -0.5),
        'c_w_cv': nrm(ks[9], (N_C_LAYERS, C_CMP_LEN, HEAD_DIM, HEAD_DIM), (C_CMP_LEN * HEAD_DIM) ** -0.5),
        'c_pos': nrm(ks[10], (N_C_LAYERS, C_CMP_LEN, HEAD_DIM), 0.5),
        'c_w_out': nrm(ks[11], (N_C_LAYERS, C_WIDTH, D_MODEL), C_WIDTH ** -0.5 * DEEPNORM_BETA),
        'ln_g': 1.0 + nrm(ks[12], (DEPTH, D_MODEL), 0.05),
        'ln_b': nrm(ks[13], (DEPTH, D_MODEL), 0.05),
        'ple_w_proj': nrm(ks[14], (DEPTH, PLE_DIM, D_MODEL), PLE_DIM ** -0.5),
        'ple_w_gate': nrm(ks[15], (DEPTH, D_MODEL, D_MODEL), D_MODEL ** -0.5),
    }

def second_block(x, p, a_w_in, a_w_out, b_w_in, b_sinks, b_w_out, c_w_in, c_w_ck, c_w_cv, c_pos, c_w_out, ln_g, ln_b, ple_w_proj, ple_w_gate):
    cos, sin = rope_tables(x.shape[1])
    for i in range(DEPTH):
        j = i // N_MIXERS
        kind = i % N_MIXERS
        if kind == 0:
            h = mixer_a(x, a_w_in[j], a_w_out[j], cos, sin)
        elif kind == 1:
            h = mixer_b(x, b_w_in[j], b_sinks[j], b_w_out[j], cos, sin)
        else:
            h = mixer_c(x, c_w_in[j], c_w_ck[j], c_w_cv[j], c_pos[j], c_w_out[j], cos, sin)
        x = layer_norm(DEEPNORM_ALPHA * x + h, ln_g[i], ln_b[i])
        gate = jax.nn.sigmoid((x @ ple_w_gate[i]).astype(jnp.float32))
        x = (x.astype(jnp.float32) + gate * (p[i] @ ple_w_proj[i]).astype(jnp.float32)).astype(x.dtype)
    return x


def setup_inputs(seed=0):
    out = dict(first_inputs(seed))
    for name, value in second_inputs(seed + 1).items():
        if name != "x":
            out[name + "_2"] = value
    return out


def reference(
    x, c, ctx, c_ctx, w_mod, b_mod, g_pre_mix, w_in, mla_q_norm, w_uq, mla_kv_norm, w_ukv,
    sc_conv_w, ssd_conv_w, ssd_conv_b, ssd_a_log, ssd_dt_bias, ssd_d, ssd_norm, w_out,
    g_post_mix, g_pre_ffn, w_ff1, w_ff2, g_post_ffn, p_2, a_w_in_2, a_w_out_2, b_w_in_2,
    b_sinks_2, b_w_out_2, c_w_in_2, c_w_ck_2, c_w_cv_2, c_pos_2, c_w_out_2, ln_g_2, ln_b_2,
    ple_w_proj_2, ple_w_gate_2,
):
    x = first_block(
        x, c, ctx, c_ctx, w_mod, b_mod, g_pre_mix, w_in, mla_q_norm, w_uq, mla_kv_norm, w_ukv,
        sc_conv_w, ssd_conv_w, ssd_conv_b, ssd_a_log, ssd_dt_bias, ssd_d, ssd_norm, w_out,
        g_post_mix, g_pre_ffn, w_ff1, w_ff2, g_post_ffn,
    )
    return second_block(
        x, p_2, a_w_in_2, a_w_out_2, b_w_in_2, b_sinks_2, b_w_out_2, c_w_in_2, c_w_ck_2,
        c_w_cv_2, c_pos_2, c_w_out_2, ln_g_2, ln_b_2, ple_w_proj_2, ple_w_gate_2,
    )


_drawn_inputs = setup_inputs


def setup_inputs(seed=0):
    import zlib

    import numpy as np

    out = dict(_drawn_inputs(seed))
    spreads = {}
    factors = {'ctx': 4.209,
     'mla_q_norm': 8.0,
     'w_uq': 3.072,
     'mla_kv_norm': 8.0,
     'ssd_conv_b': 8.0,
     'ssd_d': 30.777,
     'b_sinks_2': 8.0,
     'ssd_a_log': 7.032,
     'ssd_dt_bias': 2.987,
     'ssd_norm': 3.229}
    for name, (base, spread) in spreads.items():
        noise = np.random.default_rng([zlib.crc32(name.encode()), seed]).standard_normal(out[name].shape)
        drawn = base * np.exp(spread * noise) if base else spread * noise
        out[name] = jnp.asarray(drawn.astype(out[name].dtype))
    for name, factor in factors.items():
        out[name] = (out[name] * factor).astype(out[name].dtype)
    return out
```

```python
import math

import numpy as np

import concourse.bass as bass
from concourse import mybir

F32 = mybir.dt.float32
F32R = mybir.dt.float32r
ALU = mybir.AluOpType
ACT = mybir.ActivationFunctionType
AX = mybir.AxisListType

P = 128
D = 1024
KC = D // P
SEQ = 256
T = 2 * SEQ
CTX = (0, SEQ)
X = (SEQ, T)
ALL = (0, T)
LAYERS = 2
EPS = 1e-6
LN_EPS = 1e-5
ALPHA = (2 * LAYERS) ** 0.25

MLA_HEADS, NOPE, ROPE, VH = 4, 64, 32, 64
QK = NOPE + ROPE
MLA_SCALE = QK ** -0.5
Q_LORA, KV_LORA = 256, 128
SSD_HEADS, STATE = 8, 64
CHUNKS = T // P
D_FF = 4 * D
COL_KV, COL_GB, COL_GC, COL_VAL, COL_Z, COL_XBC, COL_DT = 256, 416, 672, 928, 1184, 1696, 2464
D_IN = 2480
NEG = -1e30
HEAD = 64
HEADS = 16
SCALE = HEAD ** -0.5
RAW_SLOTS, HALF_SLOTS = 4, 3
UNIT_COLS = 272
HALF = 4 * UNIT_COLS

VEC = {}
_at = 0
for _name, _n in (("b_mod", 48), ("g_pre_mix", 8), ("g_post_mix", 8), ("g_pre_ffn", 8), ("g_post_ffn", 8),
                  ("ssd_norm", 4), ("mla_q_norm", 2), ("mla_kv_norm", 1), ("sc_conv_w", 6), ("ssd_conv_w", 18),
                  ("ssd_conv_b", 6)):
    VEC[_name] = (_at, _n)
    _at += _n
VEC_ROWS = _at
VEC2 = {"c": (0, 8), "c_ctx": (8, 8), "ln_g0": (16, 8), "ln_g1": (24, 8), "ln_b0": (32, 8), "ln_b1": (40, 8)}
VEC2_ROWS = 48

LOG1P_TERMS = 9
CONSTS = 4 + 7 + 2 * len(VEC) + len(VEC2) + 4 * LAYERS + 1


def constants():
    i = np.arange(P)
    out = {"ident": np.eye(P, dtype=np.float32)}
    freq = 1.0 / (np.float32(10000.0) ** (np.arange(0, HEAD, 2, dtype=np.float32) / np.float32(HEAD)))
    ang = (np.arange(SEQ, dtype=np.float32)[None, :] * freq.astype(np.float32)[:, None]).astype(np.float32)
    sign = np.where((i % HEAD) < HEAD // 2, -1.0, 1.0)[:, None]
    out["rope"] = np.stack([np.cos(ang)[i % 32], np.sin(ang)[i % 32] * sign], 1).astype(np.float32)
    half = ROPE // 2
    inv = np.float32(10000.0) ** (-np.arange(0, half, 2, dtype=np.float32) / np.float32(half))
    t = np.arange(SEQ)
    a_r = ((t // 64).astype(np.float32)[None, :] * inv[:, None]).astype(np.float32)
    a_c = ((t % 64).astype(np.float32)[None, :] * inv[:, None]).astype(np.float32)
    ang = np.concatenate([a_r, a_r, a_c, a_c], 0)
    sgn = np.where((np.arange(32) // 8) % 2 == 0, -1.0, 1.0)[:, None]
    axial = np.zeros((P, 2, SEQ), np.float32)
    axial[64:96, 0] = np.cos(ang)
    axial[64:96, 1] = np.sin(ang) * sgn
    out["axial"] = axial
    s, u = i[:, None], i[None, :]
    out["tri"] = np.stack([(s <= u), (s >= u)], 1).astype(np.float32)
    out["tri_neg"] = np.stack([np.where(s <= u, 0, NEG), np.where(s >= u, 0, NEG)], 1).astype(np.float32)
    last = np.zeros((P, 2, P), np.float32)
    last[P - 1, 0] = 1
    last[0, 1] = 1
    out["last"] = last
    sel = np.zeros((16, 16, P), np.float32)
    for h in range(16):
        sel[h, h] = 1
    out["sel"] = sel

    def banded(dil, most, q0, nk):
        q, k = (q0 + i)[:, None], np.arange(nk)[None, :]
        d = q - k
        return np.where((d >= 0) & (d % dil == 0) & (d // dil <= most), 0, NEG).astype(np.float32)

    groups = ((1, 128), (4, 128), (16, 128))
    out["mask_a"] = np.concatenate([banded(d, m, 0, P) for d, m in groups] + [banded(d, m, P, SEQ) for d, m in groups], 1)
    out["mask_b"] = np.concatenate([banded(1, 127, 0, P), banded(1, 127, P, SEQ)], 1)
    return out


class Signal:

    def __init__(self, name, sem, counts):
        self.name, self.sem, self.counts, self.n, self.mine = name, sem, counts, 0, {}

    newest = [None]

    def tick(self, *keys):
        self.n += 1
        Signal.newest[0] = self
        for k in keys:
            self.mine[k] = self.n
        return self.sem, 1

    def at(self, key):
        return self.counts[key] if self.counts is not None else 1


class Waits:

    def __init__(self, engine):
        self.engine, self.reached = engine, {}

    def wait_ge(self, signal, value):
        if value > self.reached.get(signal.name, 0):
            self.reached[signal.name] = value
            self.engine.wait_ge(signal.sem, value)


class Unit:

    def __init__(self, kind, loads, n, key, id, blocks, x, t=None):
        self.kind, self.loads, self.n, self.key, self.id = kind, loads, n, key, id
        self.blocks, self.x, self.t = blocks, x, t
        self.first_half_done = False


def build(nc, A, out, counts):
    signals = {}

    def signal(name):
        signals[name] = Signal(name, nc.alloc_semaphore(name), None if counts is None else counts[name])
        return signals[name]

    def so_far():
        s = Signal.newest[0]
        return (s, s.n) if s is not None else (s_gemm, 0)

    s_aa = signal("aa")
    s_ab = signal("ab")
    s_acc = signal("acc")
    s_bd = signal("bd")
    s_conv = signal("conv")
    s_cos2 = signal("cos2")
    s_cos_on = signal("cos_on")
    s_cs = signal("cs")
    s_cs32 = signal("cs32")
    s_cs_hi = signal("cs_hi")
    s_cs_tok = signal("cs_tok")
    s_cst = signal("cst")
    s_ctd = signal("ctd")
    s_dec = signal("dec")
    s_df = signal("df")
    s_dve_chain = signal("dve_chain")
    s_e2 = signal("e2")
    s_ecs = signal("ecs")
    s_ed = signal("ed")
    s_ee = signal("ee")
    s_ex = signal("ex")
    s_f_add = signal("f_add")
    s_fh = signal("fh")
    s_fq = signal("fq")
    s_fused = signal("fused")
    s_g2_hi = signal("g2_hi")
    s_gemm = signal("gemm")
    s_gmul = signal("gmul")
    s_gt = signal("gt")
    s_gz = signal("gz")
    s_h32 = signal("h32")
    s_hh = signal("hh")
    s_hi_ready = signal("hi_ready")
    s_init_t = signal("init_t")
    s_inv = signal("inv")
    s_kr_rope = signal("kr_rope")
    s_kt = signal("kt")
    s_la = signal("la")
    s_ln_acc = signal("ln_acc")
    s_ln_d = signal("ln_d")
    s_ln_sq = signal("ln_sq")
    s_ln_stat = signal("ln_stat")
    s_ln_total = signal("ln_total")
    s_ln_v = signal("ln_v")
    s_ln_x = signal("ln_x")
    s_lo_ready = signal("lo_ready")
    s_mla_e = signal("mla_e")
    s_mla_k = signal("mla_k")
    s_mla_kr = signal("mla_kr")
    s_mla_mx = signal("mla_mx")
    s_mla_n = signal("mla_n")
    s_mla_o = signal("mla_o")
    s_mla_p = signal("mla_p")
    s_mla_pt = signal("mla_pt")
    s_mla_q = signal("mla_q")
    s_mla_qr = signal("mla_qr")
    s_mla_rs = signal("mla_rs")
    s_mla_s = signal("mla_s")
    s_mla_sq = signal("mla_sq")
    s_mla_sum = signal("mla_sum")
    s_mla_t = signal("mla_t")
    s_mla_v = signal("mla_v")
    s_mla_y = signal("mla_y")
    s_mod_col = signal("mod_col")
    s_mod_row = signal("mod_row")
    s_mod_t = signal("mod_t")
    s_mx2 = signal("mx2")
    s_norm_sum = signal("norm_sum")
    s_o2 = signal("o2")
    s_ones = signal("ones")
    s_out_rows = signal("out_rows")
    s_out_t = signal("out_t")
    s_p2 = signal("p2")
    s_p_hi = signal("p_hi")
    s_p_lo = signal("p_lo")
    s_p_t = signal("p_t")
    s_pads = signal("pads")
    s_parts = signal("parts")
    s_parts2 = signal("parts2")
    s_parts_f = signal("parts_f")
    s_parts_g2 = signal("parts_g2")
    s_parts_y = signal("parts_y")
    s_parts_y2 = signal("parts_y2")
    s_pj = signal("pj")
    s_pt2 = signal("pt2")
    s_qt = signal("qt")
    s_rec = signal("rec")
    s_relu = signal("relu")
    s_rope2 = signal("rope2")
    s_rs = signal("rs")
    s_s2 = signal("s2")
    s_sc = signal("sc")
    s_sg = signal("sg")
    s_sh2 = signal("sh2")
    s_sin2 = signal("sin2")
    s_sq = signal("sq")
    s_ssd_a = signal("ssd_a")
    s_ssd_gt = signal("ssd_gt")
    s_ssd_m = signal("ssd_m")
    s_ssd_row = signal("ssd_row")
    s_ssd_rs = signal("ssd_rs")
    s_ssd_sq = signal("ssd_sq")
    s_ssd_st = signal("ssd_st")
    s_ssd_sum = signal("ssd_sum")
    s_ssd_tk = signal("ssd_tk")
    s_ssd_y = signal("ssd_y")
    s_ssd_yn = signal("ssd_yn")
    s_ssd_ys = signal("ssd_ys")
    s_st = signal("st")
    s_t2 = signal("t2")
    s_u_out = signal("u_out")
    s_v2 = signal("v2")
    s_v32 = signal("v32")
    s_val = signal("val")
    s_vb2 = signal("vb2")
    s_vt = signal("vt")
    s_vv = signal("vv")
    s_wd = signal("wd")
    s_ww = signal("ww")
    s_x2_hi = signal("x2_hi")
    s_x2_new = signal("x2_new")
    s_x_new = signal("x_new")
    s_xc = signal("xc")
    s_xn = signal("xn")
    s_xn_pool = signal("xn_pool")
    s_xr = signal("xr")
    s_xt = signal("xt")
    s_xtk = signal("xtk")
    s_y2_hi = signal("y2_hi")
    s_y_copy = signal("y_copy")
    s_ya = signal("ya")
    s_yh = signal("yh")
    s_z2 = signal("z2")

    base = (nc.sbuf_base + 63) // 64 * 64
    end = nc.sbuf_usable_end
    where = {"at": base}

    def at(name, shape, offset, dt=F32):
        return nc.alloc_sbuf_tensor_at(name, shape, dt, offset=offset).ap()

    def size(shape):
        return (int(np.prod(shape[1:])) * 4 + 31) // 32 * 32

    def place(name, shape, dt=F32):
        o = where["at"]
        where["at"] = o + size(shape)
        assert where["at"] <= end, (name, where["at"], end)
        return at(name, shape, o, dt)

    def region(start, items):
        made = []
        for name, shape, *dt in items:
            made.append(at(name, shape, start, *dt))
            start += size(shape)
        assert start <= end, (items[-1][0], start, end)
        return made, start

    raw = [place(f"raw{i}", [P, 8 * UNIT_COLS]) for i in range(RAW_SLOTS)]
    whi = [place(f"whi{i}", [P, HALF], F32R) for i in range(HALF_SLOTS)]
    wlo = [place(f"wlo{i}", [P, HALF], F32R) for i in range(HALF_SLOTS)]
    XT = place("XT", [P, KC, T])
    ident = place("ident_sb", [P, P])
    ones = place("ones_sb", [P, P])
    rope = place("rope_sb", [P, 2, SEQ])
    axial = place("axial_sb", [P, 2, SEQ])
    tri = place("tri_sb", [P, 2, P])
    tri_neg = place("tri_neg_sb", [P, 2, P])
    last = place("last_sb", [P, 2, P])
    sel = place("sel_sb", [P, 16, P])
    VT = [place(f"VT{i}", [P, P]) for i in range(3)]
    w_uq = place("w_uq_sb", [P, 2, MLA_HEADS * QK])
    w_ukv = place("w_ukv_sb", [P, MLA_HEADS * (NOPE + VH)])
    modT = [place(f"modT{i}", [P, 48, 2]) for i in range(LAYERS)]
    fA = place("fuse_scale", [P, KC, 2])
    fG = place("fuse_gate", [P, KC, 2])
    cs32 = place("silu_c", [P, 2, KC])
    cs = place("silu_c_parts", [P, KC, 4], F32R)
    mrow = [place(f"mod_row{i}", [4, 256]) for i in range(2)]
    dt_bias = place("dt_bias_sb", [P, LAYERS, 16])
    a_log = place("a_log_sb", [P, LAYERS, 16])
    d_skip = place("d_skip_sb", [P, LAYERS, 4])
    sinks = place("sinks_sb", [P, HEADS])
    sinks8 = place("sinks8_sb", [P, HEADS])
    eps_c = place("eps_c", [P, 2])
    small = place("small", [P, 64])
    R3 = where["at"]
    (HH, HL), R4 = region(R3, [("HH", [P, KC, T], F32R), ("HL", [P, KC, T], F32R)])
    (YM,), R5 = region(R4, [("YM", [P, KC, T])])
    (xtok,), _ = region(R3, [("xtok", [P, 4, D])])
    (vrow,), _ = region(R5, [("vrow", [P, 3, P])])
    (QT, KT, VV), o = region(R3, [("QT", [P, MLA_HEADS, T]), ("KT", [P, MLA_HEADS, T]), ("VV", [P, 4, 256])])
    (PR0, PR1, PT0), o2 = region(o, [("PR0", [P, T]), ("PR1", [P, T]), ("PT0", [P, 4, SEQ])])
    (PT1,), o3 = region(o2, [("PT1", [P, 4, SEQ])])
    assert o3 <= R4
    (SQM, RSM, ROT), _ = region(o, [("SQM", [P, 2, T]), ("RSM", [P, 2, T]), ("ROT", [P, 4, SEQ])])
    (GT, CTd, E00, E01, E10, E11), o = region(R3, [("GT", [P, 2, T]), ("CTd", [P, 2, T])] + [(f"E{i}{j}", [P, T]) for i in (0, 1) for j in (0, 1)])
    EE = [[E00, E01], [E10, E11]]
    (M0, M1, Ce0, Ce1, ec0, ec1, Bd0, Bd1), o = region(o, [(n, [P, T]) for n in ("M0", "M1", "Ce0", "Ce1", "ec0", "ec1", "Bd0", "Bd1")])
    assert o <= R4
    (SQS, RSS), _ = region(R3, [("SQS", [P, 4, T]), ("RSS", [P, 2, T])])
    (XN0, XN1, H320, H321, XN2, XN3), o = region(R5, [(n, [P, T]) for n in ("XN0", "XN1", "H320", "H321", "XN2", "XN3")])
    (SQ0, SQ1, ACC, RS), _ = region(R5 + 2 * size([P, KC, T]), [(n, [P, T]) for n in ("SQ0", "SQ1", "ACC", "RS")])
    (ZS, XC, dtT), o = region(R5, [("ZS", [P, 4, T]), ("XC", [P, 6, T]), ("dtT", [P, T])])
    TINY = ("XR", "AB", "EX", "DN", "RD", "Z1", "Z2", "PL", "DT", "LA", "CS", "DF", "WW", "AA")
    tiny, o = region(o, [(n, [P, 4, 16]) for n in TINY])
    XR, AB, EX, DN, RD, Z1, Z2, PL, DT, LA, CS, DF, WW, AA = tiny
    (DEC,), U0 = region(o, [("DEC", [P, 4, 8])])
    (QC, CK, KR, GC, GB, CV0, CV1), o = region(U0, [("QC", [P, 2, T]), ("CK", [P, T]), ("KR", [P, T]), ("GC", [P, 2, T]), ("GB", [P, 2, T]), ("CV0", [P, T]), ("CV1", [P, T])])
    (XP0, XP1, TP), o = region(o, [("XP0", [P, 2, 258]), ("XP1", [P, 2, 258]), ("TP", [P, 2, 2, 258])])
    (Sin, ST, XTK), o = region(U0, [("Sin", [P, 4, 512]), ("ST", [P, 4, 512]), ("XTK", [P, 4, 640])])
    CST = dtT
    (FH, FL), _ = region(R5, [("FH", [P, KC, T], F32R), ("FL", [P, KC, T], F32R)])
    (R320, R321, FQ0, FQ1), _ = region(R5 + 2 * size([P, KC, T]), [(n, [P, T]) for n in ("R320", "R321", "FQ0", "FQ1")])
    XP, CV, PR, PT = [XP0, XP1], [CV0, CV1], [PR0, PR1], [PT0, PT1]
    MM_, Ce, ec, Bd = [M0, M1], [Ce0, Ce1], [ec0, ec1], [Bd0, Bd1]
    XN, H32, SQ, R32, FQ = [XN0, XN1, XN2, XN3], [H320, H321], [SQ0, SQ1], [R320, R321], [FQ0, FQ1]
    (HA, LA_, YH, YL), o = region(R3, [("HA", [P, KC, SEQ], F32R), ("LA2", [P, KC, SEQ], F32R), ("YH", [P, KC, SEQ], F32R), ("YL", [P, KC, SEQ], F32R)])
    (mask_a, mask_b, ptok), o = region(o, [("mask_a_sb", [P, 1152]), ("mask_b_sb", [P, 384]), ("ptok", [P, 2, LAYERS, 256])])
    (SH0, SH1, RR0, RR1, YA0, YA1, A0), o = region(o, [(n, [P, SEQ]) for n in ("SH0", "SH1", "RR0", "RR1")] + [("YA0", [P, 2, SEQ]), ("YA1", [P, 2, SEQ]), ("APT", [P, 1152])])
    APT = A0
    (PH, PL_), _ = region(o, [("PH", [P, 2, SEQ], F32R), ("PLo", [P, 2, SEQ], F32R)])
    (AP0, AP1), o = region(o, [("AP0", [P, 1152]), ("AP1", [P, 1152])])
    (AZ0, AZ1), o = region(o, [("AZ0", [P, 2, SEQ]), ("AZ1", [P, 2, SEQ])])
    S0 = o
    (AQ0, AQ1, AK0, AK1, AV0, AV1), o = region(o, [(n, [P, 3, 2, SEQ]) for n in ("AQ0", "AQ1", "AK0", "AK1", "AV0", "AV1")])
    (V32, PJ, SQ8, YO0, YO1), _ = region(S0, [("V32", [P, KC, SEQ]), ("PJ", [P, KC, SEQ]), ("SQ8", [P, KC, SEQ])] + [(f"YO{i}", [P, D]) for i in (0, 1)])
    YO = [YO0, YO1]
    SH, RR, YA, AP_, AZ, AQ, AK, AV = [SH0, SH1], [RR0, RR1], [YA0, YA1], [AP0, AP1], [AZ0, AZ1], [AQ0, AQ1], [AK0, AK1], [AV0, AV1]

    banks = [nc.alloc_psum_tensor(f"bank{i}", [P, 512], F32).ap() for i in range(4)]
    wide = nc.alloc_psum_tensor("bank45", [P, 1024], F32).ap()
    banks += [wide[:, 0:512], wide[:, 512:1024]]
    banks += [nc.alloc_psum_tensor(f"bank{i}", [P, 512], F32).ap() for i in (6, 7)]
    bank_of = {}
    raw_in = [nc.alloc_semaphore(f"raw_in{i}") for i in range(RAW_SLOTS)]
    consts_in = nc.alloc_semaphore("consts_in")
    small_w_in = nc.alloc_semaphore("small_w_in")
    masks_in = nc.alloc_semaphore("masks_in")
    stored = nc.alloc_semaphore("stored")

    units, steps = [], []

    def fm(w, rows, col, n, blocks, kind, key, x, t, between=None):
        src = w[rows:rows + D, col:col + n].rearrange("(k p) n -> p k n", p=P)
        u = Unit(kind, [(0, 8 * n, src)], n, key, len(units), blocks, x, t)
        units.append(u)
        unit_steps(u, between)

    def unit_steps(u, between):
        if between:
            u.first_half_done = True
            steps.append(("first_half", u))
            between()
        steps.append(("unit", u))

    def proj_unit(i, part, between=None):
        pw = A["ple_w_proj_2"][i]
        loads = [(512 * h, 512, pw[:, 512 * part + 256 * h:512 * part + 256 * h + 256].rearrange("(k p) n -> p k n", p=P)) for h in (0, 1)]
        u = Unit("proj", loads, 256, (i, part), len(units), None, ("p2", i))
        units.append(u)
        unit_steps(u, between)

    def mod_units(l, a, b):
        for i in range(a, b):
            fm(A["w_mod"][l], 0, 256 * i, 256, [(0, 256)], "mod", (l, i), None, None)

    two = [(0, P), (P, P)]

    def w_in_units(l):
        t1 = ALL if l == 0 else X
        w, x = A["w_in"][l], ("h", l, "mix")
        fm(w, 0, COL_KV, 160, [(0, P), (P, 32)], "win", (l, "kv"), x, [ALL] * 2)
        fm(w, 0, 0, 256, two, "win", (l, "q"), x, [t1] * 2)
        fm(w, 0, COL_XBC + 512, 272, two + [(256, 16)], "win", (l, "bc"), x, [ALL] * 3)
        fm(w, 0, COL_XBC, 256, two, "win", (l, "xs0"), x, [ALL] * 2)
        fm(w, 0, COL_XBC + 256, 256, two, "win", (l, "xs1"), x, [ALL] * 2)
        fm(w, 0, COL_GC, 256, two, "win", (l, "gc"), x, [t1] * 2)
        fm(w, 0, COL_VAL, 256, two, "win", (l, "val"), x, [t1] * 2)
        fm(w, 0, COL_GB, 256, two, "win", (l, "gb"), x, [t1] * 2)
        fm(w, 0, COL_Z, 256, two, "win", (l, "z0"), x, [t1] * 2)
        fm(w, 0, COL_Z + 256, 256, two, "win", (l, "z1"), x, [t1] * 2)

    steps.append(("init",))
    steps.append(("silu_c",))
    mod_units(0, 0, 8)
    steps.append(("mod_flush",))
    for l in range(LAYERS):
        t1 = ALL if l == 0 else X
        steps.append(("mod_fuse", l, "mix"))
        steps.append(("norm", l, "mix"))
        w_in_units(l)
        steps.append(("mla_norm", l))
        steps.append(("mla_proj", l))
        att = [(l, h, sg) for h in range(MLA_HEADS) for sg in ((0, 1) if l == 0 else (1,))]
        fill = [(0, i) for i in range(8, 24)] + [(1, i) for i in range(0, 24)] if l == 0 else []

        def filler(n):
            for _ in range(n):
                if fill:
                    ll, i = fill.pop(0)
                    mod_units(ll, i, i + 1)

        for i in range(len(att) + 1):
            steps.append(("mla_att", att, i))
            filler(1)
        steps.append(("short_conv", l))
        filler(1)
        steps.append(("ssd_dt", l))
        filler(4)
        steps.append(("ssd_cs", l))
        filler(2)
        steps.append(("ssd_tok", l))
        steps.append(("ssd_g", l))
        filler(1)
        for c in range(CHUNKS):
            steps.append(("ssd_state", l, c))
            filler(1)
        steps.append(("ssd_rec", l))
        for h in range(SSD_HEADS + 1):
            steps.append(("ssd_head", l, h))
            filler(1)
        steps.append(("ssd_out", l))
        filler(40)
        if l == 0:
            steps.append(("mod_flush",))
        steps.append(("y_split", l))
        steps.append(("mod_fuse", l, "g1"))
        for i in range(4):
            fm(A["w_out"][l], 0, 256 * i, 256, two, "wout", (l, i), ("y", l), [t1] * 2)
        steps.append(("post", l, "mix"))
        steps.append(("mod_fuse", l, "ffn"))
        steps.append(("norm", l, "ffn"))
        for g in range(4):
            for i in range(4):
                fm(A["w_ff1"][l], 0, g * D + 256 * i, 256, two, "ff1", (l, g, i), ("h", l, "ffn"), [t1] * 2)
            for i in range(4):
                fm(A["w_ff2"][l], g * D, 256 * i, 256, two, "ff2", (l, g, i), ("f", l, g), [t1] * 2)
        steps.append(("mod_fuse", l, "g2"))
        steps.append(("post", l, "ffn"))
    seq2 = [(0, SEQ)] * 2
    steps.append(("split2", 0))
    aw = A["a_w_in_2"][0]
    heads = []

    def att2_step():
        n = len(heads)
        i = n // (HEADS + 2)
        h = n % (HEADS + 2)
        heads.append(n)
        steps.append(("att2", *((i, h - lag) if 0 <= h - lag < HEADS else None for lag in range(3))))

    for i in range(LAYERS):
        x = ("x2", i)
        if i == 0:
            for hq in range(4):
                us = [(3 * g * D + off + 256 * hq, "a" + what, g) for g in range(3) for what, off in (("q", 0), ("k", D))]
                us += [(9 * D + 256 * hq, "az", 0)] + [(3 * g * D + 2 * D + 256 * hq, "av", g) for g in range(3)]
                for n, (col, kind, g) in enumerate(us):
                    fm(aw, 0, col, 256, two, kind, (i, hq, g), x, seq2)
                    if hq > 0 and n < 4 or hq == 3 and n >= 7:
                        att2_step()
            att2_step()
            att2_step()
        else:
            src = A["b_w_in_2"][0]
            fm(src, 0, D, 256, [(0, P), (P, P)], "bkv", (i, 0), x, seq2)
            for hq in range(4):
                fm(src, 0, 256 * hq, 256, two, "aq", (i, hq, 0), x, seq2, att2_step if hq > 0 else None)
                if hq > 0:
                    att2_step()
                fm(src, 0, D + 256 + 256 * hq, 256, two, "az", (i, hq, 0), x, seq2, att2_step)
                att2_step()
            att2_step()
            att2_step()
            att2_step()
        for j in range(4):
            fm(A["a_w_out_2" if i == 0 else "b_w_out_2"][0], 0, 256 * j, 256, two, "out2", (i, j), ("y2", i), seq2,
               att2_step if j == 0 else None)
        steps.append(("p_split", i))
        steps.append(("ln_sum", i))
        proj_unit(i, 0)
        steps.append(("ln", i))
        proj_unit(i, 1)
        for j in range(4):
            fm(A["ple_w_gate_2"][i], 0, 256 * j, 256, two, "gate", (i, j), ("g2", i), seq2)
    steps.append(("out",))

    slot_due = [0] * RAW_SLOTS
    for u in units:
        slot_due[u.id % RAW_SLOTS] += 16 * len(u.loads)
        u.raw_due = slot_due[u.id % RAW_SLOTS]
    N_HALF = 2 * len(units)
    mods = [u.key for u in units if u.kind == "mod"]
    mod_no = {key: n for n, key in enumerate(mods)}

    last_win = {u.key[0]: u.id for u in units if u.kind == "win"}
    mla_last = {l: (l, MLA_HEADS - 1, 1) for l in range(LAYERS)}
    all_heads = [st[1] for st in steps if st[0] == "att2" and st[1]]
    before_head = dict(zip(all_heads, [None] + all_heads[:-1]))
    before_head[None] = None
    mod_step = {st[1].key: n for n, st in enumerate(steps) if st[0] == "unit" and st[1].kind == "mod"}

    def half_size(u):
        return 2 * u.n if u.kind == "proj" else 4 * u.n

    def segs(t):
        return [(s, slice(SEQ * s, SEQ * s + SEQ)) for s in (0, 1) if t[0] <= SEQ * s < t[1]]

    def vec(l, name, j=0, n=None):
        a, m = VEC[name]
        return VT[l][:, a + j:a + j + (n or 1)]

    def vec2(name, j=0, n=1):
        a, _ = VEC2[name]
        return VT[2][:, a + j:a + j + n]

    def bc(ap, shape):
        return ap.broadcast_to(shape)

    def t_of(l):
        return ALL if l == 0 else X

    def x_parts(u):
        kind = u.x[0]
        if kind in ("h", "y"):
            return HH, HL
        if kind == "f":
            return FH, FL
        if kind == "p2":
            return PH, PL_
        return parts2(kind, u.x[1])

    def parts2(kind, i):
        return (HA, LA_) if (kind == "y2") == (i == 1) else (YH, YL)

    block = nc.Block()
    ctx_block = block.__enter__()

    @ctx_block.sync
    def _(engine):
        sp = Waits(engine)
        def load(dst, src, s):
            nc.sync.dma_start(dst, src).then_inc(s, 16)

        for j in range(2):
            load(xtok[:, j, :], A["ctx"][0, j * P:(j + 1) * P, :], consts_in)
            load(xtok[:, 2 + j, :], A["x"][0, j * P:(j + 1) * P, :], consts_in)
        n = 4
        for name, dst in (("ident", ident), ("rope", rope), ("axial", axial), ("tri", tri), ("tri_neg", tri_neg), ("last", last)):
            load(dst, A["k_" + name], consts_in)
            n += 1
        load(sel[0:16], A["k_sel"], consts_in)
        n += 1
        for l in range(LAYERS):
            for name, (r, m) in VEC.items():
                src = A[name][l]
                if name in ("sc_conv_w", "ssd_conv_w"):
                    src = src.rearrange("a (b p) -> (a b) p", p=P)
                else:
                    src = src.rearrange("(a p) -> a p", p=P)
                load(vrow[r:r + m, l, :], src, consts_in)
                n += 1
        for name, (r, m) in VEC2.items():
            if name == "c":
                src = A["c"][0]
            elif name == "c_ctx":
                src = A["c_ctx"]
            else:
                src = A[name[:4] + "_2"][int(name[-1])]
            load(vrow[r:r + m, 2, :], src.rearrange("(a p) -> a p", p=P), consts_in)
            n += 1
        for l in range(LAYERS):
            load(dt_bias[:, l, :], A["ssd_dt_bias"][l].rearrange("a b -> (a b)").partition_broadcast(P), consts_in)
            load(a_log[:, l, :], A["ssd_a_log"][l].rearrange("a b -> (a b)").partition_broadcast(P), consts_in)
            for odd in (0, 1):
                with nc.allow_non_contiguous_dma(reason="eight values per layer"):
                    load(d_skip[64 * odd:64 * odd + 64, l, :],
                         A["ssd_d"][l].rearrange("(j two) -> two j", two=2)[odd].partition_broadcast(64), consts_in)
            n += 4
        load(sinks, A["b_sinks_2"][0].partition_broadcast(P), consts_in)
        n += 1
        assert counts is None or n == CONSTS, n
        where["consts"] = n

        def small_weights(l):
            load(w_uq, A["w_uq"][l].rearrange("(k p) n -> p k n", p=P), small_w_in)
            load(w_ukv, A["w_ukv"][l], small_w_in)

        small_weights(0)
        for u in units:
            if u.id >= RAW_SLOTS:
                sp.wait_ge(s_lo_ready, s_lo_ready.at(2 * (u.id - RAW_SLOTS) + 1))
            for off, width, src in u.loads:
                dst = raw[u.id % RAW_SLOTS][:, off:off + width].rearrange("p (k n) -> p k n", n=u.n)
                load(dst, src, raw_in[u.id % RAW_SLOTS])
            if u.kind == "win" and u.key == (1, "kv"):
                sp.wait_ge(s_mla_q, s_mla_q.at((0, MLA_HEADS - 1)))
                small_weights(1)
            if u.kind == "aq" and u.key == (0, 0, 0):
                sp.wait_ge(s_parts2, s_parts2.at((0, KC - 1)))
                load(mask_a, A["k_mask_a"], masks_in)
                load(mask_b, A["k_mask_b"], masks_in)
                for i in range(LAYERS):
                    load(ptok[:, :, i, :], A["p_2"][i, 0].rearrange("(a p) n -> p a n", p=P), masks_in)
        for j in range(2):
            sp.wait_ge(s_out_rows, s_out_rows.at((j, 1)))
            load(out[0, j * P:(j + 1) * P, :], YO[j], stored)
        engine.wait_ge(stored, 32)

    @ctx_block.tensor
    def _(engine):
        pe = Waits(engine)
        readers = [()] * 8

        def acquire(b, *read_by):
            for signal, key in readers[b]:
                pe.wait_ge(signal, signal.at(key))
            readers[b] = read_by
            return banks[b]

        gemm_turn = [0]

        def next_bank(tag, *read_by):
            gemm_turn[0] += 1
            bank_of[tag] = gemm_turn[0] % 3
            return acquire(gemm_turn[0] % 3, *read_by)

        def block_readers(u, bi):
            if u.kind == "win":
                return ((s_val if u.key[1] == "val" else s_u_out, u.key + (bi,)),)
            if u.kind in ("aq", "ak"):
                return ((s_cos2, u.key + (u.kind, bi)),)
            if u.kind == "bkv":
                return ((s_cos2, u.key + ("kb", 0)),) if bi == 0 else ((s_vb2, bi - 1),)
            signal = {"wout": s_y_copy, "ff1": s_relu, "ff2": s_f_add, "av": s_v2, "az": s_z2, "gate": s_sg, "out2": s_v32}[u.kind]
            return ((signal, u.key + (bi,)),)

        def mm3(o, wh, wl, xh, xl, start, stop):
            nc.tensor.matmul(o, wh, xh, start=start, stop=False)
            nc.tensor.matmul(o, wh, xl, start=False, stop=False)
            return nc.tensor.matmul(o, wl, xh, start=False, stop=stop)

        pending, open_ = [], {}

        def mod_flush():
            if pending:
                key = pending.pop()
                pe.wait_ge(s_mod_row, s_mod_row.at(key))
                b = acquire(6, (s_mod_t, key))
                for j in range(2):
                    ins = nc.tensor.transpose(b[:, 4 * j:4 * j + 4], mrow[mod_no[key] % 2][0:4, j * P:(j + 1) * P], ident[0:4, 0:4])
                ins.then_inc(*s_mod_col.tick(key))

        def unit(u, halves=(0, 1)):
            if u.kind == "mod":
                b = next_bank((u.id, 0), (s_mod_row, u.key))
                pe.wait_ge(s_cs, s_cs.at(0))
                for half in (0, 1):
                    s = (2 * u.id + half) % HALF_SLOTS
                    pe.wait_ge(s_lo_ready, s_lo_ready.at(2 * u.id + half))
                    for kk in range(4):
                        k = 4 * half + kk
                        for w in (whi[s], wlo[s]):
                            ins = nc.tensor.matmul(b[0:4, 0:256], cs[:, k, :], w[:, kk * 256:kk * 256 + 256],
                                            start=(k == 0 and w is whi[s]), stop=(k == KC - 1 and w is wlo[s]))
                    ins.then_inc(*s_gemm.tick(("half", 2 * u.id + half), ("blk", u.id, half)))
                mod_flush()
                pending.append(u.key)
                return
            if u.kind == "proj":
                xh, xl = x_parts(u)
                for half in halves:
                    s = (2 * u.id + half) % HALF_SLOTS
                    pe.wait_ge(s_lo_ready, s_lo_ready.at(2 * u.id + half))
                    for j in range(2):
                        m = 4 * u.key[1] + 2 * half + j
                        b = next_bank((u.id, 2 * half + j), (s_pj, (u.key[0], m)))
                        for k in range(2):
                            pe.wait_ge(s_p_lo, s_p_lo.at(u.key[0]))
                            w = slice(k * 256 + j * P, k * 256 + j * P + P)
                            ins = mm3(b[:, 0:SEQ], whi[s][:, w], wlo[s][:, w], xh[:, k, :], xl[:, k, :], k == 0, k == 1)
                        keys = [("blk", u.id, 2 * half + j)] + ([("half", 2 * u.id + half)] if j == 1 else [])
                        ins.then_inc(*s_gemm.tick(*keys))
                return
            xh, xl = x_parts(u)
            ready = {"h": s_parts, "y": s_parts_y, "f": s_parts_f, "x2": s_parts2, "y2": s_parts_y2, "g2": s_parts_g2}[u.x[0]]
            for half in halves:
                s = (2 * u.id + half) % HALF_SLOTS
                pe.wait_ge(s_lo_ready, s_lo_ready.at(2 * u.id + half))
                for bi, (c0, m) in enumerate(u.blocks):
                    t = u.t[bi]
                    token_major = u.kind == "av" or (u.kind == "bkv" and bi == 1)
                    if half == 0:
                        if token_major and u.kind == "bkv":
                            open_[bi] = tuple(next_bank((u.id, 1 + tt), *block_readers(u, 1 + tt)) for tt in (0, 1))
                        else:
                            open_[bi] = next_bank((u.id, bi), *block_readers(u, bi))
                    b = open_[bi]
                    for kk in range(4):
                        k = 4 * half + kk
                        pe.wait_ge(ready, ready.at(u.x[1:] + (k,)))
                        first, final = k == 0, k == KC - 1
                        if u.kind == "av":
                            ts_ = slice(bi * P, bi * P + P)
                            w = slice(kk * u.n, kk * u.n + 256)
                            o = b[:, 0:256]
                            nc.tensor.matmul(o, xh[:, k, ts_], whi[s][:, w], start=first, stop=False)
                            nc.tensor.matmul(o, xh[:, k, ts_], wlo[s][:, w], start=False, stop=False)
                            ins = nc.tensor.matmul(o, xl[:, k, ts_], whi[s][:, w], start=False, stop=final)
                        elif token_major:
                            w = slice(kk * u.n + c0, kk * u.n + c0 + m)
                            for tt in (0, 1):
                                ts_ = slice(tt * P, tt * P + P)
                                o = b[tt][:, 0:P]
                                nc.tensor.matmul(o, xh[:, k, ts_], whi[s][:, w], start=first, stop=False)
                                nc.tensor.matmul(o, xh[:, k, ts_], wlo[s][:, w], start=False, stop=False)
                                ins = nc.tensor.matmul(o, xl[:, k, ts_], whi[s][:, w], start=False, stop=final)
                        else:
                            w = slice(kk * u.n + c0, kk * u.n + c0 + m)
                            ins = mm3(b[0:m, 0:t[1] - t[0]], whi[s][:, w], wlo[s][:, w],
                                      xh[:, k, t[0]:t[1]], xl[:, k, t[0]:t[1]], first, final)
                    keys = []
                    if bi == len(u.blocks) - 1:
                        keys.append(("half", 2 * u.id + half))
                    if half == 1:
                        keys.append(("blk", u.id, bi))
                    if keys:
                        ins.then_inc(*s_gemm.tick(*keys))

        def init():
            engine.wait_ge(consts_in, 16 * CONSTS)
            pe.wait_ge(s_ones, s_ones.at(0))
            for i in range(3):
                n = VEC_ROWS if i < 2 else VEC2_ROWS
                b = next_bank(("vec", i), (s_vt, i))
                nc.tensor.transpose(b[:, 0:n], vrow[0:n, i, :], ident[0:n, 0:n]).then_inc(*s_init_t.tick(("vec", i)))
            for k in range(KC):
                b = next_bank(("x", k), (s_xt, k))
                for j in range(4):
                    ins = nc.tensor.transpose(b[:, j * P:(j + 1) * P], xtok[:, j, k * P:(k + 1) * P], ident)
                ins.then_inc(*s_init_t.tick(("x", k)))

        def total(summed, key, src, n, ready, ready_key, read_by):
            b = acquire(7, read_by)
            pe.wait_ge(ready, ready.at(ready_key))
            nc.tensor.matmul(b[:, 0:n], ones, src, start=True, stop=True).then_inc(*summed.tick(key))

        def mla_norm(l):
            t = t_of(l)
            n = t[1] - t[0]
            b = acquire(3, (s_inv, ("mla", l, "kv")))
            pe.wait_ge(s_mla_sq, s_mla_sq.at((l, 2)))
            nc.tensor.matmul(b[:, 0:T], ones, RSM[:, 0, :], start=True, stop=True).then_inc(*s_mla_sum.tick(("mla", l, "kv")))
            b = acquire(4, (s_inv, ("mla", l, "q")))
            for j in (0, 1):
                ins = nc.tensor.matmul(b[:, 0:n], ones, SQM[:, j, t[0]:t[1]], start=j == 0, stop=j == 1)
            ins.then_inc(*s_mla_sum.tick(("mla", l, "q")))

        def mla_proj(l):
            t = t_of(l)
            n = t[1] - t[0]
            engine.wait_ge(small_w_in, 32 * (l + 1))
            pe.wait_ge(s_mla_n, s_mla_n.at((l, "kv")))
            for h in range(MLA_HEADS):
                b = acquire(3 + h % 2, (s_kt, (l, h)))
                nc.tensor.matmul(b[0:NOPE, 0:T], w_ukv[:, h * P:h * P + NOPE], CK, start=True, stop=True)\
                    .then_inc(*s_mla_k.tick((l, h)))
            for j in range(4):
                b = acquire(5 + j % 2, (s_vv, (l, j)))
                nc.tensor.matmul(b[:, 0:256].rearrange("p (h d) -> p h d", h=4), CK[:, j * P:(j + 1) * P],
                          w_ukv.rearrange("p (h d) -> p h d", h=4)[:, :, NOPE:P], start=True, stop=True)\
                    .then_inc(*s_mla_v.tick((l, j)))
            pe.wait_ge(s_mla_n, s_mla_n.at((l, "q")))
            for h in range(MLA_HEADS):
                b = acquire(3 + h % 2, (s_qt, (l, h)))
                for k in range(2):
                    ins = nc.tensor.matmul(b[0:QK, 0:n], w_uq[:, k, h * QK:(h + 1) * QK], QC[:, k, t[0]:t[1]], start=k == 0, stop=k == 1)
                ins.then_inc(*s_mla_q.tick((l, h)))

        def mla_att(att, i):
            if i < len(att):
                l, h, sg = att[i]
                nk = T if sg else SEQ
                pe.wait_ge(s_mla_qr, s_mla_qr.at(l))
                pe.wait_ge(s_mla_kr, s_mla_kr.at(l))
                pe.wait_ge(s_vv, s_vv.at((l, 3)))
                for j in range(2):
                    b = acquire(3 + j, (s_mla_e, (att[i], j)))
                    q0 = sg * SEQ + j * P
                    nc.tensor.matmul(b[:, 0:nk], QT[0:QK, h, q0:q0 + P], KT[0:QK, h, 0:nk], start=True, stop=True)\
                        .then_inc(*s_mla_s.tick((att[i], j)))
            if i > 0:
                l, h, sg = att[i - 1]
                nt = 4 if sg else 2
                for j in range(2):
                    pe.wait_ge(s_mla_p, s_mla_p.at((att[i - 1], j)))
                    b = acquire(5 + j, (s_mla_pt, (att[i - 1], j)))
                    for kt in range(nt):
                        ins = nc.tensor.transpose(b[:, kt * P:kt * P + P], PR[j][:, kt * P:kt * P + P], ident)
                    ins.then_inc(*s_mla_t.tick((att[i - 1], j)))
                b = acquire(7, (s_mla_y, att[i - 1]))
                for kt in range(nt):
                    pe.wait_ge(s_mla_pt, s_mla_pt.at((att[i - 1], 1)))
                    ins = nc.tensor.matmul(b[:, 0:SEQ], VV[:, kt, (h // 2) * P:(h // 2) * P + P], PT[(i - 1) % 2][:, kt, :],
                                    start=kt == 0, stop=kt == nt - 1)
                ins.then_inc(*s_mla_o.tick(att[i - 1]))

        def ssd_dt(l):
            pe.wait_ge(s_u_out, s_u_out.at((l, "bc", 2)))
            b = acquire(3, (s_xr, l))
            for c in range(CHUNKS):
                ins = nc.tensor.transpose(b[:, c * 16:c * 16 + 16], dtT[0:16, c * P:(c + 1) * P], ident[0:16, 0:16])
            ins.then_inc(*s_ssd_a.tick((l, "dt")))

        def ssd_cs(l):
            pe.wait_ge(s_la, s_la.at(l))
            b = acquire(3, (s_cs_tok, l))
            for d in (0, 1):
                ins = nc.tensor.matmul(b[:, 32 * d:32 * d + 32].rearrange("p (c h) -> p c h", c=4), tri[:, d, :],
                                LA[:, :, 8 * d:8 * d + 8], start=True, stop=True)
            ins.then_inc(*s_ssd_a.tick((l, "cs")))
            pe.wait_ge(s_cs_tok, s_cs_tok.at(l))
            b = acquire(4, (s_df, l), (s_dec, l))
            for d in (0, 1):
                ins = nc.tensor.matmul(b[:, 32 * d:32 * d + 32].rearrange("p (c h) -> p c h", c=4), last[:, d, :],
                                CS[:, :, 8 * d:8 * d + 8], start=True, stop=True)
            ins.then_inc(*s_ssd_a.tick((l, "last")))
            b = acquire(5, (s_cst, l))
            for c in range(CHUNKS):
                ins = nc.tensor.transpose(b[0:16, c * P:(c + 1) * P], CS[:, c, :], ident)
            ins.then_inc(*s_ssd_a.tick((l, "cst")))

        def ssd_tok(l):
            for j in range(5):
                pe.wait_ge(s_xc, s_xc.at((l, j)))
                b = acquire(3 + j % 2, (s_xtk, (l, j)))
                for c in range(CHUNKS):
                    ins = nc.tensor.transpose(b[:, c * P:(c + 1) * P], XC[:, j, c * P:(c + 1) * P], ident)
                ins.then_inc(*s_ssd_tk.tick((l, j)))

        def ssd_g(l):
            pe.wait_ge(s_xc, s_xc.at((l, 5)))
            for g in (0, 1):
                b = acquire(5 + 2 * g, (s_gt, (l, g)))
                r = slice(64 * g, 64 * g + 64)
                for c in range(CHUNKS):
                    ins = nc.tensor.matmul(b[:, c * P:(c + 1) * P], XC[r, 4, c * P:(c + 1) * P], XC[r, 5, c * P:(c + 1) * P],
                                    start=True, stop=True)
                ins.then_inc(*s_ssd_gt.tick((l, g)))

        def ssd_state(l, c):
            b = acquire(3 + c % 2, (s_st, (l, c)))
            pe.wait_ge(s_xtk, s_xtk.at((l, 3)))
            for g in (0, 1):
                pe.wait_ge(s_bd, s_bd.at((l, c, g)))
                for h4 in range(4):
                    h = 4 * g + h4
                    ins = nc.tensor.matmul(b[:, 64 * h:64 * h + 64], Bd[g][:, P * h4:P * h4 + P], XTK[:, c, 64 * h:64 * h + 64],
                                    start=True, stop=True)
                ins.then_inc(*s_ssd_st.tick((l, c, g)))

        def ssd_head(l, h):
            cc = range(CHUNKS) if l == 0 else range(2, 4)
            t0 = cc[0] * P
            n = len(cc) * P
            if h < SSD_HEADS:
                for d in (0, 1):
                    pe.wait_ge(s_cst, s_cst.at(l))
                    b = acquire(3 + d, (s_ed, (l, h, d)))
                    nc.tensor.matmul(b[:, 0:n], sel[0:16, 8 * d + h, :], CST[0:16, t0:T], start=True, stop=True)\
                        .then_inc(*s_ssd_row.tick((l, h, d)))
            if h > 0:
                g = h - 1
                pe.wait_ge(s_ssd_m, s_ssd_m.at((l, g)))
                pe.wait_ge(s_rec, s_rec.at(l))
                b = acquire(5 if g % 2 else 7, (s_ssd_ys, (l, g)))
                for c in cc:
                    o = b[:, c * P - t0:c * P - t0 + P]
                    nc.tensor.matmul(o, XTK[:, c, P * (g // 2):P * (g // 2) + P], MM_[g % 2][:, c * P:(c + 1) * P], start=True, stop=False)
                    ins = nc.tensor.matmul(o, Sin[:, c, P * (g // 2):P * (g // 2) + P], Ce[g % 2][:, c * P:(c + 1) * P], start=False, stop=True)
                ins.then_inc(*s_ssd_y.tick((l, g)))

        def ssd_out(l):
            t = t_of(l)
            n = t[1] - t[0]
            for g in (0, 1):
                b = acquire(3 + g, (s_inv, ("ssd", l, g)))
                for j in (0, 1):
                    pe.wait_ge(s_ssd_sq, s_ssd_sq.at((l, 2 * g + j)))
                    ins = nc.tensor.matmul(b[:, 0:n], ones, SQS[:, 2 * g + j, t[0]:t[1]], start=j == 0, stop=j == 1)
                ins.then_inc(*s_ssd_sum.tick(("ssd", l, g)))

        def norm(l, which):
            t = ALL if which == "mix" else t_of(l)
            b = acquire(7, (s_inv, ("n", l, which)))
            for k in range(KC):
                pe.wait_ge(s_sq, s_sq.at(("n", l, which, k)))
                nc.tensor.matmul(b[:, 0:t[1] - t[0]], ones, SQ[k % 2][:, t[0]:t[1]], start=k == 0, stop=k == KC - 1)\
                    .then_inc(*s_norm_sum.tick(("n", l, which, k), *([("n", l, which)] if k == KC - 1 else [])))

        def post(l, which):
            t = t_of(l)
            total(s_norm_sum, ("p", l, which), ACC[:, t[0]:t[1]], t[1] - t[0], s_acc, ("p", l, which, KC - 1), (s_inv, ("p", l, which)))

        def att2(ih):
            i, h = ih
            G = 3 if i == 0 else 1
            buf, hl = (h // 4) % 2, h % 4
            blk, r = hl // 2, slice(64 * (hl % 2), 64 * (hl % 2) + 64)
            q = AQ[buf]
            b0 = acquire(3, (s_mx2, (ih, 0)))
            acquire(4, (s_mx2, (ih, 1)))
            acquire(5, (s_mx2, (ih, 1)))
            for g in range(G):
                pe.wait_ge(s_rope2, s_rope2.at((i, h // 4, g, "aq", blk)))
                if i == 0:
                    pe.wait_ge(s_rope2, s_rope2.at((i, h // 4, g, "ak", blk)))
                    k_ = AK[buf][r, g, blk, :]
                else:
                    pe.wait_ge(s_rope2, s_rope2.at((1, 0, "kb", 0)))
                    k_ = AK[0][r, 0, h // 8, :]
                nc.tensor.matmul(b0[:, g * P:(g + 1) * P], q[r, g, blk, 0:P], k_[:, 0:P], start=True, stop=True)
                ins = nc.tensor.matmul(wide[:, g * SEQ:(g + 1) * SEQ], q[r, g, blk, P:SEQ], k_, start=True, stop=True)
            ins.then_inc(*s_s2.tick(ih))

        def att2_turn(ih, batches):
            i, h = ih
            G = 3 if i == 0 else 1
            p_ = AP_[h % 2]
            pe.wait_ge(s_p2, s_p2.at((ih, 1)))
            dst = []
            for g in range(G):
                dst += [(g * SEQ, g * P), (g * SEQ + P, G * P + g * SEQ)]
            for g in range(G):
                dst += [(G * SEQ + g * P, G * P + g * SEQ + P)]
            for n in batches:
                b = acquire(6 if n % 2 == 0 else 7, (s_pt2, (ih, n)))
                for o, src in dst:
                    if o // 512 == n:
                        ins = nc.tensor.transpose(b[:, o % 512:o % 512 + P], p_[:, src:src + P], ident)
                ins.then_inc(*s_t2.tick((ih, n)))

        def att2_pv(ih):
            i, h = ih
            G = 3 if i == 0 else 1
            buf, hl = (h // 4) % 2, h % 4
            blk = hl // 2
            pe.wait_ge(s_pt2, s_pt2.at((ih, (G * 384 - 1) // 512)))
            b = acquire(7, (s_ya, ih))
            if i == 0:
                for g in range(G):
                    pe.wait_ge(s_v2, s_v2.at((i, h // 4, g, 0)))
                    pe.wait_ge(s_v2, s_v2.at((i, h // 4, g, 1)))
            else:
                pe.wait_ge(s_vb2, s_vb2.at(1))

            def v(g, kt):
                return AV[buf][:, g, kt, blk * P:blk * P + P] if i == 0 else AV[0][:, h // 8, kt, 0:P]

            for g in range(G):
                nc.tensor.matmul(b[:, 0:SEQ], v(g, 0), APT[:, g * SEQ:(g + 1) * SEQ], start=g == 0, stop=False)
            for g in range(G):
                ins = nc.tensor.matmul(b[:, P:SEQ], v(g, 1), APT[:, G * SEQ + g * P:G * SEQ + (g + 1) * P], start=False, stop=g == G - 1)
            ins.then_inc(*s_o2.tick(ih))

        def ln_sum(i):
            total(s_ln_total, (i, "mean"), RR[0], SEQ, s_ln_acc, (i, "mean"), (s_ln_stat, (i, "mean")))

        def ln(i):
            b = acquire(7, (s_inv, ("ln", i)))
            for k in range(KC):
                pe.wait_ge(s_ln_sq, s_ln_sq.at((i, k)))
                ins = nc.tensor.matmul(b[:, 0:SEQ], ones, SQ8[:, k, :], start=k == 0, stop=k == KC - 1)
            ins.then_inc(*s_ln_total.tick(("ln", i)))

        def p_split(i):
            engine.wait_ge(masks_in, 64)
            b = acquire(6, (s_p_lo, i))
            for k in range(2):
                for j in range(2):
                    ins = nc.tensor.transpose(b[:, k * SEQ + j * P:k * SEQ + (j + 1) * P], ptok[:, j, i, k * P:(k + 1) * P], ident)
            ins.then_inc(*s_p_t.tick(i))

        def out_step():
            for j in range(2):
                for k in range(KC):
                    if k % 4 == 0:
                        b = acquire(3 + k // 4, (s_out_rows, (j, k // 4)))
                    pe.wait_ge(s_x2_new, s_x2_new.at((1, k)))
                    ins = nc.tensor.transpose(b[:, (k % 4) * P:(k % 4) * P + P], XT[:, k, SEQ + j * P:SEQ + (j + 1) * P], ident)
                    if k % 4 == 3:
                        ins.then_inc(*s_out_t.tick((j, k // 4)))

        for st in steps:
            kind, args = st[0], st[1:]
            if kind == "unit":
                unit(args[0], (1,) if args[0].first_half_done else (0, 1))
            elif kind == "first_half":
                unit(args[0], (0,))
            elif kind == "init":
                init()
            elif kind == "mod_flush":
                mod_flush()
            elif kind == "norm":
                norm(*args)
            elif kind == "post":
                post(*args)
            elif kind == "mla_norm":
                mla_norm(*args)
            elif kind == "mla_proj":
                mla_proj(*args)
            elif kind == "mla_att":
                mla_att(*args)
            elif kind == "ssd_dt":
                ssd_dt(*args)
            elif kind == "ssd_cs":
                ssd_cs(*args)
            elif kind == "ssd_tok":
                ssd_tok(*args)
            elif kind == "ssd_g":
                ssd_g(*args)
            elif kind == "ssd_state":
                ssd_state(*args)
            elif kind == "ssd_head":
                ssd_head(*args)
            elif kind == "ssd_out":
                ssd_out(*args)
            elif kind == "att2":
                newest, next_, oldest = args
                if oldest:
                    att2_pv(oldest)
                if next_:
                    att2_turn(next_, (0,))
                if newest:
                    att2(newest)
                if next_ and next_[0] == 0:
                    att2_turn(next_, (1, 2))
            elif kind == "p_split":
                p_split(*args)
            elif kind == "ln_sum":
                ln_sum(*args)
            elif kind == "ln":
                ln(*args)
            elif kind == "out":
                out_step()

    @ctx_block.scalar
    def _(engine):
        act = Waits(engine)
        f = nc.scalar.activation
        Signal.newest[0] = None
        split_at = [0]

        def splits(upto):
            while split_at[0] <= min(upto, N_HALF - 1):
                h = split_at[0]
                u = units[h // 2]
                if h % 2 == 0:
                    engine.wait_ge(raw_in[u.id % RAW_SLOTS], u.raw_due)
                if h >= HALF_SLOTS:
                    act.wait_ge(s_gemm, s_gemm.at(("half", h - HALF_SLOTS)))
                n = half_size(u)
                f(whi[h % HALF_SLOTS][:, 0:n], raw[u.id % RAW_SLOTS][:, (h % 2) * n:(h % 2) * n + n], ACT.Copy)\
                    .then_inc(*s_hi_ready.tick(h))
                split_at[0] += 1

        late = []

        def run_late():
            while late:
                late.pop(0)()
                act.wait_ge(*so_far())

        def bank(u, bi):
            act.wait_ge(s_gemm, s_gemm.at(("blk", u.id, bi)))
            return banks[bank_of[(u.id, bi)]]

        def square_y(l, which, m):
            t = t_of(l)
            if which == "mix":
                act.wait_ge(s_y_copy, s_y_copy.at((l, m // 2, m % 2)))
            else:
                act.wait_ge(s_f_add, s_f_add.at((l, 3, m // 2, m % 2)))
            if m >= 2:
                act.wait_ge(s_acc, s_acc.at(("p", l, which, m - 2)))
            f(SQ[m % 2][:, t[0]:t[1]], YM[:, m, t[0]:t[1]], ACT.Square, scale=2 * D ** -0.5).then_inc(*s_sq.tick(("p", l, which, m)))

        xp_turn = [0]
        sh_turn = [0]

        def unit(u):
            splits(2 * u.id + (2 if u.kind == "proj" else 3))
            act.wait_ge(*so_far())
            run_late()
            act.wait_ge(*so_far())
            kind = u.kind
            if kind == "mod":
                n = mod_no[u.key]
                if n >= 2:
                    act.wait_ge(s_mod_col, s_mod_col.at(mods[n - 2]))
                act.wait_ge(s_gemm, s_gemm.at(("blk", u.id, 1)))
                f(mrow[n % 2][0:4, :], banks[bank_of[(u.id, 0)]][0:4, 0:256], ACT.Copy).then_inc(*s_mod_row.tick(u.key))
            elif kind == "win":
                l, part = u.key
                if part == "val":
                    return
                for bi, (c0, m) in enumerate(u.blocks):
                    b = bank(u, bi)
                    t = u.t[bi]
                    ps = b[0:m, 0:t[1] - t[0]]
                    key = s_u_out.tick
                    if part == "kv" and bi == 0:
                        f(CK, ps, ACT.Copy).then_inc(*key(u.key + (bi,)))
                    elif part == "kv":
                        f(KR[64:96, :], ps, ACT.Copy).then_inc(*key(u.key + (bi,)))
                    elif part in ("q", "gc", "gb"):
                        dst = {"q": QC, "gc": GC, "gb": GB}[part]
                        f(dst[:, bi, t[0]:t[1]], ps, ACT.Copy).then_inc(*key(u.key + (bi,)))
                    elif part in ("z0", "z1"):
                        f(ZS[:, 2 * int(part[1]) + bi, t[0]:t[1]], ps, ACT.Silu).then_inc(*key(u.key + (bi,)))
                    elif part == "bc" and bi == 2:
                        f(dtT[0:16, :], ps, ACT.Copy).then_inc(*key(u.key + (bi,)))
                    else:
                        j = 4 + bi if part == "bc" else 2 * int(part[2]) + bi
                        act.wait_ge(s_pads, s_pads.at(l))
                        if xp_turn[0] >= 2:
                            act.wait_ge(s_conv, s_conv.at(xp_turn[0] - 2))
                        f(XP[xp_turn[0] % 2][:, :, 1:257], ps.rearrange("p (s t) -> p s t", s=2), ACT.Copy)\
                            .then_inc(*key(u.key + (bi,)))

                        def silu(l=l, j=j, n=xp_turn[0]):
                            act.wait_ge(s_conv, s_conv.at(n))
                            f(XC[:, j, :], CV[n % 2], ACT.Silu, bias=vec(l, "ssd_conv_b", j)).then_inc(*s_xc.tick((l, j), ("n", n)))

                        late.append(silu)
                        xp_turn[0] += 1
            elif kind == "wout":
                l, i = u.key
                for m in (2 * i, 2 * i + 1):
                    late.append(lambda l=l, m=m: square_y(l, "mix", m))
            elif kind == "ff1":
                l, g, i = u.key
                t = t_of(l)
                sl = slice(t[0], t[1])
                for bi in (0, 1):
                    j = 2 * i + bi
                    b = bank(u, bi)
                    if j >= 2:
                        act.wait_ge(s_fq, s_fq.at((l, g, j - 2)))
                    elif g > 0:
                        act.wait_ge(s_fq, s_fq.at((l, g - 1, 6 + j)))
                    f(R32[j % 2][:, sl], b[:, 0:t[1] - t[0]], ACT.Relu).then_inc(*s_relu.tick(u.key + (bi,)))
                for bi in (0, 1):
                    j = 2 * i + bi
                    act.wait_ge(s_relu, s_relu.at(u.key + (bi,)))
                    f(FH[:, j, sl], R32[j % 2][:, sl], ACT.Square).then_inc(*s_fh.tick((l, g, j)))
            elif kind == "ff2":
                l, g, i = u.key
                if g == 3:
                    for m in (2 * i, 2 * i + 1):
                        late.append(lambda l=l, m=m: square_y(l, "ffn", m))
            elif kind in ("aq", "ak") or kind == "bkv":
                for bi in ((0, 1) if kind != "bkv" else (0,)):
                    b = bank(u, bi)
                    key = u.key + ((kind, bi) if kind != "bkv" else ("kb", 0))
                    if sh_turn[0] >= 2:
                        act.wait_ge(s_rope2, s_rope2.at(("n", sh_turn[0] - 2)))
                    for q in range(4):
                        o = q ^ 1
                        ins = f(SH[sh_turn[0] % 2][32 * q:32 * q + 32, :], b[32 * o:32 * o + 32, 0:SEQ], ACT.Copy)
                    ins.then_inc(*s_sh2.tick(key))
                    sh_turn[0] += 1
                if kind == "bkv":
                    for tt in (0, 1):
                        b = bank(u, 1)
                        b = banks[bank_of[(u.id, 1 + tt)]]
                        src = b[:, 0:P].rearrange("p (h d) -> p h d", h=2)
                        for dup in (0, 1):
                            ins = f(AV[0][:, 0:2, tt, 64 * dup:64 * dup + 64], src, ACT.Copy)
                        ins.then_inc(*s_vb2.tick(tt))
            elif kind == "av":
                i, hq, g = u.key
                if hq >= 2:
                    act.wait_ge(s_o2, s_o2.at((i, 4 * (hq - 2) + 3)))
                for bi in (0, 1):
                    f(AV[hq % 2][:, g, bi, :], bank(u, bi)[:, 0:256], ACT.Copy).then_inc(*s_v2.tick(u.key + (bi,)))
            elif kind == "az":
                i, hq, g = u.key
                if hq >= 2:
                    act.wait_ge(s_ya, s_ya.at((i, 4 * (hq - 2) + 3)))
                for bi in (0, 1):
                    f(AZ[hq % 2][:, bi, :], bank(u, bi)[:, 0:SEQ], ACT.Silu).then_inc(*s_z2.tick(u.key + (bi,)))
            elif kind == "proj":
                i, part = u.key
                for n in range(4):
                    if n == 2:
                        splits(2 * u.id + 3)
                    m = 4 * part + n
                    f(PJ[:, m, :], bank(u, n)[:, 0:SEQ], ACT.Copy).then_inc(*s_pj.tick((i, m)))
            elif kind == "gate":
                i, j = u.key
                for bi in (0, 1):
                    m = 2 * j + bi
                    if m >= 2:
                        act.wait_ge(s_gmul, s_gmul.at((i, m - 2)))
                    f(SH[m % 2], bank(u, bi)[:, 0:SEQ], ACT.Sigmoid).then_inc(*s_sg.tick(u.key + (bi,)))
                    if i == 0:
                        def part(m=m):
                            act.wait_ge(s_x2_new, s_x2_new.at((0, m)))
                            f(parts2("x2", 1)[0][:, m, :], XT[:, m, SEQ:T], ACT.Copy).then_inc(*s_x2_hi.tick((1, m)))

                        late.append(part)

        def init():
            for i in range(3):
                n = VEC_ROWS if i < 2 else VEC2_ROWS
                act.wait_ge(s_init_t, s_init_t.at(("vec", i)))
                f(VT[i][:, 0:n], banks[bank_of[("vec", i)]][:, 0:n], ACT.Copy).then_inc(*s_vt.tick(i))
            for k in range(KC):
                act.wait_ge(s_init_t, s_init_t.at(("x", k)))
                f(XT[:, k, :], banks[bank_of[("x", k)]], ACT.Copy).then_inc(*s_xt.tick(k))

        def silu_c():
            act.wait_ge(s_vt, s_vt.at(2))
            f(cs32, VT[2][:, 0:16].rearrange("p (c k) -> p c k", c=2), ACT.Silu).then_inc(*s_cs32.tick(0))
            act.wait_ge(s_cs32, s_cs32.at(0))
            f(cs[:, :, 0:2], cs32.rearrange("p c k -> p k c"), ACT.Copy).then_inc(*s_cs_hi.tick(0))

        def half_root(summed, key, src, dst, eps):
            act.wait_ge(summed, summed.at(key))
            f(dst, src, ACT.Abs_reciprocal_sqrt, bias=eps_c[:, eps:eps + 1]).then_inc(*s_rs.tick(key))

        def norm(l, which):
            t = ALL if which == "mix" else t_of(l)
            sl = slice(t[0], t[1])
            for k in range(KC):
                if (l, which) == (0, "mix"):
                    act.wait_ge(s_xt, s_xt.at(k))
                else:
                    act.wait_ge(s_x_new, s_x_new.at((l, "mix", k) if which == "ffn" else (l - 1, "ffn", k)))
                if k >= 2:
                    act.wait_ge(s_norm_sum, s_norm_sum.at(("n", l, which, k - 2)))
                f(SQ[k % 2][:, sl], XT[:, k, sl], ACT.Square, scale=2 * D ** -0.5).then_inc(*s_sq.tick(("n", l, which, k)))
            half_root(s_norm_sum, ("n", l, which), banks[7][:, 0:t[1] - t[0]], RS[:, sl], 0)
            a = 0 if which == "mix" else 3 * KC
            act.wait_ge(s_fused, s_fused.at((l, which)))
            for k in range(KC):
                scaled = s_xn if k % 2 == 0 else s_xn_pool
                act.wait_ge(scaled, scaled.at((l, "n", which, k)))
                for s, ts_ in segs(t):
                    ins = f(HH[:, k, ts_], XN[k % 4][:, ts_], ACT.Identity, scale=fA[:, k, 1 - s:2 - s], bias=modT[l][:, a + k, 1 - s:2 - s])
                ins.then_inc(*s_hh.tick((l, which, k)))

        def post(l, which):
            run_late()
            t = t_of(l)
            half_root(s_norm_sum, ("p", l, which), banks[7][:, 0:t[1] - t[0]], RS[:, t[0]:t[1]], 0)

        def mla_norm(l):
            run_late()
            t = t_of(l)
            sl = slice(t[0], t[1])
            n = t[1] - t[0]
            act.wait_ge(s_gemm, s_gemm.at(("blk", last_win[l], 1)))
            act.wait_ge(s_u_out, s_u_out.at((l, "q", 1)))
            f(RSM[:, 0, :], CK, ACT.Square, scale=2 * KV_LORA ** -0.5).then_inc(*s_mla_sq.tick((l, 0)))
            for j in (0, 1):
                f(SQM[:, j, sl], QC[:, j, sl], ACT.Square, scale=2 * Q_LORA ** -0.5).then_inc(*s_mla_sq.tick((l, 1 + j)))
            half_root(s_mla_sum, ("mla", l, "kv"), banks[3][:, 0:T], RSM[:, 1, :], 0)
            half_root(s_mla_sum, ("mla", l, "q"), banks[4][:, 0:n], RSM[:, 0, sl], 0)

        def mla_proj(l):
            t = t_of(l)
            sl = slice(t[0], t[1])
            for h in range(MLA_HEADS):
                act.wait_ge(s_mla_k, s_mla_k.at((l, h)))
                f(KT[0:NOPE, h, :], banks[3 + h % 2][0:NOPE, 0:T], ACT.Copy).then_inc(*s_kt.tick((l, h)))
            for j in range(4):
                act.wait_ge(s_mla_v, s_mla_v.at((l, j)))
                f(VV[:, j, :], banks[5 + j % 2][:, 0:256], ACT.Copy).then_inc(*s_vv.tick((l, j)))
            act.wait_ge(s_kr_rope, s_kr_rope.at(l))
            for h in range(MLA_HEADS):
                ins = f(KT[NOPE:QK, h, :], KR[64:96, :], ACT.Copy)
            ins.then_inc(*s_mla_kr.tick(l))
            for h in range(MLA_HEADS):
                act.wait_ge(s_mla_q, s_mla_q.at((l, h)))
                f(QT[0:QK, h, sl], banks[3 + h % 2][0:QK, 0:t[1] - t[0]], ACT.Copy).then_inc(*s_qt.tick((l, h)))

        def mla_att(att, i):
            if i < len(att):
                nk = T if att[i][2] else SEQ
                for j in (0, 1):
                    act.wait_ge(s_mla_mx, s_mla_mx.at((att[i], j)))
                    if i >= 1:
                        act.wait_ge(s_mla_t, s_mla_t.at((att[i - 1], j)))
                    c = 8 * (i % 2)
                    f(PR[j][:, 0:nk], banks[3 + j][:, 0:nk], ACT.Exp, bias=small[:, c + 2 + j:c + 3 + j], scale=MLA_SCALE,
                      accum_out=small[:, c + 4 + j:c + 5 + j]).then_inc(*s_mla_e.tick((att[i], j)))
            if i > 0:
                nt = 4 if att[i - 1][2] else 2
                if i >= 3:
                    act.wait_ge(s_mla_o, s_mla_o.at(att[i - 3]))
                for j in (0, 1):
                    act.wait_ge(s_mla_t, s_mla_t.at((att[i - 1], j)))
                    f(PT[(i - 1) % 2][:, 0:nt, j * P:(j + 1) * P], banks[5 + j][:, 0:nt * P].rearrange("p (k q) -> p k q", q=P),
                      ACT.Copy).then_inc(*s_mla_pt.tick((att[i - 1], j)))

        def ssd_dt(l):
            act.wait_ge(s_ab, s_ab.at(l))
            f(EX, AB, ACT.Exp, scale=-1.0).then_inc(*s_ex.tick(l))
            f(AA[:, 0, :], a_log[:, l, :], ACT.Exp).then_inc(*s_aa.tick(l))

        def ssd_cs(l):
            act.wait_ge(s_df, s_df.at(l))
            f(WW, DF, ACT.Exp).then_inc(*s_ww.tick(l))
            for d in (0, 1):
                r = slice(64 * d, 64 * d + 64)
                ins = f(DEC[r], banks[4][r, 32 * d:32 * d + 32].rearrange("p (c h) -> p c h", c=4), ACT.Exp)
            ins.then_inc(*s_dec.tick(l))
            act.wait_ge(s_ssd_a, s_ssd_a.at((l, "cst")))
            f(CST[0:16, :], banks[5][0:16, :], ACT.Copy).then_inc(*s_cst.tick(l))

        def ssd_tok(l):
            act.wait_ge(s_sc, s_sc.at((l, 1)))
            act.wait_ge(s_mla_y, s_mla_y.at(mla_last[l]))
            for j in range(5):
                act.wait_ge(s_ssd_tk, s_ssd_tk.at((l, j)))
                f(XTK[:, :, j * P:(j + 1) * P], banks[3 + j % 2].rearrange("p (c f) -> p c f", c=4), ACT.Copy)\
                    .then_inc(*s_xtk.tick((l, j)))

        def ssd_g(l):
            act.wait_ge(s_xc, s_xc.at((l, 5)))
            for g in (0, 1):
                for d in (0, 1):
                    ins = f(CTd[64 * d:64 * d + 64, g, :], XC[64 * g:64 * g + 64, 5, :], ACT.Copy)
            ins.then_inc(*s_ctd.tick(l))
            for g in (0, 1):
                act.wait_ge(s_ssd_gt, s_ssd_gt.at((l, g)))
                f(GT[:, g, :], banks[5 + 2 * g], ACT.Copy).then_inc(*s_gt.tick((l, g)))

        def ssd_state(l, c):
            act.wait_ge(s_ssd_st, s_ssd_st.at((l, c, 1)))
            f(ST[:, c, :], banks[3 + c % 2], ACT.Copy).then_inc(*s_st.tick((l, c)))

        def ssd_head(l, h):
            cc = range(CHUNKS) if l == 0 else range(2, 4)
            t0 = cc[0] * P
            if h < SSD_HEADS:
                if h >= 2:
                    act.wait_ge(s_ssd_m, s_ssd_m.at((l, h - 2)))
                for d in (0, 1):
                    r = slice(64 * d, 64 * d + 64)
                    act.wait_ge(s_ssd_row, s_ssd_row.at((l, h, d)))
                    f(ec[h % 2][r, t0:T], banks[3 + d][r, 0:T - t0], ACT.Exp).then_inc(*s_ecs.tick((l, h, d)))
                for d in (0, 1):
                    act.wait_ge(s_ed, s_ed.at((l, h, d)))
                    e = EE[d][h % 2][:, t0:T]
                    f(e, e, ACT.Exp).then_inc(*s_ee.tick((l, h, d)))

        def ssd_out(l):
            t = t_of(l)
            sl = slice(t[0], t[1])
            for j in range(4):
                act.wait_ge(s_gz, s_gz.at((l, j)))
                f(SQS[:, j, sl], YM[:, 4 + j, sl], ACT.Square, scale=2 * 256 ** -0.5).then_inc(*s_ssd_sq.tick((l, j)))
            for g in (0, 1):
                half_root(s_ssd_sum, ("ssd", l, g), banks[3 + g][:, 0:t[1] - t[0]], RSS[:, g, sl], 0)

        def y_split(l):
            t = t_of(l)
            sl = slice(t[0], t[1])
            act.wait_ge(s_ssd_yn, s_ssd_yn.at((l, 3)))
            for k in range(KC):
                f(HH[:, k, sl], YM[:, k, sl], ACT.Copy).then_inc(*s_yh.tick((l, k)))

        def att2(ih):
            i, h = ih
            G = 3 if i == 0 else 1
            c = 16 + 16 * (h % 2)
            p_ = AP_[h % 2]
            for j, (a, n) in enumerate(((0, G * P), (G * P, G * SEQ))):
                act.wait_ge(s_mx2, s_mx2.at((ih, 2 + j)))
                f(p_[:, a:a + n], p_[:, a:a + n], ACT.Exp, bias=small[:, c + 2 + j:c + 3 + j], scale=SCALE,
                  accum_out=small[:, c + 4 + j:c + 5 + j]).then_inc(*s_e2.tick((ih, j)))
                if i == 1:
                    f(small[:, c + 8 + j:c + 9 + j], sinks[:, h:h + 1], ACT.Exp, bias=small[:, c + 2 + j:c + 3 + j])\
                        .then_inc(*s_e2.tick((ih, j), (ih, "sink", j)))

        def att2_turn(ih):
            i, h = ih
            G = 3 if i == 0 else 1
            prev = before_head[ih]
            if prev:
                act.wait_ge(s_o2, s_o2.at(prev))
            for n in range((G * 384 + 511) // 512):
                w = min(512, G * 384 - 512 * n)
                act.wait_ge(s_t2, s_t2.at((ih, n)))
                f(APT[:, 512 * n:512 * n + w], banks[6 if n % 2 == 0 else 7][:, 0:w], ACT.Copy).then_inc(*s_pt2.tick((ih, n)))

        def att2_y(ih):
            i, h = ih
            if h % 4 == 3:
                act.wait_ge(s_ya, s_ya.at(ih))
                for b in (0, 1):
                    k = 2 * (h // 4) + b
                    f(parts2("y2", i)[0][:, k, :], YA[(h // 4) % 2][:, b, :], ACT.Copy).then_inc(*s_y2_hi.tick((i, k)))

        engine.wait_ge(consts_in, 16 * CONSTS)
        act.wait_ge(s_ones, s_ones.at(1))
        for st in steps:
            kind, args = st[0], st[1:]
            act.wait_ge(*so_far())
            if kind == "unit":
                unit(args[0])
            elif kind == "init":
                init()
            elif kind == "silu_c":
                silu_c()
            elif kind == "norm":
                norm(*args)
            elif kind == "post":
                post(*args)
            elif kind == "mla_norm":
                mla_norm(*args)
            elif kind == "mla_proj":
                mla_proj(*args)
            elif kind == "mla_att":
                mla_att(*args)
            elif kind == "ssd_dt":
                ssd_dt(*args)
            elif kind == "ssd_cs":
                ssd_cs(*args)
            elif kind == "ssd_tok":
                ssd_tok(*args)
            elif kind == "ssd_g":
                ssd_g(*args)
            elif kind == "ssd_state":
                ssd_state(*args)
            elif kind == "ssd_head":
                ssd_head(*args)
            elif kind == "ssd_out":
                ssd_out(*args)
            elif kind == "y_split":
                y_split(*args)
            elif kind == "split2":
                for k in range(KC):
                    act.wait_ge(s_x_new, s_x_new.at((1, "ffn", k)))
                    f(HA[:, k, :], XT[:, k, SEQ:T], ACT.Copy).then_inc(*s_x2_hi.tick((0, k)))
            elif kind == "att2":
                newest, next_, oldest = args
                if next_:
                    att2_turn(next_)
                if newest:
                    att2(newest)
                if oldest:
                    att2_y(oldest)
            elif kind == "p_split":
                i = args[0]
                act.wait_ge(s_p_t, s_p_t.at(i))
                f(PH, banks[6].rearrange("p (k t) -> p k t", k=2), ACT.Copy).then_inc(*s_p_hi.tick(i))
            elif kind == "ln_sum":
                i = args[0]
                act.wait_ge(s_ln_total, s_ln_total.at((i, "mean")))
                f(SH[0], banks[7][:, 0:SEQ], ACT.Copy, scale=1.0 / D).then_inc(*s_ln_stat.tick((i, "mean")))
                for k in range(KC):
                    act.wait_ge(s_ln_d, s_ln_d.at((i, k)))
                    f(SQ8[:, k, :], V32[:, k, :], ACT.Square, scale=2 * D ** -0.5).then_inc(*s_ln_sq.tick((i, k)))
            elif kind == "ln":
                i = args[0]
                half_root(s_ln_total, ("ln", i), banks[7][:, 0:SEQ], SH[1], 1)
                for k in range(KC):
                    act.wait_ge(s_ln_v, s_ln_v.at((i, k)))
                    f(parts2("g2", i)[0][:, k, :], V32[:, k, :], ACT.Identity, bias=vec2(f"ln_b{i}", k)).then_inc(*s_g2_hi.tick((i, k)))
                for k in range(KC):
                    f(XT[:, k, SEQ:T], V32[:, k, :], ACT.Identity, bias=vec2(f"ln_b{i}", k)).then_inc(*s_ln_x.tick((i, k)))
            elif kind == "out":
                run_late()
                for j in (0, 1):
                    for half in (0, 1):
                        act.wait_ge(s_out_t, s_out_t.at((j, half)))
                        f(YO[j][:, 512 * half:512 * half + 512], banks[3 + half], ACT.Copy).then_inc(*s_out_rows.tick((j, half)))

    @ctx_block.vector
    def _(engine):
        dve = Waits(engine)
        v = nc.vector
        Signal.newest[0] = None
        split_at = [0]

        def splits(upto):
            while split_at[0] <= min(upto, N_HALF - 1):
                h = split_at[0]
                u = units[h // 2]
                dve.wait_ge(s_hi_ready, s_hi_ready.at(h))
                n = half_size(u)
                v.tensor_tensor(wlo[h % HALF_SLOTS][:, 0:n], raw[u.id % RAW_SLOTS][:, (h % 2) * n:(h % 2) * n + n],
                                whi[h % HALF_SLOTS][:, 0:n].bitcast(F32), ALU.subtract).then_inc(*s_lo_ready.tick(h))
                split_at[0] += 1

        late = []

        def run_late():
            while late:
                late.pop(0)()
                dve.wait_ge(*so_far())

        def chain(ins):
            ins.then_inc(*s_dve_chain.tick(s_dve_chain.n))
            dve.wait_ge(*so_far())

        def bank(u, bi):
            dve.wait_ge(s_gemm, s_gemm.at(("blk", u.id, bi)))
            return banks[bank_of[(u.id, bi)]]

        def rest(dst, src, hi, ready):
            v.tensor_tensor(dst, src, hi.bitcast(F32), ALU.subtract).then_inc(*ready)

        def add_square(key, k, sl):
            dve.wait_ge(s_sq, s_sq.at(key + (k,)))
            if k == 0:
                ins = v.tensor_copy(ACC[:, sl], SQ[0][:, sl])
            else:
                dve.wait_ge(s_acc, s_acc.at(key + (k - 1,)))
                ins = v.tensor_tensor(ACC[:, sl], ACC[:, sl], SQ[k % 2][:, sl], ALU.add)
            ins.then_inc(*s_acc.tick(key + (k,)))

        xp_turn = [0]
        sh_turn = [0]

        def unit(u):
            splits(2 * u.id + 3)
            dve.wait_ge(*so_far())
            run_late()
            dve.wait_ge(*so_far())
            kind = u.kind
            if kind == "mod":
                n = mod_no[u.key]
                if n > 0:
                    mod_flush(mods[n - 1])
            elif kind == "win":
                l, part = u.key
                if part == "val":
                    for bi in (0, 1):
                        t = u.t[bi]
                        b = bank(u, bi)
                        dve.wait_ge(s_u_out, s_u_out.at((l, "gc", bi)))
                        dve.wait_ge(s_pads, s_pads.at(l))
                        s0, ns = (0, 2) if l == 0 else (1, 1)
                        v.tensor_tensor(TP[:, bi, s0:2, 1:257], b[:, 0:t[1] - t[0]].rearrange("p (s t) -> p s t", s=ns),
                                        GC[:, bi, t[0]:t[1]].rearrange("p (s t) -> p s t", s=ns), ALU.mult)\
                            .then_inc(*s_val.tick((l, "val", bi)))
                elif part in ("bc", "xs0", "xs1"):
                    for bi in (0, 1):
                        j = 4 + bi if part == "bc" else 2 * int(part[2]) + bi
                        n = xp_turn[0]
                        dve.wait_ge(s_u_out, s_u_out.at(u.key + (bi,)))
                        if n >= 2:
                            dve.wait_ge(s_xc, s_xc.at(("n", n - 2)))
                        conv(l, "ssd_conv_w", j, 6, XP[n % 2], CV[n % 2].rearrange("p (s t) -> p s t", s=2), s_conv, n)
                        xp_turn[0] += 1
            elif kind == "wout":
                l, i = u.key
                t = t_of(l)
                sl = slice(t[0], t[1])
                for bi in (0, 1):
                    m = 2 * i + bi
                    v.tensor_copy(YM[:, m, sl], bank(u, bi)[:, 0:t[1] - t[0]]).then_inc(*s_y_copy.tick(u.key + (bi,)))
                    late.append(lambda m=m: add_square(("p", l, "mix"), m, sl))
            elif kind == "ff1":
                l, g, i = u.key
                t = t_of(l)
                sl = slice(t[0], t[1])
                for bi in (0, 1):
                    j = 2 * i + bi
                    dve.wait_ge(s_relu, s_relu.at(u.key + (bi,)))
                    v.tensor_tensor(FQ[j % 2][:, sl], R32[j % 2][:, sl], R32[j % 2][:, sl], ALU.mult).then_inc(*s_fq.tick((l, g, j)))
                for bi in (0, 1):
                    j = 2 * i + bi
                    dve.wait_ge(s_fh, s_fh.at((l, g, j)))
                    dve.wait_ge(s_fq, s_fq.at((l, g, j)))
                    rest(FL[:, j, sl], FQ[j % 2][:, sl], FH[:, j, sl], s_parts_f.tick((l, g, j)))
            elif kind == "ff2":
                l, g, i = u.key
                t = t_of(l)
                sl = slice(t[0], t[1])
                for bi in (0, 1):
                    m = 2 * i + bi
                    b = bank(u, bi)[:, 0:t[1] - t[0]]
                    if g == 0:
                        ins = v.tensor_copy(YM[:, m, sl], b)
                    else:
                        dve.wait_ge(s_f_add, s_f_add.at((l, g - 1, i, bi)))
                        ins = v.tensor_tensor(YM[:, m, sl], YM[:, m, sl], b, ALU.add)
                    ins.then_inc(*s_f_add.tick(u.key + (bi,)))
                    if g == 3:
                        late.append(lambda m=m: add_square(("p", l, "ffn"), m, sl))
            elif kind in ("aq", "ak", "bkv"):
                for bi in ((0, 1) if kind != "bkv" else (0,)):
                    n = sh_turn[0]
                    b = bank(u, bi)
                    key = u.key + ((kind, bi) if kind != "bkv" else ("kb", 0))
                    i, hq, g = (1, 0, 0) if kind == "bkv" else u.key
                    dve.wait_ge(s_sh2, s_sh2.at(key))
                    v.tensor_tensor(RR[n % 2], b[:, 0:SEQ], rope[:, 0, :], ALU.mult).then_inc(*s_cos2.tick(key))
                    v.tensor_tensor(SH[n % 2], SH[n % 2], rope[:, 1, :], ALU.mult).then_inc(*s_sin2.tick(n))
                    dve.wait_ge(s_cos2, s_cos2.at(key))
                    dve.wait_ge(s_sin2, s_sin2.at(n))
                    if kind != "bkv":
                        if hq >= 2:
                            dve.wait_ge(s_s2, s_s2.at((i, 4 * (hq - 2) + 3)))
                        dst = (AQ if kind == "aq" else AK)[hq % 2]
                        v.tensor_tensor(dst[:, g, bi, :], RR[n % 2], SH[n % 2], ALU.add)\
                            .then_inc(*s_rope2.tick(key, ("n", n)))
                    else:
                        for kv in (0, 1):
                            for dup in (0, 1):
                                r, o = slice(64 * kv, 64 * kv + 64), slice(64 * dup, 64 * dup + 64)
                                ins = v.tensor_tensor(AK[0][o, 0, kv, :], RR[n % 2][r], SH[n % 2][r], ALU.add)
                        ins.then_inc(*s_rope2.tick(key, ("n", n)))
                    sh_turn[0] += 1
            elif kind == "out2":
                i, j = u.key
                for bi in (0, 1):
                    m = 2 * j + bi
                    v.scalar_tensor_tensor(out=V32[:, m, :], in0=XT[:, m, SEQ:T], scalar=ALPHA, in1=bank(u, bi)[:, 0:SEQ],
                                           op0=ALU.mult, op1=ALU.add).then_inc(*s_v32.tick(u.key + (bi,)))

                    def add(i=i, m=m):
                        dve.wait_ge(s_v32, s_v32.at((i, m // 2, m % 2)))
                        if m == 0:
                            ins = v.tensor_copy(RR[0], V32[:, 0, :])
                        else:
                            dve.wait_ge(s_ln_acc, s_ln_acc.at((i, "mean", m - 1)))
                            ins = v.tensor_tensor(RR[0], RR[0], V32[:, m, :], ALU.add)
                        ins.then_inc(*s_ln_acc.tick((i, "mean", m), *([(i, "mean")] if m == KC - 1 else [])))

                    late.append(add)
            elif kind == "gate":
                i, j = u.key
                for bi in (0, 1):
                    m = 2 * j + bi
                    dve.wait_ge(s_sg, s_sg.at(u.key + (bi,)))
                    dve.wait_ge(s_pj, s_pj.at((i, m)))
                    dve.wait_ge(s_ln_x, s_ln_x.at((i, m)))
                    v.tensor_tensor(RR[m % 2], SH[m % 2], PJ[:, m, :], ALU.mult).then_inc(*s_gmul.tick((i, m)))
                    dve.wait_ge(s_gmul, s_gmul.at((i, m)))
                    v.tensor_tensor(XT[:, m, SEQ:T], XT[:, m, SEQ:T], RR[m % 2], ALU.add).then_inc(*s_x2_new.tick((i, m)))
                    if i == 0:
                        def part(m=m):
                            dve.wait_ge(s_x2_hi, s_x2_hi.at((1, m)))
                            dve.wait_ge(s_x2_new, s_x2_new.at((0, m)))
                            hi, lo = parts2("x2", 1)
                            rest(lo[:, m, :], XT[:, m, SEQ:T], hi[:, m, :], s_parts2.tick((1, m)))

                        late.append(part)

        def conv(l, name, j, blocks, src, dst, signal, key, s0=0):
            dve.wait_ge(s_vt, s_vt.at(l))
            w = [vec(l, name, blocks * k + j) for k in range(3)]
            chain(v.tensor_scalar(dst, src[:, s0:2, 0:256], w[0], None, ALU.mult))
            chain(v.scalar_tensor_tensor(out=dst, in0=src[:, s0:2, 1:257], scalar=w[1], in1=dst, op0=ALU.mult, op1=ALU.add))
            ins = v.scalar_tensor_tensor(out=dst, in0=src[:, s0:2, 2:258], scalar=w[2], in1=dst, op0=ALU.mult, op1=ALU.add)
            if signal is None:
                chain(ins)
            else:
                ins.then_inc(*signal.tick(key))

        flushed = set()

        def mod_flush(key):
            if key in flushed:
                return
            flushed.add(key)
            l, i = key
            dve.wait_ge(s_mod_col, s_mod_col.at(key))
            v.tensor_reduce(modT[l][:, 2 * i:2 * i + 2, :], banks[6][:, 0:8].rearrange("p (b h c) -> p b c h", b=2, h=2), AX.X, ALU.add)\
                .then_inc(*s_mod_t.tick(key))

        def mod_fuse(l, part):
            dve.wait_ge(s_vt, s_vt.at(l))
            a, n, last_key = {"mix": (0, 16, (l, 7)), "g1": (16, 8, (l, 11)), "ffn": (24, 16, (l, 19)), "g2": (40, 8, (l, 23))}[part]
            dve.wait_ge(s_mod_t, s_mod_t.at(last_key))
            m = modT[l][:, a:a + n, :]
            chain(v.tensor_tensor(m, m, bc(vec(l, "b_mod", a, n).unsqueeze(2), [P, n, 2]), ALU.add))
            if part in ("mix", "ffn"):
                g = vec(l, "g_pre_mix" if part == "mix" else "g_pre_ffn", 0, KC)
                v.scalar_tensor_tensor(out=fA, in0=modT[l][:, a + KC:a + 2 * KC, :], scalar=1.0, in1=bc(g.unsqueeze(2), [P, KC, 2]),
                                       op0=ALU.add, op1=ALU.mult).then_inc(*s_fused.tick((l, part)))
            else:
                g = vec(l, "g_post_mix" if part == "g1" else "g_post_ffn", 0, KC)
                v.tensor_tensor(fG, m, bc(g.unsqueeze(2), [P, KC, 2]), ALU.mult).then_inc(*s_fused.tick((l, part)))

        def refine(key, src, h, tmp, eps):
            dve.wait_ge(s_rs, s_rs.at(key))
            chain(v.scalar_tensor_tensor(out=tmp, in0=h, scalar=-1.0, in1=h, op0=ALU.mult, op1=ALU.mult))
            chain(v.scalar_tensor_tensor(out=tmp, in0=src, scalar=4 * eps, in1=tmp, op0=ALU.add, op1=ALU.mult))
            v.scalar_tensor_tensor(out=h, in0=tmp, scalar=3.0, in1=h, op0=ALU.add, op1=ALU.mult).then_inc(*s_inv.tick(key))

        def norm(l, which):
            t = ALL if which == "mix" else t_of(l)
            sl = slice(t[0], t[1])
            refine(("n", l, which), banks[7][:, 0:t[1] - t[0]], RS[:, sl], ACC[:, sl], EPS)
            dve.wait_ge(s_fused, s_fused.at((l, which)))
            dve.wait_ge(s_inv, s_inv.at(("n", l, which)))
            a = 0 if which == "mix" else 3 * KC

            def low(k):
                dve.wait_ge(s_hh, s_hh.at((l, which, k)))
                dve.wait_ge(s_h32, s_h32.at((l, which, k)))
                rest(HL[:, k, sl], H32[k % 2][:, sl], HH[:, k, sl], s_parts.tick((l, which, k)))

            for k in range(KC):
                if k >= 4:
                    dve.wait_ge(s_hh, s_hh.at((l, which, k - 4)))
                if k % 2 == 0:
                    v.tensor_tensor(XN[k % 4][:, sl], XT[:, k, sl], RS[:, sl], ALU.mult).then_inc(*s_xn.tick((l, "n", which, k)))
                if k >= 2:
                    low(k - 2)
                    dve.wait_ge(*so_far())
                scaled = s_xn if k % 2 == 0 else s_xn_pool
                dve.wait_ge(scaled, scaled.at((l, "n", which, k)))
                for s, ts_ in segs(t):
                    ins = v.tensor_scalar(H32[k % 2][:, ts_], XN[k % 4][:, ts_], fA[:, k, 1 - s:2 - s], modT[l][:, a + k, 1 - s:2 - s],
                                          ALU.mult, ALU.add)
                ins.then_inc(*s_h32.tick((l, which, k)))
            low(KC - 2)
            low(KC - 1)

        def post(l, which):
            run_late()
            t = t_of(l)
            sl = slice(t[0], t[1])
            refine(("p", l, which), banks[7][:, 0:t[1] - t[0]], RS[:, sl], ACC[:, sl], EPS)
            dve.wait_ge(s_fused, s_fused.at((l, "g1" if which == "mix" else "g2")))
            dve.wait_ge(s_inv, s_inv.at(("p", l, which)))
            for k in range(KC):
                if k % 2 == 0:
                    if k >= 4:
                        dve.wait_ge(s_x_new, s_x_new.at((l, which, k - 4)))
                    v.tensor_tensor(XN[k % 4][:, sl], YM[:, k, sl], RS[:, sl], ALU.mult).then_inc(*s_xn.tick((l, "p", which, k)))
                scaled = s_xn if k % 2 == 0 else s_xn_pool
                dve.wait_ge(scaled, scaled.at((l, "p", which, k)))
                for s, ts_ in segs(t):
                    ins = v.scalar_tensor_tensor(out=XT[:, k, ts_], in0=XN[k % 4][:, ts_], scalar=fG[:, k, 1 - s:2 - s],
                                                 in1=XT[:, k, ts_], op0=ALU.mult, op1=ALU.add)
                ins.then_inc(*s_x_new.tick((l, which, k)))

        def mla_norm(l):
            t = t_of(l)
            sl = slice(t[0], t[1])
            dve.wait_ge(s_u_out, s_u_out.at((l, "kv", 1)))
            dve.wait_ge(s_gemm, s_gemm.at(("blk", last_win[l], 1)))
            rotate(KR[64:96, SEQ:T].unsqueeze(1), ROT[64:96, 0:1, :], 1)
            v.tensor_copy(small[0:1, 63:64], small[0:1, 62:63]).then_inc(*s_kr_rope.tick(l))
            refine(("mla", l, "kv"), banks[3][:, 0:T], RSM[:, 1, :], ROT[:, 0:2, :].rearrange("p a b -> p (a b)"), EPS)
            dve.wait_ge(s_inv, s_inv.at(("mla", l, "kv")))
            v.scalar_tensor_tensor(out=CK, in0=CK, scalar=vec(l, "mla_kv_norm"), in1=RSM[:, 1, :], op0=ALU.mult, op1=ALU.mult)\
                .then_inc(*s_mla_n.tick((l, "kv")))
            refine(("mla", l, "q"), banks[4][:, 0:t[1] - t[0]], RSM[:, 0, sl], ROT[:, 2:4, :].rearrange("p a b -> p (a b)")[:, sl], EPS)
            dve.wait_ge(s_inv, s_inv.at(("mla", l, "q")))
            for j in (0, 1):
                ins = v.scalar_tensor_tensor(out=QC[:, j, sl], in0=QC[:, j, sl], scalar=vec(l, "mla_q_norm", j), in1=RSM[:, 0, sl],
                                             op0=ALU.mult, op1=ALU.mult)
            ins.then_inc(*s_mla_n.tick((l, "q")))

        def rotate(a, tmp, n):
            cos = bc(axial[64:96, 0:1, :], [32, n, SEQ])
            sin = bc(axial[64:96, 1:2, :], [32, n, SEQ])
            swap = [(i + 8) if (i // 8) % 2 == 0 else (i - 8) for i in range(32)]
            for j in range(n):
                chain(v.stream_shuffle(tmp[:, j, :], a[:, j, :], swap))
            chain(v.tensor_tensor(tmp, tmp, sin, ALU.mult))
            chain(v.tensor_tensor(a, a, cos, ALU.mult))
            chain(v.tensor_tensor(a, a, tmp, ALU.add))

        def mla_proj(l):
            dve.wait_ge(s_qt, s_qt.at((l, MLA_HEADS - 1)))
            rotate(QT[64:96, :, SEQ:T], ROT[64:96], MLA_HEADS)
            v.tensor_copy(small[0:1, 63:64], small[0:1, 62:63]).then_inc(*s_mla_qr.tick(l))

        def mla_att(att, i):
            if i < len(att):
                nk = T if att[i][2] else SEQ
                c = 8 * (i % 2)
                for j in (0, 1):
                    dve.wait_ge(s_mla_s, s_mla_s.at((att[i], j)))
                    chain(v.tensor_reduce(small[:, c + j:c + j + 1], banks[3 + j][:, 0:nk], AX.X, ALU.max))
                    v.tensor_scalar(small[:, c + 2 + j:c + 3 + j], small[:, c + j:c + j + 1], -MLA_SCALE, None, ALU.mult)\
                        .then_inc(*s_mla_mx.tick((att[i], j)))
                for j in (0, 1):
                    dve.wait_ge(s_mla_e, s_mla_e.at((att[i], j)))
                    chain(v.reciprocal(small[:, c + 6 + j:c + 7 + j], small[:, c + 4 + j:c + 5 + j]))
                    v.tensor_scalar(PR[j][:, 0:nk], PR[j][:, 0:nk], small[:, c + 6 + j:c + 7 + j], None, ALU.mult)\
                        .then_inc(*s_mla_p.tick((att[i], j)))
            if i > 0:
                l, h, sg = att[i - 1]
                dve.wait_ge(s_mla_o, s_mla_o.at(att[i - 1]))
                r = slice(64 * (h % 2), 64 * (h % 2) + 64)
                v.tensor_copy(YM[r, h // 2, SEQ * sg:SEQ * sg + SEQ], banks[7][r, 0:SEQ]).then_inc(*s_mla_y.tick(att[i - 1]))

        def short_conv(l):
            t = t_of(l)
            s0 = 0 if l == 0 else 1
            for j in (0, 1):
                dve.wait_ge(s_val, s_val.at((l, "val", j)))
                y = YM[:, 2 + j, t[0]:t[1]]
                conv(l, "sc_conv_w", j, 2, TP[:, j], y.rearrange("p (s t) -> p s t", t=SEQ), None, None, s0)
                dve.wait_ge(s_u_out, s_u_out.at((l, "gb", j)))
                v.tensor_tensor(y, y, GB[:, j, t[0]:t[1]], ALU.mult).then_inc(*s_sc.tick((l, j)))

        def ssd_dt(l):
            dve.wait_ge(s_ssd_a, s_ssd_a.at((l, "dt")))
            ps = banks[3][:, 0:64].rearrange("p (c h) -> p c h", c=4)
            v.tensor_tensor(XR, ps, bc(dt_bias[:, l:l + 1, :], [P, 4, 16]), ALU.add).then_inc(*s_xr.tick(l))
            dve.wait_ge(s_xr, s_xr.at(l))
            v.scalar_tensor_tensor(out=AB, in0=XR, scalar=-1.0, in1=XR, op0=ALU.mult, op1=ALU.max).then_inc(*s_ab.tick(l))
            dve.wait_ge(s_ex, s_ex.at(l))
            chain(v.tensor_scalar(DN, EX, 2.0, None, ALU.add))
            chain(v.reciprocal(RD, DN))
            chain(v.tensor_tensor(Z1, EX, RD, ALU.mult))
            chain(v.tensor_tensor(Z2, Z1, Z1, ALU.mult))
            chain(v.tensor_scalar(PL, Z2, 1.0 / (2 * LOG1P_TERMS - 1), None, ALU.mult))
            for n in range(LOG1P_TERMS - 2, 0, -1):
                chain(v.scalar_tensor_tensor(out=PL, in0=PL, scalar=1.0 / (2 * n + 1), in1=Z2, op0=ALU.add, op1=ALU.mult))
            chain(v.scalar_tensor_tensor(out=PL, in0=PL, scalar=1.0, in1=Z1, op0=ALU.add, op1=ALU.mult))
            chain(v.tensor_scalar(PL, PL, 2.0, None, ALU.mult))
            chain(v.scalar_tensor_tensor(out=DT, in0=XR, scalar=0.0, in1=PL, op0=ALU.max, op1=ALU.add))
            dve.wait_ge(s_aa, s_aa.at(l))
            v.scalar_tensor_tensor(out=LA, in0=DT, scalar=-1.0, in1=bc(AA[:, 0:1, :], [P, 4, 16]), op0=ALU.mult, op1=ALU.mult)\
                .then_inc(*s_la.tick(l))

        def by_direction(ap):
            return ap.rearrange("p c (d h) -> p d c h", d=2)

        def ssd_cs(l):
            dve.wait_ge(s_ssd_a, s_ssd_a.at((l, "cs")))
            for d in (0, 1):
                ins = v.tensor_copy(CS[:, :, 8 * d:8 * d + 8], banks[3][:, 32 * d:32 * d + 32].rearrange("p (c h) -> p c h", c=4))
            ins.then_inc(*s_cs_tok.tick(l))
            dve.wait_ge(s_ssd_a, s_ssd_a.at((l, "last")))
            dve.wait_ge(s_cs_tok, s_cs_tok.at(l))
            for d in (0, 1):
                ins = v.tensor_tensor(DF[:, :, 8 * d:8 * d + 8], banks[4][:, 32 * d:32 * d + 32].rearrange("p (c h) -> p c h", c=4),
                                      CS[:, :, 8 * d:8 * d + 8], ALU.subtract)
            ins.then_inc(*s_df.tick(l))
            dve.wait_ge(s_ww, s_ww.at(l))
            v.tensor_tensor(WW, WW, DT, ALU.mult).then_inc(*s_wd.tick(l))

        def ssd_state(l, c):
            for g in (0, 1):
                dve.wait_ge(s_xtk, s_xtk.at((l, 4)))
                dve.wait_ge(s_wd, s_wd.at(l))
                dve.wait_ge(s_mla_y, s_mla_y.at(mla_last[l]))
                if c > 0:
                    dve.wait_ge(s_ssd_st, s_ssd_st.at((l, c - 1, g)))
                b = XTK[:, c, 512 + 64 * g:512 + 64 * g + 64].unsqueeze(1)
                w = WW[:, c, :].rearrange("p (d g h) -> p g h d", d=2, g=2)[:, g]
                for d in (0, 1):
                    o = Bd[g].rearrange("p (h d n) -> p h d n", h=4, d=2)[:, :, d, :]
                    ins = v.tensor_tensor(o, bc(b, [P, 4, 64]), bc(w[:, :, d].unsqueeze(2), [P, 4, 64]), ALU.mult)
                ins.then_inc(*s_bd.tick((l, c, g)))

        def ssd_rec(l):
            dve.wait_ge(s_dec, s_dec.at(l))
            runs = ((slice(0, 64), (0, 1, 2, 3)), (slice(64, 128), (1, 0, 3, 2)))
            for r, order in runs:
                v.memset(Sin[r, order[0], :], 0.0)
            for r, order in runs:
                dve.wait_ge(s_st, s_st.at((l, order[0])))
                ins = v.tensor_copy(Sin[r, order[1], :], ST[r, order[0], :])
            chain(ins)
            for n in (1, 2):
                for r, order in runs:
                    a, b = order[n], order[n + 1]
                    ins = v.tensor_tensor(Sin[r, b, :].rearrange("p (h d) -> p h d", h=8), Sin[r, a, :].rearrange("p (h d) -> p h d", h=8),
                                          bc(DEC[r, a, :].unsqueeze(2), [64, 8, 64]), ALU.mult)
                chain(ins)
                for r, order in runs:
                    a, b = order[n], order[n + 1]
                    dve.wait_ge(s_st, s_st.at((l, a)))
                    ins = v.tensor_tensor(Sin[r, b, :], Sin[r, b, :], ST[r, a, :], ALU.add)
                if n == 1:
                    chain(ins)
                else:
                    ins.then_inc(*s_rec.tick(l))

        def ssd_head(l, h):
            cc = range(CHUNKS) if l == 0 else range(2, 4)
            t0 = cc[0] * P
            if h < SSD_HEADS:
                dve.wait_ge(s_gt, s_gt.at((l, 1)))
                dve.wait_ge(s_ctd, s_ctd.at(l))
                for d in (0, 1):
                    dve.wait_ge(s_ecs, s_ecs.at((l, h, d)))
                    for c in cc:
                        ins = v.scalar_tensor_tensor(out=EE[d][h % 2][:, c * P:(c + 1) * P], in0=banks[3 + d][:, c * P - t0:c * P - t0 + P],
                                                     scalar=CS[:, c, 8 * d + h:8 * d + h + 1], in1=tri_neg[:, d, :],
                                                     op0=ALU.subtract, op1=ALU.add)
                    ins.then_inc(*s_ed.tick((l, h, d)))
                if h >= 2:
                    dve.wait_ge(s_ssd_y, s_ssd_y.at((l, h - 2)))
                m = MM_[h % 2]
                v.tensor_tensor(Ce[h % 2][:, t0:T], CTd[:, h // 4, t0:T], ec[h % 2][:, t0:T], ALU.mult)
                dve.wait_ge(s_ee, s_ee.at((l, h, 0)))
                for c in cc:
                    ins = v.tensor_scalar(m[:, c * P:(c + 1) * P], EE[0][h % 2][:, c * P:(c + 1) * P], DT[:, c, h:h + 1], None, ALU.mult)
                chain(ins)
                dve.wait_ge(s_ee, s_ee.at((l, h, 1)))
                for c in cc:
                    ins = v.scalar_tensor_tensor(out=m[:, c * P:(c + 1) * P], in0=EE[1][h % 2][:, c * P:(c + 1) * P],
                                                 scalar=DT[:, c, 8 + h:9 + h], in1=m[:, c * P:(c + 1) * P], op0=ALU.mult, op1=ALU.add)
                chain(ins)
                v.tensor_tensor(m[:, t0:T], m[:, t0:T], GT[:, h // 4, t0:T], ALU.mult).then_inc(*s_ssd_m.tick((l, h)))
            if h > 0:
                g = h - 1
                dve.wait_ge(s_ssd_y, s_ssd_y.at((l, g)))
                r = slice(64 * (g % 2), 64 * (g % 2) + 64)
                v.scalar_tensor_tensor(out=YM[r, 4 + g // 2, t0:T], in0=XC[r, g // 2, t0:T], scalar=d_skip[r, l, g // 2:g // 2 + 1],
                                       in1=banks[5 if g % 2 else 7][r, 0:T - t0], op0=ALU.mult, op1=ALU.add)\
                    .then_inc(*s_ssd_ys.tick((l, g)))

        def ssd_out(l):
            t = t_of(l)
            sl = slice(t[0], t[1])
            dve.wait_ge(s_ssd_ys, s_ssd_ys.at((l, SSD_HEADS - 1)))
            for j in range(4):
                v.tensor_tensor(YM[:, 4 + j, sl], YM[:, 4 + j, sl], ZS[:, j, sl], ALU.mult).then_inc(*s_gz.tick((l, j)))
            for g in (0, 1):
                refine(("ssd", l, g), banks[3 + g][:, 0:t[1] - t[0]], RSS[:, g, sl], SQS[:, 2 * g, sl], EPS)
            for j in range(4):
                dve.wait_ge(s_inv, s_inv.at(("ssd", l, j // 2)))
                y = YM[:, 4 + j, sl]
                v.scalar_tensor_tensor(out=y, in0=y, scalar=vec(l, "ssd_norm", j), in1=RSS[:, j // 2, sl], op0=ALU.mult, op1=ALU.mult)\
                    .then_inc(*s_ssd_yn.tick((l, j)))

        def y_split(l):
            t = t_of(l)
            sl = slice(t[0], t[1])
            dve.wait_ge(s_ssd_yn, s_ssd_yn.at((l, 3)))
            for k in range(KC):
                dve.wait_ge(s_yh, s_yh.at((l, k)))
                rest(HL[:, k, sl], YM[:, k, sl], HH[:, k, sl], s_parts_y.tick((l, k)))

        def att2(ih):
            i, h = ih
            G = 3 if i == 0 else 1
            c = 16 + 16 * (h % 2)
            p_ = AP_[h % 2]
            mask = mask_a if i == 0 else mask_b
            if ih == (0, 0):
                engine.wait_ge(masks_in, 64)
            dve.wait_ge(s_s2, s_s2.at(ih))
            if before_head[before_head[ih]]:
                before = before_head[before_head[ih]]
                dve.wait_ge(s_t2, s_t2.at((before, 2 if before[0] == 0 else 0)))
            parts = ((0, G * P, banks[3]), (G * P, G * SEQ, wide))
            for j, (a, n, ps) in enumerate(parts):
                v.tensor_tensor_reduce(out=p_[:, a:a + n], in0=ps[:, 0:n], in1=mask[:, a:a + n], scale=1.0, scalar=-3e38,
                                       op0=ALU.add, op1=ALU.max, accum_out=small[:, c + j:c + j + 1])\
                    .then_inc(*s_mx2.tick((ih, j)))
            dve.wait_ge(s_mx2, s_mx2.at((ih, 1)))
            if i == 1:
                chain(v.tensor_scalar(small[:, c:c + 2], small[:, c:c + 2], sinks8[:, h:h + 1], None, ALU.max))
            v.tensor_scalar(small[:, c + 2:c + 4], small[:, c:c + 2], -SCALE, None, ALU.mult)\
                .then_inc(*s_mx2.tick((ih, 2), (ih, 3)))
            dve.wait_ge(s_e2, s_e2.at((ih, 1)))
            if i == 1:
                chain(v.tensor_tensor(small[:, c + 4:c + 6], small[:, c + 4:c + 6], small[:, c + 8:c + 10], ALU.add))
            chain(v.reciprocal(small[:, c + 6:c + 8], small[:, c + 4:c + 6]))
            for j, (a, n, ps) in enumerate(parts):
                v.tensor_scalar(p_[:, a:a + n], p_[:, a:a + n], small[:, c + 6 + j:c + 7 + j], None, ALU.mult)\
                    .then_inc(*s_p2.tick((ih, j)))

        def att2_y(ih):
            i, h = ih
            blk = (h % 4) // 2
            r = slice(64 * (h % 2), 64 * (h % 2) + 64)
            buf = (h // 4) % 2
            dve.wait_ge(s_o2, s_o2.at(ih))
            dve.wait_ge(s_z2, s_z2.at((i, h // 4, 0, blk)))
            if h % 4 == 0 and h >= 8:
                dve.wait_ge(s_y2_hi, s_y2_hi.at((i, 2 * (h // 4 - 2) + 1)))
            v.tensor_tensor(YA[buf][r, blk, :], banks[7][r, 0:SEQ], AZ[buf][r, blk, :], ALU.mult).then_inc(*s_ya.tick(ih))

        def att2_y_low(ih):
            i, h = ih
            if h % 4 == 3:
                buf = (h // 4) % 2
                hi, lo = parts2("y2", i)
                for b in (0, 1):
                    k = 2 * (h // 4) + b
                    dve.wait_ge(s_y2_hi, s_y2_hi.at((i, k)))
                    rest(lo[:, k, :], YA[buf][:, b, :], hi[:, k, :], s_parts_y2.tick((i, k)))

        engine.wait_ge(consts_in, 16 * CONSTS)
        dve.wait_ge(s_ones, s_ones.at(1))
        v.tensor_scalar(sinks8, sinks, 1.0 / SCALE, None, ALU.mult).then_inc(*s_cos_on.tick(0))
        for at_step, st in enumerate(steps):
            kind, args = st[0], st[1:]
            dve.wait_ge(*so_far())
            if kind == "unit":
                unit(args[0])
            elif kind == "silu_c":
                dve.wait_ge(s_cs_hi, s_cs_hi.at(0))
                v.tensor_tensor(cs[:, :, 2:4], cs32.rearrange("p c k -> p k c"), cs[:, :, 0:2].bitcast(F32), ALU.subtract)\
                    .then_inc(*s_cs.tick(0))
            elif kind == "mod_flush":
                for key in mods:
                    if at_step > mod_step[key]:
                        mod_flush(key)
            elif kind == "mod_fuse":
                mod_fuse(*args)
            elif kind == "norm":
                norm(*args)
            elif kind == "post":
                post(*args)
            elif kind == "mla_norm":
                run_late()
                mla_norm(*args)
            elif kind == "mla_proj":
                mla_proj(*args)
            elif kind == "mla_att":
                mla_att(*args)
            elif kind == "short_conv":
                short_conv(*args)
            elif kind == "ssd_dt":
                ssd_dt(*args)
            elif kind == "ssd_cs":
                ssd_cs(*args)
            elif kind == "ssd_state":
                ssd_state(*args)
            elif kind == "ssd_rec":
                ssd_rec(*args)
            elif kind == "ssd_head":
                ssd_head(*args)
            elif kind == "ssd_out":
                ssd_out(*args)
            elif kind == "y_split":
                y_split(*args)
            elif kind == "split2":
                for k in range(KC):
                    dve.wait_ge(s_x2_hi, s_x2_hi.at((0, k)))
                    rest(LA_[:, k, :], XT[:, k, SEQ:T], HA[:, k, :], s_parts2.tick((0, k)))
            elif kind == "att2":
                newest, next_, oldest = args
                if oldest:
                    att2_y(oldest)
                if newest:
                    att2(newest)
                if oldest:
                    att2_y_low(oldest)
            elif kind == "p_split":
                i = args[0]
                dve.wait_ge(s_p_hi, s_p_hi.at(i))
                v.tensor_tensor(PL_, banks[6].rearrange("p (k t) -> p k t", k=2), PH.bitcast(F32), ALU.subtract)\
                    .then_inc(*s_p_lo.tick(i))
            elif kind == "ln_sum":
                i = args[0]
                run_late()
                dve.wait_ge(s_ln_stat, s_ln_stat.at((i, "mean")))
                for k in range(KC):
                    v.tensor_tensor(V32[:, k, :], V32[:, k, :], SH[0], ALU.subtract).then_inc(*s_ln_d.tick((i, k)))
            elif kind == "ln":
                i = args[0]
                refine(("ln", i), banks[7][:, 0:SEQ], SH[1], RR[1], LN_EPS)
                dve.wait_ge(s_inv, s_inv.at(("ln", i)))
                hi, lo = parts2("g2", i)
                for k in range(KC + 1):
                    if k < KC:
                        v.scalar_tensor_tensor(out=V32[:, k, :], in0=V32[:, k, :], scalar=vec2(f"ln_g{i}", k), in1=SH[1],
                                               op0=ALU.mult, op1=ALU.mult).then_inc(*s_ln_v.tick((i, k)))
                    if k > 0:
                        dve.wait_ge(s_ln_v, s_ln_v.at((i, k - 1)))
                        dve.wait_ge(s_g2_hi, s_g2_hi.at((i, k - 1)))
                        v.scalar_tensor_tensor(out=lo[:, k - 1, :], in0=V32[:, k - 1, :], scalar=vec2(f"ln_b{i}", k - 1),
                                               in1=hi[:, k - 1, :].bitcast(F32), op0=ALU.add, op1=ALU.subtract)\
                            .then_inc(*s_parts_g2.tick((i, k - 1)))

    @ctx_block.gpsimd
    def _(engine):
        pool = Waits(engine)
        Signal.newest[0] = None
        nc.gpsimd.memset(ones, 1.0).then_inc(*s_ones.tick(0))
        nc.gpsimd.memset(eps_c[:, 0:1], 4 * EPS)
        nc.gpsimd.memset(eps_c[:, 1:2], 4 * LN_EPS)
        nc.gpsimd.memset(small, 0.0).then_inc(*s_ones.tick(1))
        for st in steps:
            kind, args = st[0], st[1:]
            pool.wait_ge(*so_far())
            if kind == "norm":
                l, which = args
                t = ALL if which == "mix" else t_of(l)
                sl = slice(t[0], t[1])
                pool.wait_ge(s_inv, s_inv.at(("n", l, which)))
                for k in range(1, KC, 2):
                    pool.wait_ge(*so_far())
                    if k >= 4:
                        pool.wait_ge(s_hh, s_hh.at((l, which, k - 4)))
                        pool.wait_ge(s_h32, s_h32.at((l, which, k - 4)))
                    nc.gpsimd.tensor_tensor(XN[k % 4][:, sl], XT[:, k, sl], RS[:, sl], ALU.mult)\
                        .then_inc(*s_xn_pool.tick((l, "n", which, k)))
                if which == "mix":
                    if l > 0:
                        pool.wait_ge(s_x_new, s_x_new.at((l - 1, "ffn", KC - 1)))
                    nc.gpsimd.memset(XP0, 0.0)
                    nc.gpsimd.memset(XP1, 0.0)
                    nc.gpsimd.memset(TP, 0.0).then_inc(*s_pads.tick(l))
            elif kind == "post":
                l, which = args
                t = t_of(l)
                sl = slice(t[0], t[1])
                pool.wait_ge(s_inv, s_inv.at(("p", l, which)))
                for k in range(1, KC, 2):
                    pool.wait_ge(*so_far())
                    if k >= 4:
                        pool.wait_ge(s_x_new, s_x_new.at((l, which, k - 4)))
                    nc.gpsimd.tensor_tensor(XN[k % 4][:, sl], YM[:, k, sl], RS[:, sl], ALU.mult)\
                        .then_inc(*s_xn_pool.tick((l, "p", which, k)))
    block.__exit__(None, None, None)
    return {name: s.mine for name, s in signals.items()}


_INS = ['x', 'c', 'ctx', 'c_ctx', 'w_mod', 'b_mod', 'g_pre_mix', 'w_in', 'mla_q_norm', 'w_uq', 'mla_kv_norm', 'w_ukv',
        'sc_conv_w', 'ssd_conv_w', 'ssd_conv_b', 'ssd_a_log', 'ssd_dt_bias', 'ssd_d', 'ssd_norm', 'w_out',
        'g_post_mix', 'g_pre_ffn', 'w_ff1', 'w_ff2', 'g_post_ffn', 'p_2', 'a_w_in_2', 'a_w_out_2', 'b_w_in_2',
        'b_sinks_2', 'b_w_out_2', 'ln_g_2', 'ln_b_2', 'ple_w_proj_2', 'ple_w_gate_2']


def kernel(**inputs):
    import numpy as _np
    import concourse.bacc as _bacc
    from concourse import mybir as _mybir
    from concourse.bass_utils import run_bass_kernel_spmd as _run

    tables = constants()

    def program(counts):
        nc = _bacc.Bacc("TRN2", target_bir_lowering=False, num_devices=1)
        arrays, A = {}, {}
        for name in _INS:
            a = _np.ascontiguousarray(inputs[name])
            arrays[f"in_{name}_dram"] = a
            A[name] = nc.dram_tensor(f"in_{name}_dram", a.shape, _mybir.dt.from_np(a.dtype), kind="ExternalInput").ap()
        for name, a in tables.items():
            arrays[f"k_{name}_dram"] = a
            A["k_" + name] = nc.dram_tensor(f"k_{name}_dram", a.shape, _mybir.dt.from_np(a.dtype), kind="ExternalInput").ap()
        out = nc.dram_tensor("out_0_dram", (1, SEQ, D), F32, kind="ExternalOutput").ap()
        return nc, arrays, build(nc, A, out, counts)

    _, _, counts = program(None)
    nc, arrays, _ = program(counts)
    r = _run(nc, [arrays], core_ids=[0])
    return r.results[0]["out_0_dram"]
```

```python
import math

import numpy as np

import concourse.bass as bass
from concourse import mybir

F32 = mybir.dt.float32
F32R = mybir.dt.float32r
ALU = mybir.AluOpType
ACT = mybir.ActivationFunctionType
AX = mybir.AxisListType

P = 128
D = 1024
KC = D // P
SEQ = 256
T = 2 * SEQ
CTX = (0, SEQ)
X = (SEQ, T)
ALL = (0, T)
LAYERS = 2
EPS = 1e-6
LN_EPS = 1e-5
ALPHA = (2 * LAYERS) ** 0.25

MLA_HEADS, NOPE, ROPE, VH = 4, 64, 32, 64
QK = NOPE + ROPE
MLA_SCALE = QK ** -0.5
Q_LORA, KV_LORA = 256, 128
SSD_HEADS, STATE = 8, 64
CHUNKS = T // P
D_FF = 4 * D
COL_KV, COL_GB, COL_GC, COL_VAL, COL_Z, COL_XBC, COL_DT = 256, 416, 672, 928, 1184, 1696, 2464
D_IN = 2480
NEG = -1e30
HEAD = 64
HEADS = 16
SCALE = HEAD ** -0.5
RAW_SLOTS, HALF_SLOTS = 3, 4
UNIT_COLS = 272
AHEAD = 4
HALF = 4 * UNIT_COLS

VEC = {}
_at = 0
for _name, _n in (("b_mod", 48), ("g_pre_mix", 8), ("g_post_mix", 8), ("g_pre_ffn", 8), ("g_post_ffn", 8),
                  ("ssd_norm", 4), ("mla_q_norm", 2), ("mla_kv_norm", 1), ("sc_conv_w", 6), ("ssd_conv_w", 18),
                  ("ssd_conv_b", 6)):
    VEC[_name] = (_at, _n)
    _at += _n
VEC_ROWS = _at
VEC2 = {"c": (0, 8), "c_ctx": (8, 8), "ln_g0": (16, 8), "ln_g1": (24, 8), "ln_b0": (32, 8), "ln_b1": (40, 8)}
VEC2_ROWS = 48

LOG1P_TERMS = 9
CONSTS = 6 + 4 * LAYERS + 1


def constants():
    i = np.arange(P)
    out = {"ident": np.eye(P, dtype=np.float32)}
    freq = 1.0 / (np.float32(10000.0) ** (np.arange(0, HEAD, 2, dtype=np.float32) / np.float32(HEAD)))
    ang = (np.arange(SEQ, dtype=np.float32)[None, :] * freq.astype(np.float32)[:, None]).astype(np.float32)
    sign = np.where((i % HEAD) < HEAD // 2, -1.0, 1.0)[:, None]
    out["rope"] = np.stack([np.cos(ang)[i % 32], np.sin(ang)[i % 32] * sign], 1).astype(np.float32)
    half = ROPE // 2
    inv = np.float32(10000.0) ** (-np.arange(0, half, 2, dtype=np.float32) / np.float32(half))
    t = np.arange(SEQ)
    a_r = ((t // 64).astype(np.float32)[None, :] * inv[:, None]).astype(np.float32)
    a_c = ((t % 64).astype(np.float32)[None, :] * inv[:, None]).astype(np.float32)
    ang = np.concatenate([a_r, a_r, a_c, a_c], 0)
    sgn = np.where((np.arange(32) // 8) % 2 == 0, -1.0, 1.0)[:, None]
    axial = np.zeros((P, 2, SEQ), np.float32)
    axial[64:96, 0] = np.cos(ang)
    axial[64:96, 1] = np.sin(ang) * sgn
    out["axial"] = axial
    s, u = i[:, None], i[None, :]
    out["tri"] = np.stack([(s <= u), (s >= u)], 1).astype(np.float32)
    out["tri_neg"] = np.stack([np.where(s <= u, 0, NEG), np.where(s >= u, 0, NEG)], 1).astype(np.float32)
    last = np.zeros((P, 2, P), np.float32)
    last[P - 1, 0] = 1
    last[0, 1] = 1
    out["last"] = last
    sel = np.zeros((48, 16, P), np.float32)
    for h in range(16):
        sel[h, h] = sel[32 + h, h] = 1
    out["sel"] = sel

    def banded(dil, most, q0, nk):
        q, k = (q0 + i)[:, None], np.arange(nk)[None, :]
        d = q - k
        return np.where((d >= 0) & (d % dil == 0) & (d // dil <= most), 0, NEG).astype(np.float32)

    groups = ((1, 128), (4, 128), (16, 128))
    out["mask_a"] = np.concatenate([banded(d, m, 0, P) for d, m in groups] + [banded(d, m, P, SEQ) for d, m in groups], 1)
    out["mask_b"] = np.concatenate([banded(1, 127, 0, P), banded(1, 127, P, SEQ)], 1)
    return out


FILL = {
    "mla": ((2, (0, 24)), (2, (1, 20))),
    "g": ((1, (0, 24)), (1, (1, 20))),
    "state": ((3, (0, 24)), (3, (1, 20))),
    "head": ((1, (0, 24)), (1, (1, 20))),
    "out": ((1, (0, 24)), (2, (1, 20))),
}
FILL_HEADS = ((1, 4, 7), (1, 3, 5, 7))


class Signal:

    def __init__(self, name, sem, counts):
        self.name, self.sem, self.counts, self.n, self.mine = name, sem, counts, 0, {}

    newest = [None]

    def tick(self, *keys):
        self.n += 1
        Signal.newest[0] = self
        for k in keys:
            self.mine[k] = self.n
        return self.sem, 1

    def at(self, key):
        return self.counts[key] if self.counts is not None else 1


class Waits:

    def __init__(self, engine):
        self.engine, self.reached = engine, {}

    def wait_ge(self, signal, value):
        if value > self.reached.get(signal.name, 0):
            self.reached[signal.name] = value
            self.engine.wait_ge(signal.sem, value)


class Unit:

    def __init__(self, kind, loads, n, key, id, blocks, x, t=None):
        self.kind, self.loads, self.n, self.key, self.id = kind, loads, n, key, id
        self.blocks, self.x, self.t = blocks, x, t
        self.first_half_done = False


def build(nc, A, out, counts):
    signals = {}

    def signal(name):
        signals[name] = Signal(name, nc.alloc_semaphore(name), None if counts is None else counts[name])
        return signals[name]

    def so_far():
        s = Signal.newest[0]
        return (s, s.n) if s is not None else (s_gemm, 0)

    s_aa = signal("aa")
    s_ab = signal("ab")
    s_acc = signal("acc")
    s_bd = signal("bd")
    s_ce = signal("ce")
    s_conv = signal("conv")
    s_cos2 = signal("cos2")
    s_sinks8 = signal("sinks8")
    s_sel = signal("sel")
    s_cst_lo = signal("cst_lo")
    s_cs = signal("cs")
    s_cs32 = signal("cs32")
    s_cs_hi = signal("cs_hi")
    s_cs_tok = signal("cs_tok")
    s_cst = signal("cst")
    s_ncs = signal("ncs")
    s_mg = signal("mg")
    s_sin0 = signal("sin0")
    s_rec0 = signal("rec0")
    s_rec_back = signal("rec_back")
    s_ctd = signal("ctd")
    s_dec = signal("dec")
    s_df = signal("df")
    s_dve_chain = signal("dve_chain")
    s_e2 = signal("e2")
    s_ecs = signal("ecs")
    s_ed = signal("ed")
    s_ee = signal("ee")
    s_ex = signal("ex")
    s_f_add = signal("f_add")
    s_fh = signal("fh")
    s_fq = signal("fq")
    s_fused = signal("fused")
    s_g2_hi = signal("g2_hi")
    s_gemm = signal("gemm")
    s_gmul = signal("gmul")
    s_gt = signal("gt")
    s_gz = signal("gz")
    s_h32 = signal("h32")
    s_hh = signal("hh")
    s_hi_ready = signal("hi_ready")
    s_init_t = signal("init_t")
    s_inv = signal("inv")
    s_kr_rope = signal("kr_rope")
    s_kt = signal("kt")
    s_la = signal("la")
    s_ln_acc = signal("ln_acc")
    s_ln_d = signal("ln_d")
    s_ln_sq = signal("ln_sq")
    s_ln_stat = signal("ln_stat")
    s_ln_total = signal("ln_total")
    s_ln_v = signal("ln_v")
    s_ln_x = signal("ln_x")
    s_lo_ready = signal("lo_ready")
    s_mla_e = signal("mla_e")
    s_mla_k = signal("mla_k")
    s_mla_kr = signal("mla_kr")
    s_mla_mx = signal("mla_mx")
    s_mla_n = signal("mla_n")
    s_mla_o = signal("mla_o")
    s_mla_p = signal("mla_p")
    s_mla_pt = signal("mla_pt")
    s_mla_q = signal("mla_q")
    s_mla_qr = signal("mla_qr")
    s_mla_s = signal("mla_s")
    s_mla_sq = signal("mla_sq")
    s_mla_sum = signal("mla_sum")
    s_mla_t = signal("mla_t")
    s_mla_v = signal("mla_v")
    s_mla_y = signal("mla_y")
    s_mod_col = signal("mod_col")
    s_mod_row = signal("mod_row")
    s_mod_t = signal("mod_t")
    s_mx2 = signal("mx2")
    s_norm_sum = signal("norm_sum")
    s_o2 = signal("o2")
    s_ones = signal("ones")
    s_out_rows = signal("out_rows")
    s_out_t = signal("out_t")
    s_p2 = signal("p2")
    s_p_hi = signal("p_hi")
    s_p_lo = signal("p_lo")
    s_p_t = signal("p_t")
    s_pads = signal("pads")
    s_parts = signal("parts")
    s_parts2 = signal("parts2")
    s_parts_f = signal("parts_f")
    s_parts_g2 = signal("parts_g2")
    s_parts_y = signal("parts_y")
    s_parts_y2 = signal("parts_y2")
    s_pj = signal("pj")
    s_pt2 = signal("pt2")
    s_qt = signal("qt")
    s_rec = signal("rec")
    s_relu = signal("relu")
    s_rope2 = signal("rope2")
    s_rs = signal("rs")
    s_s2 = signal("s2")
    s_sc = signal("sc")
    s_sg = signal("sg")
    s_sh2 = signal("sh2")
    s_sin2 = signal("sin2")
    s_sq = signal("sq")
    s_ssd_a = signal("ssd_a")
    s_ssd_gt = signal("ssd_gt")
    s_ssd_m = signal("ssd_m")
    s_ssd_row = signal("ssd_row")
    s_ssd_sq = signal("ssd_sq")
    s_ssd_st = signal("ssd_st")
    s_ssd_sum = signal("ssd_sum")
    s_ssd_tk = signal("ssd_tk")
    s_ssd_y = signal("ssd_y")
    s_ssd_yn = signal("ssd_yn")
    s_ssd_ys = signal("ssd_ys")
    s_st = signal("st")
    s_t2 = signal("t2")
    s_u_out = signal("u_out")
    s_v2 = signal("v2")
    s_v32 = signal("v32")
    s_val = signal("val")
    s_vb2 = signal("vb2")
    s_vt = signal("vt")
    s_vv = signal("vv")
    s_wd = signal("wd")
    s_ww = signal("ww")
    s_x2_hi = signal("x2_hi")
    s_x2_new = signal("x2_new")
    s_x_new = signal("x_new")
    s_xc = signal("xc")
    s_xn = signal("xn")
    s_xn_pool = signal("xn_pool")
    s_xr = signal("xr")
    s_xt = signal("xt")
    s_xtk = signal("xtk")
    s_y2_hi = signal("y2_hi")
    s_y_copy = signal("y_copy")
    s_ya = signal("ya")
    s_yh = signal("yh")
    s_z2 = signal("z2")

    base = (nc.sbuf_base + 63) // 64 * 64
    end = nc.sbuf_usable_end
    where = {"at": base}

    def at(name, shape, offset, dt=F32):
        return nc.alloc_sbuf_tensor_at(name, shape, dt, offset=offset).ap()

    def size(shape):
        return (int(np.prod(shape[1:])) * 4 + 31) // 32 * 32

    def place(name, shape, dt=F32):
        o = where["at"]
        where["at"] = o + size(shape)
        assert where["at"] <= end, (name, where["at"], end)
        return at(name, shape, o, dt)

    def region(start, items):
        made = []
        for name, shape, *dt in items:
            made.append(at(name, shape, start, *dt))
            start += size(shape)
        assert start <= end, (items[-1][0], start, end)
        return made, start

    raw = [place(f"raw{i}", [P, 8 * UNIT_COLS]) for i in range(RAW_SLOTS)]
    whi = [place(f"whi{i}", [P, HALF], F32R) for i in range(HALF_SLOTS)]
    wlo = [place(f"wlo{i}", [P, HALF], F32R) for i in range(HALF_SLOTS)]
    XT = place("XT", [P, KC, T])
    ident = place("ident_sb", [P, P])
    ones = place("ones_sb", [P, P])
    rope = place("rope_sb", [P, 2, SEQ])
    axial = place("axial_sb", [P, 2, SEQ])
    tri = place("tri_sb", [P, 2, P])
    tri_neg = place("tri_neg_sb", [P, 2, P])
    last = place("last_sb", [P, 2, P])
    sel_r = at("sel_r", [P, 16, P], where["at"], F32R)
    sel = place("sel_sb", [P, 16, P])
    VT = [place(f"VT{i}", [P, P]) for i in range(3)]
    w_uq = place("w_uq_sb", [P, 2, MLA_HEADS * QK])
    w_ukv = place("w_ukv_sb", [P, MLA_HEADS * (NOPE + VH)])
    modT = [place(f"modT{i}", [P, 48, 2]) for i in range(LAYERS)]
    fA = place("fuse_scale", [P, KC, 2])
    fG = place("fuse_gate", [P, KC, 2])
    cs32 = place("silu_c", [P, 2, KC])
    cs = place("silu_c_parts", [P, KC, 4], F32R)
    mrow = [place(f"mod_row{i}", [4, 256]) for i in range(3)]
    dt_bias = place("dt_bias_sb", [P, LAYERS, 16])
    a_log = place("a_log_sb", [P, LAYERS, 16])
    d_skip = place("d_skip_sb", [P, LAYERS, 4])
    sinks = place("sinks_sb", [P, HEADS])
    sinks8 = place("sinks8_sb", [P, HEADS])
    eps_c = place("eps_c", [P, 2])
    small = place("small", [P, 64])
    R3 = where["at"]
    (HH, HL), R4 = region(R3, [("HH", [P, KC, T], F32R), ("HL", [P, KC, T], F32R)])
    (YM,), R5 = region(R4, [("YM", [P, KC, T])])
    (xtok,), _ = region(R3, [("xtok", [P, 4, D])])
    (vrow,), _ = region(R5, [("vrow", [P, 3, P])])
    (QT, KT, VV), o = region(R3, [("QT", [P, MLA_HEADS, T]), ("KT", [P, MLA_HEADS, T]), ("VV", [P, 4, 256])])
    (PR0, PR1, PT0), o2 = region(o, [("PR0", [P, T]), ("PR1", [P, T]), ("PT0", [P, 4, SEQ])])
    (PT1,), o3 = region(o2, [("PT1", [P, 4, SEQ])])
    assert o3 <= R4
    (ROT,), _ = region(o, [("ROT", [P, 4, SEQ])])
    (SQM, RSM), _ = region(R4 + size([P, 4, T]), [("SQM", [P, 2, T]), ("RSM", [P, 2, T])])
    (TMP0, TMP1), _ = region(R4, [("TMP0", [P, T]), ("TMP1", [P, T])])
    (PR2, PR3), _ = region(R4 + size([P, 4, T]), [("PR2", [P, T]), ("PR3", [P, T])])
    (GT, CTd, E00, E01, E10, E11), o = region(R3, [("GT", [P, 2, T]), ("CTd", [P, 2, T])] + [(f"E{i}{j}", [P, T]) for i in (0, 1) for j in (0, 1)])
    EE = [[E00, E01], [E10, E11]]
    (M0, M1, Ce0, Ce1, ec0, ec1, Bd0, Bd1), o = region(o, [(n, [P, T]) for n in ("M0", "M1", "Ce0", "Ce1", "ec0", "ec1", "Bd0", "Bd1")])
    assert o <= R4
    (XN0, XN1, H320, H321, XN2, XN3), o = region(R5, [(n, [P, T]) for n in ("XN0", "XN1", "H320", "H321", "XN2", "XN3")])
    (SQ0, SQ1, ACC, RS), _ = region(R5 + 2 * size([P, KC, T]), [(n, [P, T]) for n in ("SQ0", "SQ1", "ACC", "RS")])
    (ZS, XC, dtT), o = region(R5, [("ZS", [P, 4, T]), ("XC", [P, 6, T]), ("dtT", [P, T])])
    TINY = ("XR", "AB", "EX", "DN", "RD", "Z1", "Z2", "PL", "DT", "LA", "CS", "DF", "WW", "AA", "NCS")
    tiny, o = region(o, [(n, [P, 4, 16]) for n in TINY])
    XR, AB, EX, DN, RD, Z1, Z2, PL, DT, LA, CS, DF, WW, AA, NCS = tiny
    (DEC,), U0 = region(o, [("DEC", [P, 4, 8])])
    (QC, CK, KR, GC, GB, CV0, CV1), o = region(U0, [("QC", [P, 2, T]), ("CK", [P, T]), ("KR", [P, T]), ("GC", [P, 2, T]), ("GB", [P, 2, T]), ("CV0", [P, T]), ("CV1", [P, T])])
    (XP0, XP1, TP), o = region(o, [("XP0", [P, 2, 258]), ("XP1", [P, 2, 258]), ("TP", [P, 2, 2, 258])])
    (Sin, ST, XTK), o = region(U0, [("Sin", [P, 4, 512]), ("ST", [P, 4, 512]), ("XTK", [P, 4, 640])])
    SQS, RSS = XC[:, 0:4, :], XC[:, 4:6, :]
    CST = at("CST", [P, T], R5 + 10 * size([P, T]), F32R)
    (FH, FL), _ = region(R5, [("FH", [P, KC, T], F32R), ("FL", [P, KC, T], F32R)])
    (R320, R321, FQ0, FQ1), _ = region(R5 + 2 * size([P, KC, T]), [(n, [P, T]) for n in ("R320", "R321", "FQ0", "FQ1")])
    XP, CV, PR, PT = [XP0, XP1], [CV0, CV1], [[PR0, PR1], [PR2, PR3]], [PT0, PT1]
    MM_, Ce, ec, Bd = [M0, M1], [Ce0, Ce1], [ec0, ec1], [[Bd0, Bd1], [E00, E01], [E10, E11], [M0, M1]]
    XN, H32, SQ, R32, FQ = [XN0, XN1, XN2, XN3], [H320, H321], [SQ0, SQ1], [R320, R321], [FQ0, FQ1]
    (HA, LA_, YH, YL), o = region(R3, [("HA", [P, KC, SEQ], F32R), ("LA2", [P, KC, SEQ], F32R), ("YH", [P, KC, SEQ], F32R), ("YL", [P, KC, SEQ], F32R)])
    (mask_a, mask_b, ptok), o = region(o, [("mask_a_sb", [P, 1152]), ("mask_b_sb", [P, 384]), ("ptok", [P, 2, LAYERS, 256])])
    (SH0, SH1, RR0, RR1, YA0, YA1, A0), o = region(o, [(n, [P, SEQ]) for n in ("SH0", "SH1", "RR0", "RR1")] + [("YA0", [P, 2, SEQ]), ("YA1", [P, 2, SEQ]), ("APT", [P, 1152])])
    APT = A0
    (PH, PL_), _ = region(o, [("PH", [P, 2, SEQ], F32R), ("PLo", [P, 2, SEQ], F32R)])
    (AP0, AP1), o = region(o, [("AP0", [P, 1152]), ("AP1", [P, 1152])])
    (AZ0, AZ1), o = region(o, [("AZ0", [P, 2, SEQ]), ("AZ1", [P, 2, SEQ])])
    S0 = o
    (AQ0, AQ1, AK0, AK1, AV0, AV1), o = region(o, [(n, [P, 3, 2, SEQ]) for n in ("AQ0", "AQ1", "AK0", "AK1", "AV0", "AV1")])
    (V32, PJ, SQ8, YO0, YO1), _ = region(S0, [("V32", [P, KC, SEQ]), ("PJ", [P, KC, SEQ]), ("SQ8", [P, KC, SEQ])] + [(f"YO{i}", [P, D]) for i in (0, 1)])
    YO = [YO0, YO1]
    SH, RR, YA, AP_, AZ, AQ, AK, AV = [SH0, SH1], [RR0, RR1], [YA0, YA1], [AP0, AP1], [AZ0, AZ1], [AQ0, AQ1], [AK0, AK1], [AV0, AV1]

    banks = [nc.alloc_psum_tensor(f"bank{i}", [P, 512], F32).ap() for i in range(4)]
    wide = nc.alloc_psum_tensor("bank45", [P, 1024], F32).ap()
    banks += [wide[:, 0:512], wide[:, 512:1024]]
    banks += [nc.alloc_psum_tensor(f"bank{i}", [P, 512], F32).ap() for i in (6, 7)]
    bank_of = {}
    raw_in = [nc.alloc_semaphore(f"raw_in{i}") for i in range(RAW_SLOTS)]
    consts_in = nc.alloc_semaphore("consts_in")
    x_in = nc.alloc_semaphore("x_in")
    vec_in = nc.alloc_semaphore("vec_in")
    rows_in = nc.alloc_semaphore("rows_in")
    small_w_in = nc.alloc_semaphore("small_w_in")
    masks_in = nc.alloc_semaphore("masks_in")
    stored = nc.alloc_semaphore("stored")

    units, steps = [], []

    def fm(w, rows, col, n, blocks, kind, key, x, t, between=None):
        src = w[rows:rows + D, col:col + n].rearrange("(k p) n -> p k n", p=P)
        u = Unit(kind, [(0, 8 * n, src)], n, key, len(units), blocks, x, t)
        units.append(u)
        unit_steps(u, between)

    def unit_steps(u, between):
        if between:
            u.first_half_done = True
            steps.append(("first_half", u))
            between()
        steps.append(("unit", u))

    def proj_unit(i, part, between=None):
        pw = A["ple_w_proj_2"][i]
        loads = [(512 * h, 512, pw[:, 512 * part + 256 * h:512 * part + 256 * h + 256].rearrange("(k p) n -> p k n", p=P)) for h in (0, 1)]
        u = Unit("proj", loads, 256, (i, part), len(units), None, ("p2", i))
        units.append(u)
        unit_steps(u, between)

    def mod_units(l, a, b):
        for i in range(a, b):
            fm(A["w_mod"][l], 0, 256 * i, 256, [(0, 256)], "mod", (l, i), None, None)

    two = [(0, P), (P, P)]

    def w_in_units(l):
        t1 = ALL if l == 0 else X
        w, x = A["w_in"][l], ("h", l, "mix")
        fm(w, 0, COL_KV, 160, [(0, P), (P, 32)], "win", (l, "kv"), x, [ALL] * 2)
        fm(w, 0, 0, 256, two, "win", (l, "q"), x, [t1] * 2)
        fm(w, 0, COL_XBC + 512, 272, two + [(256, 16)], "win", (l, "bc"), x, [ALL] * 3)
        fm(w, 0, COL_XBC, 256, two, "win", (l, "xs0"), x, [ALL] * 2)
        steps.append(("mla_square", l))
        fm(w, 0, COL_XBC + 256, 256, two, "win", (l, "xs1"), x, [ALL] * 2)
        steps.append(("mla_norm", l))
        fm(w, 0, COL_GC, 256, two, "win", (l, "gc"), x, [t1] * 2)
        fm(w, 0, COL_VAL, 256, two, "win", (l, "val"), x, [t1] * 2)
        steps.append(("ssd_dt", l))
        fm(w, 0, COL_GB, 256, two, "win", (l, "gb"), x, [t1] * 2)
        fm(w, 0, COL_Z, 256, two, "win", (l, "z0"), x, [t1] * 2)
        steps.append(("ssd_cs", l))
        steps.append(("short_conv", l))
        fm(w, 0, COL_Z + 256, 256, two, "win", (l, "z1"), x, [t1] * 2)

    steps.append(("init",))
    steps.append(("silu_c",))
    mod_units(0, 0, 2)
    steps.append(("init_x",))
    mod_units(0, 2, 4)
    steps.append(("norm_sum", 0, "mix"))
    mod_units(0, 4, 8)
    steps.append(("consts",))
    fill = [(0, i) for i in range(8, 24)] + [(1, i) for i in range(0, 24)]

    def filler(n, upto):
        for _ in range(n):
            if fill and fill[0] < upto:
                ll, i = fill.pop(0)
                mod_units(ll, i, i + 1)

    for l in range(LAYERS):
        t1 = ALL if l == 0 else X
        filler(40, (l, 8))
        steps.append(("mod_flush",))
        steps.append(("mod_fuse", l, "mix"))
        if l > 0:
            steps.append(("norm_sum", l, "mix"))
        steps.append(("norm", l, "mix"))
        w_in_units(l)
        steps.append(("mla_proj", l))
        att = [(l, h, sg) for h in range(MLA_HEADS) for sg in ((0, 1) if l == 0 else (1,))]
        for i in range(len(att) + 3):
            steps.append(("mla_att", att, i))
            filler(*FILL["mla"][l])
        steps.append(("ssd_tok", l))
        steps.append(("ssd_g", l))
        filler(*FILL["g"][l])
        for c in range(CHUNKS):
            steps.append(("ssd_state", l, c))
        filler(*FILL["state"][l])
        for h in range(SSD_HEADS + 2):
            if h == 1:
                steps.append(("ssd_rec", l))
            steps.append(("ssd_head", l, h))
            if h in FILL_HEADS[l]:
                filler(*FILL["head"][l])
        steps.append(("ssd_out", l))
        filler(*FILL["out"][l])
        steps.append(("y_split", l))
        for i in range(4):
            fm(A["w_out"][l], 0, 256 * i, 256, two, "wout", (l, i), ("y", l), [t1] * 2)
            filler(40 if i == 0 else 0, (l, 20))
        steps.append(("mod_flush",))
        steps.append(("mod_fuse", l, "g1"))
        steps.append(("post", l, "mix"))
        steps.append(("mod_fuse", l, "ffn"))
        steps.append(("norm_sum", l, "ffn"))
        steps.append(("norm", l, "ffn"))
        for g in range(4):
            for i in range(4):
                fm(A["w_ff1"][l], 0, g * D + 256 * i, 256, two, "ff1", (l, g, i), ("h", l, "ffn"), [t1] * 2)
            for i in range(4):
                fm(A["w_ff2"][l], g * D, 256 * i, 256, two, "ff2", (l, g, i), ("f", l, g), [t1] * 2)
                filler(1, (l + 1, 8))
        steps.append(("mod_flush",))
        steps.append(("mod_fuse", l, "g2"))
        steps.append(("post", l, "ffn"))
    seq2 = [(0, SEQ)] * 2
    steps.append(("split2", 0))
    aw = A["a_w_in_2"][0]
    heads = []

    def att2_step():
        n = len(heads)
        i = n // (HEADS + 2)
        h = n % (HEADS + 2)
        heads.append(n)
        steps.append(("att2", *((i, h - lag) if 0 <= h - lag < HEADS else None for lag in range(3))))

    for i in range(LAYERS):
        x = ("x2", i)
        if i == 0:
            for hq in range(4):
                us = [(3 * g * D + off + 256 * hq, "a" + what, g) for g in range(3) for what, off in (("q", 0), ("k", D))]
                us += [(9 * D + 256 * hq, "az", 0)] + [(3 * g * D + 2 * D + 256 * hq, "av", g) for g in range(3)]
                for n, (col, kind, g) in enumerate(us):
                    fm(aw, 0, col, 256, two, kind, (i, hq, g), x, seq2)
                    if hq > 0 and n < 4 or hq == 3 and n >= 7:
                        att2_step()
            att2_step()
            att2_step()
        else:
            src = A["b_w_in_2"][0]
            fm(src, 0, D, 256, [(0, P), (P, P)], "bkv", (i, 0), x, seq2)
            for n, (kind, hq) in enumerate((("aq", 0), ("az", 0), ("aq", 1), ("az", 1), ("aq", 2), ("az", 2), ("aq", 3), ("az", 3))):
                fm(src, 0, 256 * hq + (D + 256 if kind == "az" else 0), 256, two, kind, (i, hq, 0), x, seq2,
                   att2_step if n >= 1 else None)
                if n >= 1:
                    att2_step()
            att2_step()
            att2_step()
            att2_step()
        for j in range(4):
            fm(A["a_w_out_2" if i == 0 else "b_w_out_2"][0], 0, 256 * j, 256, two, "out2", (i, j), ("y2", i), seq2,
               att2_step if j == 0 else None)
        steps.append(("p_split", i))
        steps.append(("ln_sum", i))
        proj_unit(i, 0)
        proj_unit(i, 1)
        steps.append(("ln", i))
        for j in range(4):
            fm(A["ple_w_gate_2"][i], 0, 256 * j, 256, two, "gate", (i, j), ("g2", i), seq2)
    steps.append(("out",))

    slot_due = [0] * RAW_SLOTS
    for u in units:
        slot_due[u.id % RAW_SLOTS] += 16 * len(u.loads)
        u.raw_due = slot_due[u.id % RAW_SLOTS]
    N_HALF = 2 * len(units)
    mods = [u.key for u in units if u.kind == "mod"]
    mod_no = {key: n for n, key in enumerate(mods)}

    last_win = {u.key[0]: u.id for u in units if u.kind == "win"}
    mla_last = {l: (l, MLA_HEADS - 1, 1) for l in range(LAYERS)}
    all_heads = [st[1] for st in steps if st[0] == "att2" and st[1]]
    before_head = dict(zip(all_heads, [None] + all_heads[:-1]))
    before_head[None] = None
    mod_step = {st[1].key: n for n, st in enumerate(steps) if st[0] == "unit" and st[1].kind == "mod"}

    def half_size(u):
        return 2 * u.n if u.kind == "proj" else 4 * u.n

    def segs(t):
        return [(s, slice(SEQ * s, SEQ * s + SEQ)) for s in (0, 1) if t[0] <= SEQ * s < t[1]]

    def vec(l, name, j=0, n=None):
        a, m = VEC[name]
        return VT[l][:, a + j:a + j + (n or 1)]

    def vec2(name, j=0, n=1):
        a, _ = VEC2[name]
        return VT[2][:, a + j:a + j + n]

    def bc(ap, shape):
        return ap.broadcast_to(shape)

    def t_of(l):
        return ALL if l == 0 else X

    def x_parts(u):
        kind = u.x[0]
        if kind in ("h", "y"):
            return HH, HL
        if kind == "f":
            return FH, FL
        if kind == "p2":
            return PH, PL_
        return parts2(kind, u.x[1])

    def parts2(kind, i):
        return (HA, LA_) if (kind == "y2") == (i == 1) else (YH, YL)

    block = nc.Block()
    ctx_block = block.__enter__()

    @ctx_block.sync
    def _(engine):
        sp = Waits(engine)
        def load(dst, src, s):
            nc.sync.dma_start(dst, src).then_inc(s, 16)

        load(ident, A["k_ident"], vec_in)
        for name, (r, m) in VEC2.items():
            src = {"c": A["c"][0], "c_ctx": A["c_ctx"]}.get(name)
            if src is None:
                src = A[name[:4] + "_2"][int(name[-1])]
            load(vrow[r:r + m, 2, :], src.rearrange("(a p) -> a p", p=P), vec_in)
        for j in range(2):
            load(xtok[:, j, :], A["ctx"][0, j * P:(j + 1) * P, :], x_in)
            load(xtok[:, 2 + j, :], A["x"][0, j * P:(j + 1) * P, :], x_in)

        def constant_tables():
            for name, dst in (("rope", rope), ("axial", axial), ("tri", tri), ("tri_neg", tri_neg), ("last", last)):
                load(dst, A["k_" + name], consts_in)
            load(sel[0:48], A["k_sel"], consts_in)
            for l in range(LAYERS):
                nc.sync.dma_start(dt_bias[:, l, :], A["ssd_dt_bias"][l].rearrange("a b -> (a b)").partition_broadcast(P)).then_inc(consts_in, 16)
                nc.sync.dma_start(a_log[:, l, :], A["ssd_a_log"][l].rearrange("a b -> (a b)").partition_broadcast(P)).then_inc(consts_in, 16)
                for odd in (0, 1):
                    with nc.allow_non_contiguous_dma(reason="eight values per layer"):
                        nc.sync.dma_start(d_skip[64 * odd:64 * odd + 64, l, :],
                                            A["ssd_d"][l].rearrange("(j two) -> two j", two=2)[odd].partition_broadcast(64)).then_inc(consts_in, 16)
            nc.sync.dma_start(sinks, A["b_sinks_2"][0].partition_broadcast(P)).then_inc(consts_in, 16)

        def small_weights(l):
            load(w_uq, A["w_uq"][l].rearrange("(k p) n -> p k n", p=P), small_w_in)
            load(w_ukv, A["w_ukv"][l], small_w_in)

        for u in units:
            if u.id == RAW_SLOTS:
                constant_tables()
                small_weights(0)
            if u.id >= RAW_SLOTS:
                sp.wait_ge(s_lo_ready, s_lo_ready.at(2 * (u.id - RAW_SLOTS) + 1))
            for off, width, src in u.loads:
                dst = raw[u.id % RAW_SLOTS][:, off:off + width].rearrange("p (k n) -> p k n", n=u.n)
                load(dst, src, raw_in[u.id % RAW_SLOTS])
            if u.kind == "win" and u.key == (1, "kv"):
                sp.wait_ge(s_mla_v, s_mla_v.at((0, 3)))
                small_weights(1)
            if u.kind == "av" and u.key == (0, 0, 0):
                sp.wait_ge(s_parts2, s_parts2.at((0, KC - 1)))
                load(mask_a, A["k_mask_a"], masks_in)
                load(mask_b, A["k_mask_b"], masks_in)
                for i in range(LAYERS):
                    load(ptok[:, :, i, :], A["p_2"][i, 0].rearrange("(a p) n -> p a n", p=P), masks_in)
        for j in range(2):
            sp.wait_ge(s_out_rows, s_out_rows.at((j, 1)))
            load(out[0, j * P:(j + 1) * P, :], YO[j], stored)
        engine.wait_ge(stored, 32)

    @ctx_block.tensor
    def _(engine):
        pe = Waits(engine)
        readers = [()] * 8

        def acquire(b, *read_by):
            for signal, key in readers[b]:
                pe.wait_ge(signal, signal.at(key))
            readers[b] = read_by
            return banks[b]

        gemm_turn = [0]

        def next_bank(tag, *read_by):
            gemm_turn[0] += 1
            bank_of[tag] = gemm_turn[0] % 3
            return acquire(gemm_turn[0] % 3, *read_by)

        def block_readers(u, bi):
            if u.kind == "win":
                return ((s_val if u.key[1] == "val" else s_u_out, u.key + (bi,)),)
            if u.kind in ("aq", "ak"):
                return ((s_cos2, u.key + (u.kind, bi)),)
            if u.kind == "bkv":
                return ((s_cos2, u.key + ("kb", 0)),) if bi == 0 else ((s_vb2, bi - 1),)
            signal = {"wout": s_y_copy, "ff1": s_relu, "ff2": s_f_add, "av": s_v2, "az": s_z2, "gate": s_sg, "out2": s_v32}[u.kind]
            return ((signal, u.key + (bi,)),)

        def mm3(o, wh, wl, xh, xl, start, stop):
            nc.tensor.matmul(o, wh, xh, start=start, stop=False)
            nc.tensor.matmul(o, wh, xl, start=False, stop=False)
            return nc.tensor.matmul(o, wl, xh, start=False, stop=stop)

        pending, open_ = [], {}

        def mod_flush(left):
            while len(pending) > left:
                key = pending.pop(0)
                pe.wait_ge(s_mod_row, s_mod_row.at(key))
                b = next_bank(("mod_t", key), (s_mod_t, key))
                for j in range(2):
                    ins = nc.tensor.transpose(b[:, 4 * j:4 * j + 4], mrow[mod_no[key] % 3][0:4, j * P:(j + 1) * P], ident[0:4, 0:4])
                ins.then_inc(*s_mod_col.tick(key))

        def unit(u, halves=(0, 1)):
            if u.kind == "mod":
                b = next_bank((u.id, 0), (s_mod_row, u.key))
                pe.wait_ge(s_cs, s_cs.at(0))
                for half in (0, 1):
                    s = (2 * u.id + half) % HALF_SLOTS
                    pe.wait_ge(s_lo_ready, s_lo_ready.at(2 * u.id + half))
                    for kk in range(4):
                        k = 4 * half + kk
                        for w in (whi[s], wlo[s]):
                            ins = nc.tensor.matmul(b[0:4, 0:256], cs[:, k, :], w[:, kk * 256:kk * 256 + 256],
                                            start=(k == 0 and w is whi[s]), stop=(k == KC - 1 and w is wlo[s]))
                    ins.then_inc(*s_gemm.tick(("half", 2 * u.id + half), ("blk", u.id, half)))
                pending.append(u.key)
                mod_flush(2)
                return
            if u.kind == "proj":
                xh, xl = x_parts(u)
                for half in halves:
                    s = (2 * u.id + half) % HALF_SLOTS
                    pe.wait_ge(s_lo_ready, s_lo_ready.at(2 * u.id + half))
                    for j in range(2):
                        m = 4 * u.key[1] + 2 * half + j
                        b = next_bank((u.id, 2 * half + j), (s_pj, (u.key[0], m)))
                        for k in range(2):
                            pe.wait_ge(s_p_lo, s_p_lo.at(u.key[0]))
                            w = slice(k * 256 + j * P, k * 256 + j * P + P)
                            ins = mm3(b[:, 0:SEQ], whi[s][:, w], wlo[s][:, w], xh[:, k, :], xl[:, k, :], k == 0, k == 1)
                        keys = [("blk", u.id, 2 * half + j)] + ([("half", 2 * u.id + half)] if j == 1 else [])
                        ins.then_inc(*s_gemm.tick(*keys))
                return
            xh, xl = x_parts(u)
            ready = {"h": s_parts, "y": s_parts_y, "f": s_parts_f, "x2": s_parts2, "y2": s_parts_y2, "g2": s_parts_g2}[u.x[0]]
            for half in halves:
                s = (2 * u.id + half) % HALF_SLOTS
                pe.wait_ge(s_lo_ready, s_lo_ready.at(2 * u.id + half))
                for bi, (c0, m) in enumerate(u.blocks):
                    t = u.t[bi]
                    token_major = u.kind == "av" or (u.kind == "bkv" and bi == 1)
                    if half == 0:
                        if token_major and u.kind == "bkv":
                            open_[bi] = tuple(next_bank((u.id, 1 + tt), *block_readers(u, 1 + tt)) for tt in (0, 1))
                        else:
                            open_[bi] = next_bank((u.id, bi), *block_readers(u, bi))
                    b = open_[bi]
                    for kk in range(4):
                        k = 4 * half + kk
                        pe.wait_ge(ready, ready.at(u.x[1:] + (k,)))
                        first, final = k == 0, k == KC - 1
                        if u.kind == "av":
                            ts_ = slice(bi * P, bi * P + P)
                            w = slice(kk * u.n, kk * u.n + 256)
                            o = b[:, 0:256]
                            nc.tensor.matmul(o, xh[:, k, ts_], whi[s][:, w], start=first, stop=False)
                            nc.tensor.matmul(o, xh[:, k, ts_], wlo[s][:, w], start=False, stop=False)
                            ins = nc.tensor.matmul(o, xl[:, k, ts_], whi[s][:, w], start=False, stop=final)
                        elif token_major:
                            w = slice(kk * u.n + c0, kk * u.n + c0 + m)
                            for tt in (0, 1):
                                ts_ = slice(tt * P, tt * P + P)
                                o = b[tt][:, 0:P]
                                nc.tensor.matmul(o, xh[:, k, ts_], whi[s][:, w], start=first, stop=False)
                                nc.tensor.matmul(o, xh[:, k, ts_], wlo[s][:, w], start=False, stop=False)
                                ins = nc.tensor.matmul(o, xl[:, k, ts_], whi[s][:, w], start=False, stop=final)
                        else:
                            w = slice(kk * u.n + c0, kk * u.n + c0 + m)
                            ins = mm3(b[0:m, 0:t[1] - t[0]], whi[s][:, w], wlo[s][:, w],
                                      xh[:, k, t[0]:t[1]], xl[:, k, t[0]:t[1]], first, final)
                    keys = []
                    if bi == len(u.blocks) - 1:
                        keys.append(("half", 2 * u.id + half))
                    if half == 1:
                        keys.append(("blk", u.id, bi))
                    if keys:
                        ins.then_inc(*s_gemm.tick(*keys))

        def init():
            engine.wait_ge(vec_in, 16 * (1 + len(VEC2)))
            rows(2)

        def rows(i):
            n = VEC_ROWS if i < 2 else VEC2_ROWS
            b = next_bank(("vec", i), (s_vt, i))
            nc.tensor.transpose(b[:, 0:n], vrow[0:n, i, :], ident[0:n, 0:n]).then_inc(*s_init_t.tick(("vec", i)))

        def init_x():
            engine.wait_ge(x_in, 64)
            for k in range(KC):
                b = next_bank(("x", k), (s_xt, k))
                for j in range(4):
                    ins = nc.tensor.transpose(b[:, j * P:(j + 1) * P], xtok[:, j, k * P:(k + 1) * P], ident)
                ins.then_inc(*s_init_t.tick(("x", k)))

        def total(summed, key, src, n, ready, ready_key, read_by):
            b = acquire(7, read_by)
            pe.wait_ge(ready, ready.at(ready_key))
            nc.tensor.matmul(b[:, 0:n], ones, src, start=True, stop=True).then_inc(*summed.tick(key))

        def mla_norm(l):
            t = t_of(l)
            n = t[1] - t[0]
            b = acquire(3, (s_inv, ("mla", l, "kv")))
            pe.wait_ge(s_mla_sq, s_mla_sq.at((l, 2)))
            nc.tensor.matmul(b[:, 0:T], ones, RSM[:, 0, :], start=True, stop=True).then_inc(*s_mla_sum.tick(("mla", l, "kv")))
            b = acquire(4, (s_inv, ("mla", l, "q")))
            for j in (0, 1):
                ins = nc.tensor.matmul(b[:, 0:n], ones, SQM[:, j, t[0]:t[1]], start=j == 0, stop=j == 1)
            ins.then_inc(*s_mla_sum.tick(("mla", l, "q")))

        def mla_proj(l):
            t = t_of(l)
            n = t[1] - t[0]
            engine.wait_ge(small_w_in, 32 * (l + 1))
            pe.wait_ge(s_mla_n, s_mla_n.at((l, "q")))
            for h in range(MLA_HEADS):
                b = acquire(3 + h, (s_qt, (l, h)))
                for k in range(2):
                    ins = nc.tensor.matmul(b[0:QK, 0:n], w_uq[:, k, h * QK:(h + 1) * QK], QC[:, k, t[0]:t[1]], start=k == 0, stop=k == 1)
                ins.then_inc(*s_mla_q.tick((l, h)))
            pe.wait_ge(s_mla_n, s_mla_n.at((l, "kv")))
            for h in range(MLA_HEADS):
                b = acquire(3 + h, (s_kt, (l, h)))
                nc.tensor.matmul(b[0:NOPE, 0:T], w_ukv[:, h * P:h * P + NOPE], CK, start=True, stop=True)\
                    .then_inc(*s_mla_k.tick((l, h)))
            for j in range(4):
                b = acquire((7, 3, 4, 5)[j], (s_vv, (l, j)))
                nc.tensor.matmul(b[:, 0:256].rearrange("p (h d) -> p h d", h=4), CK[:, j * P:(j + 1) * P],
                          w_ukv.rearrange("p (h d) -> p h d", h=4)[:, :, NOPE:P], start=True, stop=True)\
                    .then_inc(*s_mla_v.tick((l, j)))

        def mla_att(att, i):
            if 1 < i < len(att) + 2:
                nt = 4 if att[i - 2][2] else 2
                for j in range(2):
                    pe.wait_ge(s_mla_p, s_mla_p.at((att[i - 2], j)))
                    b = acquire(5 + j, (s_mla_pt, (att[i - 2], j)))
                    for kt in range(nt):
                        ins = nc.tensor.transpose(b[:, kt * P:kt * P + P], PR[i % 2][j][:, kt * P:kt * P + P], ident)
                    ins.then_inc(*s_mla_t.tick((att[i - 2], j)))
            if i < len(att):
                l, h, sg = att[i]
                nk = T if sg else SEQ
                pe.wait_ge(s_mla_qr, s_mla_qr.at(l))
                pe.wait_ge(s_mla_kr, s_mla_kr.at(l))
                pe.wait_ge(s_vv, s_vv.at((l, 3)))
                for j in range(2):
                    b = acquire(3 + j, (s_mla_e, (att[i], j)))
                    q0 = sg * SEQ + j * P
                    nc.tensor.matmul(b[:, 0:nk], QT[0:QK, h, q0:q0 + P], KT[0:QK, h, 0:nk], start=True, stop=True)\
                        .then_inc(*s_mla_s.tick((att[i], j)))
            if i > 2:
                l, h, sg = att[i - 3]
                nt = 4 if sg else 2
                b = acquire(7, (s_mla_y, att[i - 3]))
                for kt in range(nt):
                    pe.wait_ge(s_mla_pt, s_mla_pt.at((att[i - 3], 1)))
                    ins = nc.tensor.matmul(b[:, 0:SEQ], VV[:, kt, (h // 2) * P:(h // 2) * P + P], PT[(i - 3) % 2][:, kt, :],
                                    start=kt == 0, stop=kt == nt - 1)
                ins.then_inc(*s_mla_o.tick(att[i - 3]))

        def ssd_dt(l):
            pe.wait_ge(s_u_out, s_u_out.at((l, "bc", 2)))
            b = acquire(5, (s_xr, l))
            for c in range(CHUNKS):
                ins = nc.tensor.transpose(b[:, c * 16:c * 16 + 16], dtT[0:16, c * P:(c + 1) * P], ident[0:16, 0:16])
            ins.then_inc(*s_ssd_a.tick((l, "dt")))

        def ssd_cs(l):
            pe.wait_ge(s_la, s_la.at(l))
            b = acquire(5, (s_cs_tok, l))
            for d in (0, 1):
                ins = nc.tensor.matmul(b[:, 32 * d:32 * d + 32].rearrange("p (c h) -> p c h", c=4), tri[:, d, :],
                                LA[:, :, 8 * d:8 * d + 8], start=True, stop=True)
            ins.then_inc(*s_ssd_a.tick((l, "cs")))
            pe.wait_ge(s_cs_tok, s_cs_tok.at(l))
            b = acquire(6, (s_df, l), (s_dec, l))
            for d in (0, 1):
                ins = nc.tensor.matmul(b[:, 32 * d:32 * d + 32].rearrange("p (c h) -> p c h", c=4), last[:, d, :],
                                CS[:, :, 8 * d:8 * d + 8], start=True, stop=True)
            ins.then_inc(*s_ssd_a.tick((l, "last")))
            b = acquire(7, (s_cst_lo, l))
            for c in range(CHUNKS):
                ins = nc.tensor.transpose(b[0:16, c * P:(c + 1) * P], CS[:, c, :], ident)
            ins.then_inc(*s_ssd_a.tick((l, "cst")))

        def ssd_tok(l):
            for j in (4, 0, 1, 2, 3):
                pe.wait_ge(s_xc, s_xc.at((l, j)))
                b = acquire(3 + j % 2, (s_xtk, (l, j)))
                for c in range(CHUNKS):
                    ins = nc.tensor.transpose(b[:, c * P:(c + 1) * P], XC[:, j, c * P:(c + 1) * P], ident)
                ins.then_inc(*s_ssd_tk.tick((l, j)))

        def ssd_g(l):
            pe.wait_ge(s_xc, s_xc.at((l, 5)))
            for g in (0, 1):
                b = acquire(5 + 2 * g, (s_gt, (l, g)))
                r = slice(64 * g, 64 * g + 64)
                for c in range(CHUNKS):
                    ins = nc.tensor.matmul(b[:, c * P:(c + 1) * P], XC[r, 4, c * P:(c + 1) * P], XC[r, 5, c * P:(c + 1) * P],
                                    start=True, stop=True)
                ins.then_inc(*s_ssd_gt.tick((l, g)))

        def ssd_state(l, c):
            b = acquire(3 + c % 2, (s_st, (l, c)))
            pe.wait_ge(s_xtk, s_xtk.at((l, 3)))
            for g in (0, 1):
                pe.wait_ge(s_bd, s_bd.at((l, c, g)))
                for h4 in range(4):
                    h = 4 * g + h4
                    ins = nc.tensor.matmul(b[:, 64 * h:64 * h + 64], Bd[c][g][:, P * h4:P * h4 + P], XTK[:, c, 64 * h:64 * h + 64],
                                    start=True, stop=True)
                ins.then_inc(*s_ssd_st.tick((l, c, g)))

        def ssd_head(l, h):
            cc = range(CHUNKS) if l == 0 else range(2, 4)
            t0 = cc[0] * P
            n = len(cc) * P
            if h < SSD_HEADS:
                for d in (0, 1):
                    pe.wait_ge(s_sel, s_sel.at(0))
                    pe.wait_ge(s_cst_lo, s_cst_lo.at(l))
                    b = acquire(3 + d, (s_ed, (l, h, d)))
                    nc.tensor.matmul(b[:, 0:n], sel_r[0:48, 8 * d + h, :], CST[0:48, t0:T], start=True, stop=True)\
                        .then_inc(*s_ssd_row.tick((l, h, d)))
            if h > 1:
                g = h - 2
                pe.wait_ge(s_mg, s_mg.at((l, g)))
                pe.wait_ge(s_ce, s_ce.at((l, g)))
                pe.wait_ge(s_rec, s_rec.at(l))
                pe.wait_ge(s_rec_back, s_rec_back.at(l))
                b = acquire(5 if g % 2 else 7, (s_ssd_ys, (l, g)))
                for c in cc:
                    o = b[:, c * P - t0:c * P - t0 + P]
                    nc.tensor.matmul(o, XTK[:, c, P * (g // 2):P * (g // 2) + P], MM_[g % 2][:, c * P:(c + 1) * P], start=True, stop=False)
                    ins = nc.tensor.matmul(o, Sin[:, c, P * (g // 2):P * (g // 2) + P], Ce[g % 2][:, c * P:(c + 1) * P], start=False, stop=True)
                ins.then_inc(*s_ssd_y.tick((l, g)))

        def ssd_out(l):
            t = t_of(l)
            n = t[1] - t[0]
            for g in (0, 1):
                b = acquire(3 + g, (s_inv, ("ssd", l, g)))
                for j in (0, 1):
                    pe.wait_ge(s_ssd_sq, s_ssd_sq.at((l, 2 * g + j)))
                    ins = nc.tensor.matmul(b[:, 0:n], ones, SQS[:, 2 * g + j, t[0]:t[1]], start=j == 0, stop=j == 1)
                ins.then_inc(*s_ssd_sum.tick(("ssd", l, g)))

        def norm_sum(l, which):
            t = ALL if which == "mix" else t_of(l)
            b = acquire(7, (s_inv, ("n", l, which)))
            for k in range(KC):
                pe.wait_ge(s_sq, s_sq.at(("n", l, which, k)))
                nc.tensor.matmul(b[:, 0:t[1] - t[0]], ones, SQ[k % 2][:, t[0]:t[1]], start=k == 0, stop=k == KC - 1)\
                    .then_inc(*s_norm_sum.tick(("n", l, which, k), *([("n", l, which)] if k == KC - 1 else [])))

        def post(l, which):
            t = t_of(l)
            total(s_norm_sum, ("p", l, which), ACC[:, t[0]:t[1]], t[1] - t[0], s_acc, ("p", l, which, KC - 1), (s_inv, ("p", l, which)))

        def att2(ih):
            i, h = ih
            G = 3 if i == 0 else 1
            buf, hl = (h // 4) % 2, h % 4
            blk, r = hl // 2, slice(64 * (hl % 2), 64 * (hl % 2) + 64)
            q = AQ[buf]
            b0 = acquire(3, (s_mx2, (ih, 0)))
            acquire(4, (s_mx2, (ih, 1)))
            acquire(5, (s_mx2, (ih, 1)))
            for g in range(G):
                pe.wait_ge(s_rope2, s_rope2.at((i, h // 4, g, "aq", blk)))
                if i == 0:
                    pe.wait_ge(s_rope2, s_rope2.at((i, h // 4, g, "ak", blk)))
                    k_ = AK[buf][r, g, blk, :]
                else:
                    pe.wait_ge(s_rope2, s_rope2.at((1, 0, "kb", 0)))
                    k_ = AK[0][r, 0, h // 8, :]
                nc.tensor.matmul(b0[:, g * P:(g + 1) * P], q[r, g, blk, 0:P], k_[:, 0:P], start=True, stop=True)
                ins = nc.tensor.matmul(wide[:, g * SEQ:(g + 1) * SEQ], q[r, g, blk, P:SEQ], k_, start=True, stop=True)
            ins.then_inc(*s_s2.tick(ih))

        def att2_turn(ih, batches):
            i, h = ih
            G = 3 if i == 0 else 1
            p_ = AP_[h % 2]
            pe.wait_ge(s_p2, s_p2.at((ih, 1)))
            dst = []
            for g in range(G):
                dst += [(g * SEQ, g * P), (g * SEQ + P, G * P + g * SEQ)]
            for g in range(G):
                dst += [(G * SEQ + g * P, G * P + g * SEQ + P)]
            for n in batches:
                b = acquire(6 if n % 2 == 0 else 7, (s_pt2, (ih, n)))
                for o, src in dst:
                    if o // 512 == n:
                        ins = nc.tensor.transpose(b[:, o % 512:o % 512 + P], p_[:, src:src + P], ident)
                ins.then_inc(*s_t2.tick((ih, n)))

        def att2_pv(ih):
            i, h = ih
            G = 3 if i == 0 else 1
            buf, hl = (h // 4) % 2, h % 4
            blk = hl // 2
            pe.wait_ge(s_pt2, s_pt2.at((ih, (G * 384 - 1) // 512)))
            b = acquire(7, (s_ya, ih))
            if i == 0:
                for g in range(G):
                    pe.wait_ge(s_v2, s_v2.at((i, h // 4, g, 0)))
                    pe.wait_ge(s_v2, s_v2.at((i, h // 4, g, 1)))
            else:
                pe.wait_ge(s_vb2, s_vb2.at(1))

            def v(g, kt):
                return AV[buf][:, g, kt, blk * P:blk * P + P] if i == 0 else AV[0][:, h // 8, kt, 0:P]

            for g in range(G):
                nc.tensor.matmul(b[:, 0:SEQ], v(g, 0), APT[:, g * SEQ:(g + 1) * SEQ], start=g == 0, stop=False)
            for g in range(G):
                ins = nc.tensor.matmul(b[:, P:SEQ], v(g, 1), APT[:, G * SEQ + g * P:G * SEQ + (g + 1) * P], start=False, stop=g == G - 1)
            ins.then_inc(*s_o2.tick(ih))

        def ln_sum(i):
            total(s_ln_total, (i, "mean"), RR[0], SEQ, s_ln_acc, (i, "mean"), (s_ln_stat, (i, "mean")))

        def ln(i):
            b = acquire(7, (s_inv, ("ln", i)))
            for k in range(KC):
                pe.wait_ge(s_ln_sq, s_ln_sq.at((i, k)))
                ins = nc.tensor.matmul(b[:, 0:SEQ], ones, SQ8[:, k, :], start=k == 0, stop=k == KC - 1)
            ins.then_inc(*s_ln_total.tick(("ln", i)))

        def p_split(i):
            engine.wait_ge(masks_in, 64)
            b = acquire(6, (s_p_lo, i))
            for k in range(2):
                for j in range(2):
                    ins = nc.tensor.transpose(b[:, k * SEQ + j * P:k * SEQ + (j + 1) * P], ptok[:, j, i, k * P:(k + 1) * P], ident)
            ins.then_inc(*s_p_t.tick(i))

        def out_step():
            for j in range(2):
                for k in range(KC):
                    if k % 4 == 0:
                        b = acquire(3 + k // 4, (s_out_rows, (j, k // 4)))
                    pe.wait_ge(s_x2_new, s_x2_new.at((1, k)))
                    ins = nc.tensor.transpose(b[:, (k % 4) * P:(k % 4) * P + P], XT[:, k, SEQ + j * P:SEQ + (j + 1) * P], ident)
                    if k % 4 == 3:
                        ins.then_inc(*s_out_t.tick((j, k // 4)))

        for st in steps:
            kind, args = st[0], st[1:]
            if kind == "unit":
                unit(args[0], (1,) if args[0].first_half_done else (0, 1))
            elif kind == "first_half":
                unit(args[0], (0,))
            elif kind == "init":
                init()
            elif kind == "init_x":
                init_x()
            elif kind == "mod_flush":
                mod_flush(0)
            elif kind == "norm_sum":
                norm_sum(*args)
            elif kind == "consts":
                engine.wait_ge(consts_in, 16 * CONSTS)
                engine.wait_ge(rows_in, 16 * LAYERS * len(VEC))
                rows(0)
                rows(1)
            elif kind == "post":
                post(*args)
            elif kind == "mla_norm":
                mla_norm(*args)
            elif kind == "mla_proj":
                mla_proj(*args)
            elif kind == "mla_att":
                mla_att(*args)
            elif kind == "ssd_dt":
                ssd_dt(*args)
            elif kind == "ssd_cs":
                ssd_cs(*args)
            elif kind == "ssd_tok":
                ssd_tok(*args)
            elif kind == "ssd_g":
                ssd_g(*args)
            elif kind == "ssd_state":
                ssd_state(*args)
            elif kind == "ssd_head":
                ssd_head(*args)
            elif kind == "ssd_out":
                ssd_out(*args)
            elif kind == "att2":
                newest, next_, oldest = args
                if oldest:
                    att2_pv(oldest)
                if next_:
                    att2_turn(next_, (0,))
                if newest:
                    att2(newest)
                if next_ and next_[0] == 0:
                    att2_turn(next_, (1, 2))
            elif kind == "p_split":
                p_split(*args)
            elif kind == "ln_sum":
                ln_sum(*args)
            elif kind == "ln":
                ln(*args)
            elif kind == "out":
                out_step()

    @ctx_block.scalar
    def _(engine):
        act = Waits(engine)
        f = nc.scalar.activation
        Signal.newest[0] = None
        split_at = [0]

        def splits(upto):
            while split_at[0] <= min(upto, N_HALF - 1):
                h = split_at[0]
                u = units[h // 2]
                if h % 2 == 0:
                    engine.wait_ge(raw_in[u.id % RAW_SLOTS], u.raw_due)
                if h >= HALF_SLOTS:
                    act.wait_ge(s_gemm, s_gemm.at(("half", h - HALF_SLOTS)))
                n = half_size(u)
                f(whi[h % HALF_SLOTS][:, 0:n], raw[u.id % RAW_SLOTS][:, (h % 2) * n:(h % 2) * n + n], ACT.Copy)\
                    .then_inc(*s_hi_ready.tick(h))
                split_at[0] += 1

        late = []

        def run_late():
            while late:
                late.pop(0)()
                act.wait_ge(*so_far())

        def bank(u, bi):
            act.wait_ge(s_gemm, s_gemm.at(("blk", u.id, bi)))
            return banks[bank_of[(u.id, bi)]]

        def square_y(l, which, m):
            t = t_of(l)
            if which == "mix":
                act.wait_ge(s_y_copy, s_y_copy.at((l, m // 2, m % 2)))
            else:
                act.wait_ge(s_f_add, s_f_add.at((l, 3, m // 2, m % 2)))
            if m >= 2:
                act.wait_ge(s_acc, s_acc.at(("p", l, which, m - 2)))
            f(SQ[m % 2][:, t[0]:t[1]], YM[:, m, t[0]:t[1]], ACT.Square, scale=2 * D ** -0.5).then_inc(*s_sq.tick(("p", l, which, m)))

        xp_turn = [0]
        sh_turn = [0]

        def unit(u):
            splits(2 * u.id + 3)
            act.wait_ge(*so_far())
            run_late()
            if u.kind != "proj":
                splits(2 * u.id + AHEAD)
            act.wait_ge(*so_far())
            kind = u.kind
            if kind == "mod":
                n = mod_no[u.key]

                def row(u=u, n=n):
                    if n >= 3:
                        act.wait_ge(s_mod_col, s_mod_col.at(mods[n - 3]))
                    act.wait_ge(s_gemm, s_gemm.at(("blk", u.id, 1)))
                    f(mrow[n % 3][0:4, :], banks[bank_of[(u.id, 0)]][0:4, 0:256], ACT.Copy).then_inc(*s_mod_row.tick(u.key))

                late.append(row)
            elif kind == "win":
                l, part = u.key
                if part == "val":
                    return
                for bi, (c0, m) in enumerate(u.blocks):
                    b = bank(u, bi)
                    t = u.t[bi]
                    ps = b[0:m, 0:t[1] - t[0]]
                    key = s_u_out.tick
                    if part == "kv" and bi == 0:
                        f(CK, ps, ACT.Copy).then_inc(*key(u.key + (bi,)))
                    elif part == "kv":
                        f(KR[64:96, :], ps, ACT.Copy).then_inc(*key(u.key + (bi,)))
                    elif part in ("q", "gc", "gb"):
                        dst = {"q": QC, "gc": GC, "gb": GB}[part]
                        f(dst[:, bi, t[0]:t[1]], ps, ACT.Copy).then_inc(*key(u.key + (bi,)))
                    elif part in ("z0", "z1"):
                        f(ZS[:, 2 * int(part[1]) + bi, t[0]:t[1]], ps, ACT.Silu).then_inc(*key(u.key + (bi,)))
                    elif part == "bc" and bi == 2:
                        f(dtT[0:16, :], ps, ACT.Copy).then_inc(*key(u.key + (bi,)))
                    else:
                        j = 4 + bi if part == "bc" else 2 * int(part[2]) + bi
                        act.wait_ge(s_pads, s_pads.at(l))
                        if xp_turn[0] >= 2:
                            act.wait_ge(s_conv, s_conv.at(xp_turn[0] - 2))
                        f(XP[xp_turn[0] % 2][:, :, 1:257], ps.rearrange("p (s t) -> p s t", s=2), ACT.Copy)\
                            .then_inc(*key(u.key + (bi,)))

                        def silu(l=l, j=j, n=xp_turn[0]):
                            act.wait_ge(s_conv, s_conv.at(n))
                            f(XC[:, j, :], CV[n % 2], ACT.Silu, bias=vec(l, "ssd_conv_b", j)).then_inc(*s_xc.tick((l, j), ("n", n)))

                        late.append(silu)
                        xp_turn[0] += 1
            elif kind == "wout":
                l, i = u.key
                for m in (2 * i, 2 * i + 1):
                    late.append(lambda l=l, m=m: square_y(l, "mix", m))
            elif kind == "ff1":
                l, g, i = u.key
                t = t_of(l)
                sl = slice(t[0], t[1])
                for bi in (0, 1):
                    j = 2 * i + bi
                    b = bank(u, bi)
                    if j >= 2:
                        act.wait_ge(s_fq, s_fq.at((l, g, j - 2)))
                    elif g > 0:
                        act.wait_ge(s_fq, s_fq.at((l, g - 1, 6 + j)))
                    f(R32[j % 2][:, sl], b[:, 0:t[1] - t[0]], ACT.Relu).then_inc(*s_relu.tick(u.key + (bi,)))
                for bi in (0, 1):
                    j = 2 * i + bi
                    act.wait_ge(s_relu, s_relu.at(u.key + (bi,)))
                    f(FH[:, j, sl], R32[j % 2][:, sl], ACT.Square).then_inc(*s_fh.tick((l, g, j)))
            elif kind == "ff2":
                l, g, i = u.key
                if g == 3:
                    for m in (2 * i, 2 * i + 1):
                        late.append(lambda l=l, m=m: square_y(l, "ffn", m))
            elif kind in ("aq", "ak") or kind == "bkv":
                for bi in ((0, 1) if kind != "bkv" else (0,)):
                    b = bank(u, bi)
                    key = u.key + ((kind, bi) if kind != "bkv" else ("kb", 0))
                    if sh_turn[0] >= 2:
                        act.wait_ge(s_rope2, s_rope2.at(("n", sh_turn[0] - 2)))
                    for q in range(4):
                        o = q ^ 1
                        ins = f(SH[sh_turn[0] % 2][32 * q:32 * q + 32, :], b[32 * o:32 * o + 32, 0:SEQ], ACT.Copy)
                    ins.then_inc(*s_sh2.tick(key))
                    sh_turn[0] += 1
                if kind == "bkv":
                    for tt in (0, 1):
                        b = bank(u, 1)
                        b = banks[bank_of[(u.id, 1 + tt)]]
                        src = b[:, 0:P].rearrange("p (h d) -> p h d", h=2)
                        for dup in (0, 1):
                            ins = f(AV[0][:, 0:2, tt, 64 * dup:64 * dup + 64], src, ACT.Copy)
                        ins.then_inc(*s_vb2.tick(tt))
            elif kind == "av":
                i, hq, g = u.key
                if hq >= 2:
                    act.wait_ge(s_o2, s_o2.at((i, 4 * (hq - 2) + 3)))
                for bi in (0, 1):
                    f(AV[hq % 2][:, g, bi, :], bank(u, bi)[:, 0:256], ACT.Copy).then_inc(*s_v2.tick(u.key + (bi,)))
            elif kind == "az":
                i, hq, g = u.key
                if hq >= 2:
                    act.wait_ge(s_ya, s_ya.at((i, 4 * (hq - 2) + 3)))
                for bi in (0, 1):
                    f(AZ[hq % 2][:, bi, :], bank(u, bi)[:, 0:SEQ], ACT.Silu).then_inc(*s_z2.tick(u.key + (bi,)))
            elif kind == "proj":
                i, part = u.key
                for n in range(4):
                    if n == 2:
                        splits(2 * u.id + 3)
                    m = 4 * part + n
                    f(PJ[:, m, :], bank(u, n)[:, 0:SEQ], ACT.Copy).then_inc(*s_pj.tick((i, m)))
                splits(2 * u.id + AHEAD)
            elif kind == "gate":
                i, j = u.key
                for bi in (0, 1):
                    m = 2 * j + bi
                    if m >= 2:
                        act.wait_ge(s_gmul, s_gmul.at((i, m - 2)))
                    f(SH[m % 2], bank(u, bi)[:, 0:SEQ], ACT.Sigmoid).then_inc(*s_sg.tick(u.key + (bi,)))
                    if i == 0:
                        def part(m=m):
                            act.wait_ge(s_x2_new, s_x2_new.at((0, m)))
                            f(parts2("x2", 1)[0][:, m, :], XT[:, m, SEQ:T], ACT.Copy).then_inc(*s_x2_hi.tick((1, m)))

                        late.append(part)

        def init():
            rows(2)

        def rows(i):
            n = VEC_ROWS if i < 2 else VEC2_ROWS
            act.wait_ge(s_init_t, s_init_t.at(("vec", i)))
            f(VT[i][:, 0:n], banks[bank_of[("vec", i)]][:, 0:n], ACT.Copy).then_inc(*s_vt.tick(i))

        def init_x():
            run_late()
            for k in range(KC):
                act.wait_ge(s_init_t, s_init_t.at(("x", k)))
                f(XT[:, k, :], banks[bank_of[("x", k)]], ACT.Copy).then_inc(*s_xt.tick(k))

        def silu_c():
            act.wait_ge(s_vt, s_vt.at(2))
            f(cs32, VT[2][:, 0:16].rearrange("p (c k) -> p c k", c=2), ACT.Silu).then_inc(*s_cs32.tick(0))
            act.wait_ge(s_cs32, s_cs32.at(0))
            f(cs[:, :, 0:2], cs32.rearrange("p c k -> p k c"), ACT.Copy).then_inc(*s_cs_hi.tick(0))

        def half_root(summed, key, src, dst, eps):
            act.wait_ge(summed, summed.at(key))
            f(dst, src, ACT.Abs_reciprocal_sqrt, bias=eps_c[:, eps:eps + 1]).then_inc(*s_rs.tick(key))

        def norm_sum(l, which):
            t = ALL if which == "mix" else t_of(l)
            sl = slice(t[0], t[1])
            for k in range(KC):
                if (l, which) == (0, "mix"):
                    act.wait_ge(s_xt, s_xt.at(k))
                else:
                    act.wait_ge(s_x_new, s_x_new.at((l, "mix", k) if which == "ffn" else (l - 1, "ffn", k)))
                if k >= 2:
                    act.wait_ge(s_norm_sum, s_norm_sum.at(("n", l, which, k - 2)))
                f(SQ[k % 2][:, sl], XT[:, k, sl], ACT.Square, scale=2 * D ** -0.5).then_inc(*s_sq.tick(("n", l, which, k)))
            half_root(s_norm_sum, ("n", l, which), banks[7][:, 0:t[1] - t[0]], RS[:, sl], 0)

        def norm(l, which):
            t = ALL if which == "mix" else t_of(l)
            a = 0 if which == "mix" else 3 * KC
            act.wait_ge(s_fused, s_fused.at((l, which)))
            for k in range(KC):
                scaled = s_xn if k % 2 == 0 else s_xn_pool
                act.wait_ge(scaled, scaled.at((l, "n", which, k)))
                for s, ts_ in segs(t):
                    ins = f(HH[:, k, ts_], XN[k % 4][:, ts_], ACT.Identity, scale=fA[:, k, 1 - s:2 - s], bias=modT[l][:, a + k, 1 - s:2 - s])
                ins.then_inc(*s_hh.tick((l, which, k)))

        def post(l, which):
            f(small[0:1, 60:61], small[0:1, 61:62], ACT.Abs_reciprocal_sqrt, bias=eps_c[0:1, 0:1])
            run_late()
            t = t_of(l)
            half_root(s_norm_sum, ("p", l, which), banks[7][:, 0:t[1] - t[0]], RS[:, t[0]:t[1]], 0)

        def mla_square(l):
            run_late()
            t = t_of(l)
            sl = slice(t[0], t[1])
            n = t[1] - t[0]
            act.wait_ge(s_u_out, s_u_out.at((l, "q", 1)))
            f(RSM[:, 0, :], CK, ACT.Square, scale=2 * KV_LORA ** -0.5).then_inc(*s_mla_sq.tick((l, 0)))
            for j in (0, 1):
                f(SQM[:, j, sl], QC[:, j, sl], ACT.Square, scale=2 * Q_LORA ** -0.5).then_inc(*s_mla_sq.tick((l, 1 + j)))

        def mla_norm(l):
            t = t_of(l)
            sl = slice(t[0], t[1])
            n = t[1] - t[0]
            half_root(s_mla_sum, ("mla", l, "kv"), banks[3][:, 0:T], RSM[:, 1, :], 0)
            half_root(s_mla_sum, ("mla", l, "q"), banks[4][:, 0:n], RSM[:, 0, sl], 0)

        def mla_proj(l):
            t = t_of(l)
            sl = slice(t[0], t[1])
            act.wait_ge(s_gemm, s_gemm.at(("blk", last_win[l], 1)))
            for h in range(MLA_HEADS):
                act.wait_ge(s_mla_q, s_mla_q.at((l, h)))
                f(QT[0:QK, h, sl], banks[3 + h][0:QK, 0:t[1] - t[0]], ACT.Copy).then_inc(*s_qt.tick((l, h)))
            for h in range(MLA_HEADS):
                act.wait_ge(s_mla_k, s_mla_k.at((l, h)))
                f(KT[0:NOPE, h, :], banks[3 + h][0:NOPE, 0:T], ACT.Copy).then_inc(*s_kt.tick((l, h)))
            for j in range(4):
                act.wait_ge(s_mla_v, s_mla_v.at((l, j)))
                f(VV[:, j, :], banks[(7, 3, 4, 5)[j]][:, 0:256], ACT.Copy).then_inc(*s_vv.tick((l, j)))
            act.wait_ge(s_kr_rope, s_kr_rope.at(l))
            for h in range(MLA_HEADS):
                ins = f(KT[NOPE:QK, h, :], KR[64:96, :], ACT.Copy)
            ins.then_inc(*s_mla_kr.tick(l))

        def mla_att(att, i):
            if 1 < i < len(att) + 2:
                nt = 4 if att[i - 2][2] else 2
                if i >= 4:
                    act.wait_ge(s_mla_o, s_mla_o.at(att[i - 4]))
                for j in (0, 1):
                    act.wait_ge(s_mla_t, s_mla_t.at((att[i - 2], j)))
                    f(PT[i % 2][:, 0:nt, j * P:(j + 1) * P], banks[5 + j][:, 0:nt * P].rearrange("p (k q) -> p k q", q=P),
                      ACT.Copy).then_inc(*s_mla_pt.tick((att[i - 2], j)))
            if i < len(att):
                nk = T if att[i][2] else SEQ
                for j in (0, 1):
                    act.wait_ge(s_mla_mx, s_mla_mx.at((att[i], j)))
                    c = 8 * (i % 2)
                    f(PR[i % 2][j][:, 0:nk], banks[3 + j][:, 0:nk], ACT.Exp, bias=small[:, c + 2 + j:c + 3 + j], scale=MLA_SCALE,
                      accum_out=small[:, c + 4 + j:c + 5 + j]).then_inc(*s_mla_e.tick((att[i], j)))

        def ssd_dt(l):
            act.wait_ge(s_ab, s_ab.at(l))
            f(EX, AB, ACT.Exp, scale=-1.0).then_inc(*s_ex.tick(l))
            f(AA[:, 0, :], a_log[:, l, :], ACT.Exp).then_inc(*s_aa.tick(l))

        def ssd_cs(l):
            act.wait_ge(s_df, s_df.at(l))
            f(WW, DF, ACT.Exp).then_inc(*s_ww.tick(l))
            for d in (0, 1):
                r = slice(64 * d, 64 * d + 64)
                ins = f(DEC[r], banks[6][r, 32 * d:32 * d + 32].rearrange("p (c h) -> p c h", c=4), ACT.Exp)
            ins.then_inc(*s_dec.tick(l))
            act.wait_ge(s_ssd_a, s_ssd_a.at((l, "cst")))
            f(CST[0:16, :], banks[7][0:16, :], ACT.Copy).then_inc(*s_cst.tick(l))

        def ssd_tok(l):
            act.wait_ge(s_sc, s_sc.at((l, 1)))
            act.wait_ge(s_mla_y, s_mla_y.at(mla_last[l]))
            for j in (4, 0, 1, 2, 3):
                act.wait_ge(s_ssd_tk, s_ssd_tk.at((l, j)))
                f(XTK[:, :, j * P:(j + 1) * P], banks[3 + j % 2].rearrange("p (c f) -> p c f", c=4), ACT.Copy)\
                    .then_inc(*s_xtk.tick((l, j)))

        def ssd_g(l):
            act.wait_ge(s_xc, s_xc.at((l, 5)))
            for g in (0, 1):
                for d in (0, 1):
                    ins = f(CTd[64 * d:64 * d + 64, g, :], XC[64 * g:64 * g + 64, 5, :], ACT.Copy)
            ins.then_inc(*s_ctd.tick(l))
            for g in (0, 1):
                act.wait_ge(s_ssd_gt, s_ssd_gt.at((l, g)))
                f(GT[:, g, :], banks[5 + 2 * g], ACT.Copy).then_inc(*s_gt.tick((l, g)))

        def ssd_state(l, c):
            act.wait_ge(s_ssd_st, s_ssd_st.at((l, c, 1)))
            f(ST[:, c, :], banks[3 + c % 2], ACT.Copy).then_inc(*s_st.tick((l, c)))

        def ssd_head(l, h):
            cc = range(CHUNKS) if l == 0 else range(2, 4)
            t0 = cc[0] * P
            if h < SSD_HEADS:
                if h >= 2:
                    act.wait_ge(s_ssd_m, s_ssd_m.at((l, h - 2)))
                    act.wait_ge(s_ce, s_ce.at((l, h - 2)))
                for d in (0, 1):
                    r = slice(64 * d, 64 * d + 64)
                    act.wait_ge(s_ssd_row, s_ssd_row.at((l, h, d)))
                    f(ec[h % 2][r, t0:T], banks[3 + d][r, 0:T - t0], ACT.Exp).then_inc(*s_ecs.tick((l, h, d)))
                for d in (0, 1):
                    act.wait_ge(s_ed, s_ed.at((l, h, d)))
                    act.wait_ge(s_ncs, s_ncs.at(l))
                    for c in cc:
                        e = EE[d][h % 2][:, c * P:(c + 1) * P]
                        ins = f(e, e, ACT.Exp, bias=NCS[:, c, 8 * d + h:8 * d + h + 1])
                    ins.then_inc(*s_ee.tick((l, h, d)))

        def ssd_out(l):
            t = t_of(l)
            sl = slice(t[0], t[1])
            act.wait_ge(s_ssd_ys, s_ssd_ys.at((l, SSD_HEADS - 1)))
            for k in range(4):
                f(HH[:, k, sl], YM[:, k, sl], ACT.Copy).then_inc(*s_yh.tick((l, k)))
            for j in range(4):
                act.wait_ge(s_gz, s_gz.at((l, j)))
                f(SQS[:, j, sl], YM[:, 4 + j, sl], ACT.Square, scale=2 * 256 ** -0.5).then_inc(*s_ssd_sq.tick((l, j)))
            for g in (0, 1):
                half_root(s_ssd_sum, ("ssd", l, g), banks[3 + g][:, 0:t[1] - t[0]], RSS[:, g, sl], 0)

        def y_split(l):
            t = t_of(l)
            sl = slice(t[0], t[1])
            for k in range(4, KC):
                act.wait_ge(s_ssd_yn, s_ssd_yn.at((l, k - 4)))
                f(HH[:, k, sl], YM[:, k, sl], ACT.Copy).then_inc(*s_yh.tick((l, k)))

        def att2(ih):
            i, h = ih
            G = 3 if i == 0 else 1
            c = 16 + 16 * (h % 2)
            p_ = AP_[h % 2]
            for j, (a, n) in enumerate(((0, G * P), (G * P, G * SEQ))):
                act.wait_ge(s_mx2, s_mx2.at((ih, 2 + j)))
                f(p_[:, a:a + n], p_[:, a:a + n], ACT.Exp, bias=small[:, c + 2 + j:c + 3 + j], scale=SCALE,
                  accum_out=small[:, c + 4 + j:c + 5 + j]).then_inc(*s_e2.tick((ih, j)))
                if i == 1:
                    f(small[:, c + 8 + j:c + 9 + j], sinks[:, h:h + 1], ACT.Exp, bias=small[:, c + 2 + j:c + 3 + j])\
                        .then_inc(*s_e2.tick((ih, j), (ih, "sink", j)))

        def att2_turn(ih):
            i, h = ih
            G = 3 if i == 0 else 1
            prev = before_head[ih]
            if prev:
                act.wait_ge(s_o2, s_o2.at(prev))
            for n in range((G * 384 + 511) // 512):
                w = min(512, G * 384 - 512 * n)
                act.wait_ge(s_t2, s_t2.at((ih, n)))
                f(APT[:, 512 * n:512 * n + w], banks[6 if n % 2 == 0 else 7][:, 0:w], ACT.Copy).then_inc(*s_pt2.tick((ih, n)))

        def att2_y(ih):
            i, h = ih
            if h % 4 == 3:
                act.wait_ge(s_ya, s_ya.at(ih))
                for b in (0, 1):
                    k = 2 * (h // 4) + b
                    f(parts2("y2", i)[0][:, k, :], YA[(h // 4) % 2][:, b, :], ACT.Copy).then_inc(*s_y2_hi.tick((i, k)))

        act.wait_ge(s_ones, s_ones.at(1))
        for st in steps:
            kind, args = st[0], st[1:]
            act.wait_ge(*so_far())
            if kind == "unit":
                unit(args[0])
            elif kind == "init":
                init()
            elif kind == "init_x":
                init_x()
            elif kind == "silu_c":
                silu_c()
            elif kind == "mod_flush":
                run_late()
            elif kind == "norm_sum":
                norm_sum(*args)
            elif kind == "consts":
                engine.wait_ge(consts_in, 16 * CONSTS)
                run_late()
                rows(0)
                rows(1)
                f(sel_r[0:48], sel[0:48], ACT.Copy).then_inc(*s_sel.tick(0))
            elif kind == "norm":
                norm(*args)
            elif kind == "post":
                post(*args)
            elif kind == "mla_square":
                mla_square(*args)
            elif kind == "mla_norm":
                mla_norm(*args)
            elif kind == "mla_proj":
                mla_proj(*args)
            elif kind == "mla_att":
                mla_att(*args)
            elif kind == "ssd_dt":
                ssd_dt(*args)
            elif kind == "ssd_cs":
                ssd_cs(*args)
            elif kind == "ssd_tok":
                ssd_tok(*args)
            elif kind == "ssd_g":
                ssd_g(*args)
            elif kind == "ssd_state":
                ssd_state(*args)
            elif kind == "ssd_head":
                ssd_head(*args)
            elif kind == "ssd_out":
                ssd_out(*args)
            elif kind == "y_split":
                y_split(*args)
            elif kind == "split2":
                for k in range(KC):
                    act.wait_ge(s_x_new, s_x_new.at((1, "ffn", k)))
                    f(HA[:, k, :], XT[:, k, SEQ:T], ACT.Copy).then_inc(*s_x2_hi.tick((0, k)))
            elif kind == "att2":
                newest, next_, oldest = args
                if next_:
                    att2_turn(next_)
                if newest:
                    att2(newest)
                if oldest:
                    att2_y(oldest)
            elif kind == "p_split":
                i = args[0]
                act.wait_ge(s_p_t, s_p_t.at(i))
                f(PH, banks[6].rearrange("p (k t) -> p k t", k=2), ACT.Copy).then_inc(*s_p_hi.tick(i))
            elif kind == "ln_sum":
                i = args[0]
                act.wait_ge(s_ln_total, s_ln_total.at((i, "mean")))
                f(SH[0], banks[7][:, 0:SEQ], ACT.Copy, scale=1.0 / D).then_inc(*s_ln_stat.tick((i, "mean")))
                for k in range(KC):
                    act.wait_ge(s_ln_d, s_ln_d.at((i, k)))
                    f(SQ8[:, k, :], V32[:, k, :], ACT.Square, scale=2 * D ** -0.5).then_inc(*s_ln_sq.tick((i, k)))
            elif kind == "ln":
                i = args[0]
                f(small[0:1, 60:61], small[0:1, 61:62], ACT.Abs_reciprocal_sqrt, bias=eps_c[0:1, 0:1])
                half_root(s_ln_total, ("ln", i), banks[7][:, 0:SEQ], SH[1], 1)
                for k in range(KC):
                    act.wait_ge(s_ln_v, s_ln_v.at((i, k)))
                    f(parts2("g2", i)[0][:, k, :], V32[:, k, :], ACT.Identity, bias=vec2(f"ln_b{i}", k)).then_inc(*s_g2_hi.tick((i, k)))
                for k in range(KC):
                    f(XT[:, k, SEQ:T], V32[:, k, :], ACT.Identity, bias=vec2(f"ln_b{i}", k)).then_inc(*s_ln_x.tick((i, k)))
            elif kind == "out":
                run_late()
                for j in (0, 1):
                    for half in (0, 1):
                        act.wait_ge(s_out_t, s_out_t.at((j, half)))
                        f(YO[j][:, 512 * half:512 * half + 512], banks[3 + half], ACT.Copy).then_inc(*s_out_rows.tick((j, half)))

    @ctx_block.vector
    def _(engine):
        dve = Waits(engine)
        v = nc.vector
        Signal.newest[0] = None
        split_at = [0]

        def splits(upto):
            while split_at[0] <= min(upto, N_HALF - 1):
                h = split_at[0]
                u = units[h // 2]
                dve.wait_ge(s_hi_ready, s_hi_ready.at(h))
                n = half_size(u)
                v.tensor_tensor(wlo[h % HALF_SLOTS][:, 0:n], raw[u.id % RAW_SLOTS][:, (h % 2) * n:(h % 2) * n + n],
                                whi[h % HALF_SLOTS][:, 0:n].bitcast(F32), ALU.subtract).then_inc(*s_lo_ready.tick(h))
                split_at[0] += 1

        late = []

        def run_late():
            while late:
                late.pop(0)()
                dve.wait_ge(*so_far())

        def chain(ins):
            ins.then_inc(*s_dve_chain.tick(s_dve_chain.n))
            dve.wait_ge(*so_far())

        def bank(u, bi):
            dve.wait_ge(s_gemm, s_gemm.at(("blk", u.id, bi)))
            return banks[bank_of[(u.id, bi)]]

        def rest(dst, src, hi, ready):
            v.tensor_tensor(dst, src, hi.bitcast(F32), ALU.subtract).then_inc(*ready)

        def add_square(key, k, sl):
            dve.wait_ge(s_sq, s_sq.at(key + (k,)))
            if k == 0:
                ins = v.tensor_copy(ACC[:, sl], SQ[0][:, sl])
            else:
                dve.wait_ge(s_acc, s_acc.at(key + (k - 1,)))
                ins = v.tensor_tensor(ACC[:, sl], ACC[:, sl], SQ[k % 2][:, sl], ALU.add)
            ins.then_inc(*s_acc.tick(key + (k,)))

        xp_turn = [0]
        sh_turn = [0]

        def unit(u):
            splits(2 * u.id + 3)
            dve.wait_ge(*so_far())
            run_late()
            if u.kind != "proj":
                splits(2 * u.id + AHEAD)
            dve.wait_ge(*so_far())
            kind = u.kind
            if kind == "mod":
                n = mod_no[u.key]
                if n >= 2:
                    late.append(lambda: mod_flush(mods[n - 2]))
            elif kind == "win":
                l, part = u.key
                if part == "val":
                    for bi in (0, 1):
                        t = u.t[bi]
                        b = bank(u, bi)
                        dve.wait_ge(s_u_out, s_u_out.at((l, "gc", bi)))
                        dve.wait_ge(s_pads, s_pads.at(l))
                        s0, ns = (0, 2) if l == 0 else (1, 1)
                        v.tensor_tensor(TP[:, bi, s0:2, 1:257], b[:, 0:t[1] - t[0]].rearrange("p (s t) -> p s t", s=ns),
                                        GC[:, bi, t[0]:t[1]].rearrange("p (s t) -> p s t", s=ns), ALU.mult)\
                            .then_inc(*s_val.tick((l, "val", bi)))
                elif part in ("bc", "xs0", "xs1"):
                    for bi in (0, 1):
                        j = 4 + bi if part == "bc" else 2 * int(part[2]) + bi
                        n = xp_turn[0]
                        dve.wait_ge(s_u_out, s_u_out.at(u.key + (bi,)))
                        if n >= 2:
                            dve.wait_ge(s_xc, s_xc.at(("n", n - 2)))
                        conv(l, "ssd_conv_w", j, 6, XP[n % 2], CV[n % 2].rearrange("p (s t) -> p s t", s=2), s_conv, n)
                        xp_turn[0] += 1
            elif kind == "wout":
                l, i = u.key
                t = t_of(l)
                sl = slice(t[0], t[1])
                for bi in (0, 1):
                    m = 2 * i + bi
                    v.tensor_copy(YM[:, m, sl], bank(u, bi)[:, 0:t[1] - t[0]]).then_inc(*s_y_copy.tick(u.key + (bi,)))
                    late.append(lambda m=m: add_square(("p", l, "mix"), m, sl))
            elif kind == "ff1":
                l, g, i = u.key
                t = t_of(l)
                sl = slice(t[0], t[1])
                for bi in (0, 1):
                    j = 2 * i + bi
                    dve.wait_ge(s_relu, s_relu.at(u.key + (bi,)))
                    v.tensor_tensor(FQ[j % 2][:, sl], R32[j % 2][:, sl], R32[j % 2][:, sl], ALU.mult).then_inc(*s_fq.tick((l, g, j)))
                for bi in (0, 1):
                    j = 2 * i + bi
                    dve.wait_ge(s_fh, s_fh.at((l, g, j)))
                    dve.wait_ge(s_fq, s_fq.at((l, g, j)))
                    rest(FL[:, j, sl], FQ[j % 2][:, sl], FH[:, j, sl], s_parts_f.tick((l, g, j)))
            elif kind == "ff2":
                l, g, i = u.key
                t = t_of(l)
                sl = slice(t[0], t[1])
                for bi in (0, 1):
                    m = 2 * i + bi
                    b = bank(u, bi)[:, 0:t[1] - t[0]]
                    if g == 0:
                        ins = v.tensor_copy(YM[:, m, sl], b)
                    else:
                        dve.wait_ge(s_f_add, s_f_add.at((l, g - 1, i, bi)))
                        ins = v.tensor_tensor(YM[:, m, sl], YM[:, m, sl], b, ALU.add)
                    ins.then_inc(*s_f_add.tick(u.key + (bi,)))
                    if g == 3:
                        late.append(lambda m=m: add_square(("p", l, "ffn"), m, sl))
            elif kind in ("aq", "ak", "bkv"):
                for bi in ((0, 1) if kind != "bkv" else (0,)):
                    n = sh_turn[0]
                    b = bank(u, bi)
                    key = u.key + ((kind, bi) if kind != "bkv" else ("kb", 0))
                    i, hq, g = (1, 0, 0) if kind == "bkv" else u.key
                    dve.wait_ge(s_sh2, s_sh2.at(key))
                    v.tensor_tensor(RR[n % 2], b[:, 0:SEQ], rope[:, 0, :], ALU.mult).then_inc(*s_cos2.tick(key))
                    v.tensor_tensor(SH[n % 2], SH[n % 2], rope[:, 1, :], ALU.mult).then_inc(*s_sin2.tick(n))
                    dve.wait_ge(s_cos2, s_cos2.at(key))
                    dve.wait_ge(s_sin2, s_sin2.at(n))
                    if kind != "bkv":
                        if hq >= 2:
                            dve.wait_ge(s_s2, s_s2.at((i, 4 * (hq - 2) + 3)))
                        dst = (AQ if kind == "aq" else AK)[hq % 2]
                        v.tensor_tensor(dst[:, g, bi, :], RR[n % 2], SH[n % 2], ALU.add)\
                            .then_inc(*s_rope2.tick(key, ("n", n)))
                    else:
                        for kv in (0, 1):
                            for dup in (0, 1):
                                r, o = slice(64 * kv, 64 * kv + 64), slice(64 * dup, 64 * dup + 64)
                                ins = v.tensor_tensor(AK[0][o, 0, kv, :], RR[n % 2][r], SH[n % 2][r], ALU.add)
                        ins.then_inc(*s_rope2.tick(key, ("n", n)))
                    sh_turn[0] += 1
            elif kind == "out2":
                i, j = u.key
                for bi in (0, 1):
                    m = 2 * j + bi
                    v.scalar_tensor_tensor(out=V32[:, m, :], in0=XT[:, m, SEQ:T], scalar=ALPHA, in1=bank(u, bi)[:, 0:SEQ],
                                           op0=ALU.mult, op1=ALU.add).then_inc(*s_v32.tick(u.key + (bi,)))

                    def add(i=i, m=m):
                        dve.wait_ge(s_v32, s_v32.at((i, m // 2, m % 2)))
                        if m == 0:
                            ins = v.tensor_copy(RR[0], V32[:, 0, :])
                        else:
                            dve.wait_ge(s_ln_acc, s_ln_acc.at((i, "mean", m - 1)))
                            ins = v.tensor_tensor(RR[0], RR[0], V32[:, m, :], ALU.add)
                        ins.then_inc(*s_ln_acc.tick((i, "mean", m), *([(i, "mean")] if m == KC - 1 else [])))

                    late.append(add)
            elif kind == "proj":
                splits(2 * u.id + AHEAD)
            elif kind == "gate":
                i, j = u.key
                for bi in (0, 1):
                    m = 2 * j + bi
                    dve.wait_ge(s_sg, s_sg.at(u.key + (bi,)))
                    dve.wait_ge(s_pj, s_pj.at((i, m)))
                    dve.wait_ge(s_ln_x, s_ln_x.at((i, m)))
                    v.tensor_tensor(RR[m % 2], SH[m % 2], PJ[:, m, :], ALU.mult).then_inc(*s_gmul.tick((i, m)))
                    dve.wait_ge(s_gmul, s_gmul.at((i, m)))
                    v.tensor_tensor(XT[:, m, SEQ:T], XT[:, m, SEQ:T], RR[m % 2], ALU.add).then_inc(*s_x2_new.tick((i, m)))
                    if i == 0:
                        def part(m=m):
                            dve.wait_ge(s_x2_hi, s_x2_hi.at((1, m)))
                            dve.wait_ge(s_x2_new, s_x2_new.at((0, m)))
                            hi, lo = parts2("x2", 1)
                            rest(lo[:, m, :], XT[:, m, SEQ:T], hi[:, m, :], s_parts2.tick((1, m)))

                        late.append(part)

        def conv(l, name, j, blocks, src, dst, signal, key, s0=0):
            dve.wait_ge(s_vt, s_vt.at(l))
            w = [vec(l, name, blocks * k + j) for k in range(3)]
            chain(v.tensor_scalar(dst, src[:, s0:2, 0:256], w[0], None, ALU.mult))
            chain(v.scalar_tensor_tensor(out=dst, in0=src[:, s0:2, 1:257], scalar=w[1], in1=dst, op0=ALU.mult, op1=ALU.add))
            ins = v.scalar_tensor_tensor(out=dst, in0=src[:, s0:2, 2:258], scalar=w[2], in1=dst, op0=ALU.mult, op1=ALU.add)
            if signal is None:
                chain(ins)
            else:
                ins.then_inc(*signal.tick(key))

        flushed = set()

        def mod_flush(key):
            if key in flushed:
                return
            flushed.add(key)
            l, i = key
            dve.wait_ge(s_mod_col, s_mod_col.at(key))
            v.tensor_reduce(modT[l][:, 2 * i:2 * i + 2, :], banks[bank_of[("mod_t", key)]][:, 0:8].rearrange("p (b h c) -> p b c h", b=2, h=2), AX.X, ALU.add)\
                .then_inc(*s_mod_t.tick(key))

        def mod_fuse(l, part):
            dve.wait_ge(s_vt, s_vt.at(l))
            a, n, last_key = {"mix": (0, 16, (l, 7)), "g1": (16, 8, (l, 11)), "ffn": (24, 16, (l, 19)), "g2": (40, 8, (l, 23))}[part]
            dve.wait_ge(s_mod_t, s_mod_t.at(last_key))
            m = modT[l][:, a:a + n, :]
            chain(v.tensor_tensor(m, m, bc(vec(l, "b_mod", a, n).unsqueeze(2), [P, n, 2]), ALU.add))
            if part in ("mix", "ffn"):
                g = vec(l, "g_pre_mix" if part == "mix" else "g_pre_ffn", 0, KC)
                v.scalar_tensor_tensor(out=fA, in0=modT[l][:, a + KC:a + 2 * KC, :], scalar=1.0, in1=bc(g.unsqueeze(2), [P, KC, 2]),
                                       op0=ALU.add, op1=ALU.mult).then_inc(*s_fused.tick((l, part)))
            else:
                g = vec(l, "g_post_mix" if part == "g1" else "g_post_ffn", 0, KC)
                v.tensor_tensor(fG, m, bc(g.unsqueeze(2), [P, KC, 2]), ALU.mult).then_inc(*s_fused.tick((l, part)))

        def refine(key, src, h, tmp, eps):
            dve.wait_ge(s_rs, s_rs.at(key))
            chain(v.scalar_tensor_tensor(out=tmp, in0=h, scalar=-1.0, in1=h, op0=ALU.mult, op1=ALU.mult))
            chain(v.scalar_tensor_tensor(out=tmp, in0=src, scalar=4 * eps, in1=tmp, op0=ALU.add, op1=ALU.mult))
            v.scalar_tensor_tensor(out=h, in0=tmp, scalar=3.0, in1=h, op0=ALU.add, op1=ALU.mult).then_inc(*s_inv.tick(key))

        def norm_sum(l, which):
            t = ALL if which == "mix" else t_of(l)
            sl = slice(t[0], t[1])
            refine(("n", l, which), banks[7][:, 0:t[1] - t[0]], RS[:, sl], ACC[:, sl], EPS)

        def norm(l, which):
            t = ALL if which == "mix" else t_of(l)
            sl = slice(t[0], t[1])
            dve.wait_ge(s_fused, s_fused.at((l, which)))
            dve.wait_ge(s_inv, s_inv.at(("n", l, which)))
            a = 0 if which == "mix" else 3 * KC

            def low(k):
                dve.wait_ge(s_hh, s_hh.at((l, which, k)))
                dve.wait_ge(s_h32, s_h32.at((l, which, k)))
                rest(HL[:, k, sl], H32[k % 2][:, sl], HH[:, k, sl], s_parts.tick((l, which, k)))

            for k in range(KC):
                if k >= 4:
                    dve.wait_ge(s_hh, s_hh.at((l, which, k - 4)))
                if k % 2 == 0:
                    v.tensor_tensor(XN[k % 4][:, sl], XT[:, k, sl], RS[:, sl], ALU.mult).then_inc(*s_xn.tick((l, "n", which, k)))
                if k >= 2:
                    low(k - 2)
                    dve.wait_ge(*so_far())
                scaled = s_xn if k % 2 == 0 else s_xn_pool
                dve.wait_ge(scaled, scaled.at((l, "n", which, k)))
                for s, ts_ in segs(t):
                    ins = v.tensor_scalar(H32[k % 2][:, ts_], XN[k % 4][:, ts_], fA[:, k, 1 - s:2 - s], modT[l][:, a + k, 1 - s:2 - s],
                                          ALU.mult, ALU.add)
                ins.then_inc(*s_h32.tick((l, which, k)))
            low(KC - 2)
            low(KC - 1)

        def split2(k):
            dve.wait_ge(s_x_new, s_x_new.at((LAYERS - 1, "ffn", k)))
            dve.wait_ge(s_x2_hi, s_x2_hi.at((0, k)))
            rest(LA_[:, k, :], XT[:, k, SEQ:T], HA[:, k, :], s_parts2.tick((0, k)))

        def post(l, which):
            run_late()
            t = t_of(l)
            sl = slice(t[0], t[1])
            refine(("p", l, which), banks[7][:, 0:t[1] - t[0]], RS[:, sl], ACC[:, sl], EPS)
            dve.wait_ge(s_fused, s_fused.at((l, "g1" if which == "mix" else "g2")))
            dve.wait_ge(s_inv, s_inv.at(("p", l, which)))
            for k in range(KC):
                if k % 2 == 0:
                    if k >= 4:
                        dve.wait_ge(s_x_new, s_x_new.at((l, which, k - 4)))
                    v.tensor_tensor(XN[k % 4][:, sl], YM[:, k, sl], RS[:, sl], ALU.mult).then_inc(*s_xn.tick((l, "p", which, k)))
                scaled = s_xn if k % 2 == 0 else s_xn_pool
                dve.wait_ge(scaled, scaled.at((l, "p", which, k)))
                for s, ts_ in segs(t):
                    ins = v.scalar_tensor_tensor(out=XT[:, k, ts_], in0=XN[k % 4][:, ts_], scalar=fG[:, k, 1 - s:2 - s],
                                                 in1=XT[:, k, ts_], op0=ALU.mult, op1=ALU.add)
                ins.then_inc(*s_x_new.tick((l, which, k)))
                if (l, which) == (LAYERS - 1, "ffn") and k >= 2:
                    split2(k - 2)

        def mla_norm(l):
            t = t_of(l)
            sl = slice(t[0], t[1])
            dve.wait_ge(s_u_out, s_u_out.at((l, "kv", 1)))
            rotate(KR[64:96, SEQ:T].unsqueeze(1), TMP0[64:96, 0:SEQ].unsqueeze(1), 1)
            v.tensor_copy(small[0:1, 63:64], small[0:1, 62:63]).then_inc(*s_kr_rope.tick(l))
            refine(("mla", l, "kv"), banks[3][:, 0:T], RSM[:, 1, :], TMP0, EPS)
            dve.wait_ge(s_inv, s_inv.at(("mla", l, "kv")))
            v.scalar_tensor_tensor(out=CK, in0=CK, scalar=vec(l, "mla_kv_norm"), in1=RSM[:, 1, :], op0=ALU.mult, op1=ALU.mult)\
                .then_inc(*s_mla_n.tick((l, "kv")))
            refine(("mla", l, "q"), banks[4][:, 0:t[1] - t[0]], RSM[:, 0, sl], TMP1[:, sl], EPS)
            dve.wait_ge(s_inv, s_inv.at(("mla", l, "q")))
            for j in (0, 1):
                ins = v.scalar_tensor_tensor(out=QC[:, j, sl], in0=QC[:, j, sl], scalar=vec(l, "mla_q_norm", j), in1=RSM[:, 0, sl],
                                             op0=ALU.mult, op1=ALU.mult)
            ins.then_inc(*s_mla_n.tick((l, "q")))

        def rotate(a, tmp, n):
            cos = bc(axial[64:96, 0:1, :], [32, n, SEQ])
            sin = bc(axial[64:96, 1:2, :], [32, n, SEQ])
            swap = [(i + 8) if (i // 8) % 2 == 0 else (i - 8) for i in range(32)]
            for j in range(n):
                chain(v.stream_shuffle(tmp[:, j, :], a[:, j, :], swap))
            chain(v.tensor_tensor(tmp, tmp, sin, ALU.mult))
            chain(v.tensor_tensor(a, a, cos, ALU.mult))
            chain(v.tensor_tensor(a, a, tmp, ALU.add))

        def mla_proj(l):
            dve.wait_ge(s_gemm, s_gemm.at(("blk", last_win[l], 1)))
            dve.wait_ge(s_qt, s_qt.at((l, MLA_HEADS - 1)))
            rotate(QT[64:96, :, SEQ:T], ROT[64:96], MLA_HEADS)
            v.tensor_copy(small[0:1, 63:64], small[0:1, 62:63]).then_inc(*s_mla_qr.tick(l))

        def mla_att(att, i):
            if i < len(att):
                nk = T if att[i][2] else SEQ
                c = 8 * (i % 2)
                for j in (0, 1):
                    dve.wait_ge(s_mla_s, s_mla_s.at((att[i], j)))
                    chain(v.tensor_reduce(small[:, c + j:c + j + 1], banks[3 + j][:, 0:nk], AX.X, ALU.max))
                    v.tensor_scalar(small[:, c + 2 + j:c + 3 + j], small[:, c + j:c + j + 1], -MLA_SCALE, None, ALU.mult)\
                        .then_inc(*s_mla_mx.tick((att[i], j)))
            if i > 2:
                l, h, sg = att[i - 3]
                dve.wait_ge(s_mla_o, s_mla_o.at(att[i - 3]))
                r = slice(64 * (h % 2), 64 * (h % 2) + 64)
                v.tensor_copy(YM[r, h // 2, SEQ * sg:SEQ * sg + SEQ], banks[7][r, 0:SEQ]).then_inc(*s_mla_y.tick(att[i - 3]))
            if i < len(att):
                for j in (0, 1):
                    dve.wait_ge(s_mla_e, s_mla_e.at((att[i], j)))
                    chain(v.reciprocal(small[:, c + 6 + j:c + 7 + j], small[:, c + 4 + j:c + 5 + j]))
                    v.tensor_scalar(PR[i % 2][j][:, 0:nk], PR[i % 2][j][:, 0:nk], small[:, c + 6 + j:c + 7 + j], None, ALU.mult)\
                        .then_inc(*s_mla_p.tick((att[i], j)))

        def short_conv(l):
            t = t_of(l)
            s0 = 0 if l == 0 else 1
            for j in (0, 1):
                dve.wait_ge(s_val, s_val.at((l, "val", j)))
                y = YM[:, 2 + j, t[0]:t[1]]
                conv(l, "sc_conv_w", j, 2, TP[:, j], y.rearrange("p (s t) -> p s t", t=SEQ), None, None, s0)
                dve.wait_ge(s_u_out, s_u_out.at((l, "gb", j)))
                v.tensor_tensor(y, y, GB[:, j, t[0]:t[1]], ALU.mult).then_inc(*s_sc.tick((l, j)))

        def ssd_dt(l):
            dve.wait_ge(s_ssd_a, s_ssd_a.at((l, "dt")))
            ps = banks[5][:, 0:64].rearrange("p (c h) -> p c h", c=4)
            v.tensor_tensor(XR, ps, bc(dt_bias[:, l:l + 1, :], [P, 4, 16]), ALU.add).then_inc(*s_xr.tick(l))
            dve.wait_ge(s_xr, s_xr.at(l))
            v.scalar_tensor_tensor(out=AB, in0=XR, scalar=-1.0, in1=XR, op0=ALU.mult, op1=ALU.max).then_inc(*s_ab.tick(l))
            dve.wait_ge(s_ex, s_ex.at(l))
            chain(v.tensor_scalar(DN, EX, 2.0, None, ALU.add))
            chain(v.reciprocal(RD, DN))
            chain(v.tensor_tensor(Z1, EX, RD, ALU.mult))
            chain(v.tensor_tensor(Z2, Z1, Z1, ALU.mult))
            chain(v.tensor_scalar(PL, Z2, 1.0 / (2 * LOG1P_TERMS - 1), None, ALU.mult))
            for n in range(LOG1P_TERMS - 2, 0, -1):
                chain(v.scalar_tensor_tensor(out=PL, in0=PL, scalar=1.0 / (2 * n + 1), in1=Z2, op0=ALU.add, op1=ALU.mult))
            chain(v.scalar_tensor_tensor(out=PL, in0=PL, scalar=1.0, in1=Z1, op0=ALU.add, op1=ALU.mult))
            chain(v.tensor_scalar(PL, PL, 2.0, None, ALU.mult))
            chain(v.scalar_tensor_tensor(out=DT, in0=XR, scalar=0.0, in1=PL, op0=ALU.max, op1=ALU.add))
            dve.wait_ge(s_aa, s_aa.at(l))
            v.scalar_tensor_tensor(out=LA, in0=DT, scalar=-1.0, in1=bc(AA[:, 0:1, :], [P, 4, 16]), op0=ALU.mult, op1=ALU.mult)\
                .then_inc(*s_la.tick(l))

        def ssd_cs(l):
            dve.wait_ge(s_ssd_a, s_ssd_a.at((l, "cs")))
            for d in (0, 1):
                ins = v.tensor_copy(CS[:, :, 8 * d:8 * d + 8], banks[5][:, 32 * d:32 * d + 32].rearrange("p (c h) -> p c h", c=4))
            ins.then_inc(*s_cs_tok.tick(l))
            dve.wait_ge(s_cs_tok, s_cs_tok.at(l))
            v.tensor_scalar(NCS, CS, -1.0, None, ALU.mult).then_inc(*s_ncs.tick(l))
            dve.wait_ge(s_ssd_a, s_ssd_a.at((l, "last")))
            dve.wait_ge(s_cs_tok, s_cs_tok.at(l))
            for d in (0, 1):
                ins = v.tensor_tensor(DF[:, :, 8 * d:8 * d + 8], banks[6][:, 32 * d:32 * d + 32].rearrange("p (c h) -> p c h", c=4),
                                      CS[:, :, 8 * d:8 * d + 8], ALU.subtract)
            ins.then_inc(*s_df.tick(l))
            dve.wait_ge(s_ww, s_ww.at(l))
            v.tensor_tensor(WW, WW, DT, ALU.mult).then_inc(*s_wd.tick(l))
            dve.wait_ge(s_cst, s_cst.at(l))
            v.tensor_tensor(CST[32:48, :], banks[7][0:16, :], CST[0:16, :].bitcast(F32), ALU.subtract).then_inc(*s_cst_lo.tick(l))

        def ssd_state(l, c):
            for g in (0, 1):
                dve.wait_ge(s_xtk, s_xtk.at((l, 4)))
                dve.wait_ge(s_wd, s_wd.at(l))
                dve.wait_ge(s_mla_y, s_mla_y.at(mla_last[l]))
                b = XTK[:, c, 512 + 64 * g:512 + 64 * g + 64].unsqueeze(1)
                w = WW[:, c, :].rearrange("p (d g h) -> p g h d", d=2, g=2)[:, g]
                for d in (0, 1):
                    o = Bd[c][g].rearrange("p (h d n) -> p h d n", h=4, d=2)[:, :, d, :]
                    ins = v.tensor_tensor(o, bc(b, [P, 4, 64]), bc(w[:, :, d].unsqueeze(2), [P, 4, 64]), ALU.mult)
                ins.then_inc(*s_bd.tick((l, c, g)))

        def ssd_rec(l):
            dve.wait_ge(s_dec, s_dec.at(l))
            runs = ((slice(0, 64), (0, 1, 2, 3)), (slice(64, 128), (1, 0, 3, 2)))
            dve.wait_ge(s_sin0, s_sin0.at(l))
            for r, order in runs:
                dve.wait_ge(s_st, s_st.at((l, order[0])))
                ins = v.tensor_copy(Sin[r, order[1], :], ST[r, order[0], :])
            ins.then_inc(*s_rec0.tick(l))
            dve.wait_ge(s_rec0, s_rec0.at(l))
            r, order = runs[0]
            for n in (1, 2):
                a, b = order[n], order[n + 1]
                chain(v.tensor_tensor(Sin[r, b, :].rearrange("p (h d) -> p h d", h=8), Sin[r, a, :].rearrange("p (h d) -> p h d", h=8),
                                      bc(DEC[r, a, :].unsqueeze(2), [64, 8, 64]), ALU.mult))
                dve.wait_ge(s_st, s_st.at((l, a)))
                ins = v.tensor_tensor(Sin[r, b, :], Sin[r, b, :], ST[r, a, :], ALU.add)
                if n == 1:
                    chain(ins)
                else:
                    ins.then_inc(*s_rec.tick(l))

        def ssd_head(l, h):
            cc = range(CHUNKS) if l == 0 else range(2, 4)
            t0 = cc[0] * P
            if h < SSD_HEADS:
                dve.wait_ge(s_gt, s_gt.at((l, 1)))
                dve.wait_ge(s_ctd, s_ctd.at(l))
                for d in (0, 1):
                    dve.wait_ge(s_ecs, s_ecs.at((l, h, d)))
                    v.tensor_tensor(EE[d][h % 2][:, t0:T].rearrange("p (c t) -> p c t", t=P),
                                    banks[3 + d][:, 0:T - t0].rearrange("p (c t) -> p c t", t=P),
                                    bc(tri_neg[:, d:d + 1, :], [P, len(cc), P]), ALU.add).then_inc(*s_ed.tick((l, h, d)))
            if 0 < h <= SSD_HEADS:
                g = h - 1
                if g >= 2:
                    dve.wait_ge(s_ssd_y, s_ssd_y.at((l, g - 2)))
                m = MM_[g % 2]
                dve.wait_ge(s_ee, s_ee.at((l, g, 0)))
                for c in cc:
                    ins = v.tensor_scalar(m[:, c * P:(c + 1) * P], EE[0][g % 2][:, c * P:(c + 1) * P], DT[:, c, g:g + 1], None, ALU.mult)
                chain(ins)
                dve.wait_ge(s_ee, s_ee.at((l, g, 1)))
                for c in cc:
                    ins = v.scalar_tensor_tensor(out=m[:, c * P:(c + 1) * P], in0=EE[1][g % 2][:, c * P:(c + 1) * P],
                                                 scalar=DT[:, c, 8 + g:9 + g], in1=m[:, c * P:(c + 1) * P], op0=ALU.mult, op1=ALU.add)
                ins.then_inc(*s_ssd_m.tick((l, g)))
            if h > 1:
                g = h - 2
                dve.wait_ge(s_ssd_y, s_ssd_y.at((l, g)))
                r = slice(64 * (g % 2), 64 * (g % 2) + 64)
                v.scalar_tensor_tensor(out=YM[r, 4 + g // 2, t0:T], in0=XC[r, g // 2, t0:T], scalar=d_skip[r, l, g // 2:g // 2 + 1],
                                       in1=banks[5 if g % 2 else 7][r, 0:T - t0], op0=ALU.mult, op1=ALU.add)\
                    .then_inc(*s_ssd_ys.tick((l, g)))

        def ssd_out(l):
            t = t_of(l)
            sl = slice(t[0], t[1])
            dve.wait_ge(s_ssd_ys, s_ssd_ys.at((l, SSD_HEADS - 1)))
            for j in range(4):
                v.tensor_tensor(YM[:, 4 + j, sl], YM[:, 4 + j, sl], ZS[:, j, sl], ALU.mult).then_inc(*s_gz.tick((l, j)))
            for k in range(4):
                dve.wait_ge(s_yh, s_yh.at((l, k)))
                rest(HL[:, k, sl], YM[:, k, sl], HH[:, k, sl], s_parts_y.tick((l, k)))
            for g in (0, 1):
                refine(("ssd", l, g), banks[3 + g][:, 0:t[1] - t[0]], RSS[:, g, sl], SQS[:, 2 * g, sl], EPS)
            for j in range(4):
                dve.wait_ge(s_inv, s_inv.at(("ssd", l, j // 2)))
                y = YM[:, 4 + j, sl]
                v.scalar_tensor_tensor(out=y, in0=y, scalar=vec(l, "ssd_norm", j), in1=RSS[:, j // 2, sl], op0=ALU.mult, op1=ALU.mult)\
                    .then_inc(*s_ssd_yn.tick((l, j)))

        def y_split(l):
            t = t_of(l)
            sl = slice(t[0], t[1])
            dve.wait_ge(s_ssd_yn, s_ssd_yn.at((l, 3)))
            for k in range(4, KC):
                dve.wait_ge(s_yh, s_yh.at((l, k)))
                rest(HL[:, k, sl], YM[:, k, sl], HH[:, k, sl], s_parts_y.tick((l, k)))

        def att2(ih):
            i, h = ih
            G = 3 if i == 0 else 1
            c = 16 + 16 * (h % 2)
            p_ = AP_[h % 2]
            mask = mask_a if i == 0 else mask_b
            if ih == (0, 0):
                engine.wait_ge(masks_in, 64)
            dve.wait_ge(s_s2, s_s2.at(ih))
            if before_head[before_head[ih]]:
                before = before_head[before_head[ih]]
                dve.wait_ge(s_t2, s_t2.at((before, 2 if before[0] == 0 else 0)))
            parts = ((0, G * P, banks[3]), (G * P, G * SEQ, wide))
            for j, (a, n, ps) in enumerate(parts):
                v.tensor_tensor_reduce(out=p_[:, a:a + n], in0=ps[:, 0:n], in1=mask[:, a:a + n], scale=1.0, scalar=-3e38,
                                       op0=ALU.add, op1=ALU.max, accum_out=small[:, c + j:c + j + 1])\
                    .then_inc(*s_mx2.tick((ih, j)))
            dve.wait_ge(s_mx2, s_mx2.at((ih, 1)))
            if i == 1:
                chain(v.tensor_scalar(small[:, c:c + 2], small[:, c:c + 2], sinks8[:, h:h + 1], None, ALU.max))
            v.tensor_scalar(small[:, c + 2:c + 4], small[:, c:c + 2], -SCALE, None, ALU.mult)\
                .then_inc(*s_mx2.tick((ih, 2), (ih, 3)))
            dve.wait_ge(s_e2, s_e2.at((ih, 1)))
            if i == 1:
                chain(v.tensor_tensor(small[:, c + 4:c + 6], small[:, c + 4:c + 6], small[:, c + 8:c + 10], ALU.add))
            chain(v.reciprocal(small[:, c + 6:c + 8], small[:, c + 4:c + 6]))
            for j, (a, n, ps) in enumerate(parts):
                v.tensor_scalar(p_[:, a:a + n], p_[:, a:a + n], small[:, c + 6 + j:c + 7 + j], None, ALU.mult)\
                    .then_inc(*s_p2.tick((ih, j)))

        def att2_y(ih):
            i, h = ih
            blk = (h % 4) // 2
            r = slice(64 * (h % 2), 64 * (h % 2) + 64)
            buf = (h // 4) % 2
            dve.wait_ge(s_o2, s_o2.at(ih))
            dve.wait_ge(s_z2, s_z2.at((i, h // 4, 0, blk)))
            if h % 4 == 0 and h >= 8:
                dve.wait_ge(s_y2_hi, s_y2_hi.at((i, 2 * (h // 4 - 2) + 1)))
            v.tensor_tensor(YA[buf][r, blk, :], banks[7][r, 0:SEQ], AZ[buf][r, blk, :], ALU.mult).then_inc(*s_ya.tick(ih))

        def att2_y_low(ih):
            i, h = ih
            if h % 4 == 3:
                buf = (h // 4) % 2
                hi, lo = parts2("y2", i)
                for b in (0, 1):
                    k = 2 * (h // 4) + b
                    dve.wait_ge(s_y2_hi, s_y2_hi.at((i, k)))
                    rest(lo[:, k, :], YA[buf][:, b, :], hi[:, k, :], s_parts_y2.tick((i, k)))

        dve.wait_ge(s_ones, s_ones.at(1))
        for at_step, st in enumerate(steps):
            kind, args = st[0], st[1:]
            dve.wait_ge(*so_far())
            if kind == "unit":
                unit(args[0])
            elif kind == "silu_c":
                dve.wait_ge(s_cs_hi, s_cs_hi.at(0))
                v.tensor_tensor(cs[:, :, 2:4], cs32.rearrange("p c k -> p k c"), cs[:, :, 0:2].bitcast(F32), ALU.subtract)\
                    .then_inc(*s_cs.tick(0))
            elif kind == "mod_flush":
                for key in mods:
                    if at_step > mod_step[key] and key not in flushed:
                        mod_flush(key)
            elif kind == "mod_fuse":
                mod_fuse(*args)
            elif kind == "norm_sum":
                norm_sum(*args)
            elif kind == "consts":
                engine.wait_ge(consts_in, 16 * CONSTS)
                v.tensor_scalar(sinks8, sinks, 1.0 / SCALE, None, ALU.mult).then_inc(*s_sinks8.tick(0))
            elif kind == "norm":
                norm(*args)
            elif kind == "post":
                post(*args)
            elif kind == "mla_norm":
                run_late()
                mla_norm(*args)
            elif kind == "mla_proj":
                mla_proj(*args)
            elif kind == "mla_att":
                mla_att(*args)
            elif kind == "short_conv":
                short_conv(*args)
            elif kind == "ssd_dt":
                ssd_dt(*args)
            elif kind == "ssd_cs":
                ssd_cs(*args)
            elif kind == "ssd_g":
                for c in range(CHUNKS):
                    ssd_state(args[0], c)
            elif kind == "ssd_rec":
                ssd_rec(*args)
            elif kind == "ssd_head":
                ssd_head(*args)
            elif kind == "ssd_out":
                ssd_out(*args)
            elif kind == "y_split":
                y_split(*args)
            elif kind == "split2":
                for k in (KC - 2, KC - 1):
                    split2(k)
            elif kind == "att2":
                newest, next_, oldest = args
                if oldest:
                    att2_y(oldest)
                if newest:
                    att2(newest)
                if oldest:
                    att2_y_low(oldest)
            elif kind == "p_split":
                i = args[0]
                dve.wait_ge(s_p_hi, s_p_hi.at(i))
                v.tensor_tensor(PL_, banks[6].rearrange("p (k t) -> p k t", k=2), PH.bitcast(F32), ALU.subtract)\
                    .then_inc(*s_p_lo.tick(i))
            elif kind == "ln_sum":
                i = args[0]
                run_late()
                dve.wait_ge(s_ln_stat, s_ln_stat.at((i, "mean")))
                for k in range(KC):
                    v.tensor_tensor(V32[:, k, :], V32[:, k, :], SH[0], ALU.subtract).then_inc(*s_ln_d.tick((i, k)))
            elif kind == "ln":
                i = args[0]
                refine(("ln", i), banks[7][:, 0:SEQ], SH[1], RR[1], LN_EPS)
                dve.wait_ge(s_inv, s_inv.at(("ln", i)))
                hi, lo = parts2("g2", i)
                for k in range(KC + 1):
                    if k < KC:
                        v.scalar_tensor_tensor(out=V32[:, k, :], in0=V32[:, k, :], scalar=vec2(f"ln_g{i}", k), in1=SH[1],
                                               op0=ALU.mult, op1=ALU.mult).then_inc(*s_ln_v.tick((i, k)))
                    if k > 0:
                        dve.wait_ge(s_ln_v, s_ln_v.at((i, k - 1)))
                        dve.wait_ge(s_g2_hi, s_g2_hi.at((i, k - 1)))
                        v.scalar_tensor_tensor(out=lo[:, k - 1, :], in0=V32[:, k - 1, :], scalar=vec2(f"ln_b{i}", k - 1),
                                               in1=hi[:, k - 1, :].bitcast(F32), op0=ALU.add, op1=ALU.subtract)\
                            .then_inc(*s_parts_g2.tick((i, k - 1)))

    @ctx_block.gpsimd
    def _(engine):
        pool = Waits(engine)
        Signal.newest[0] = None
        nc.gpsimd.memset(ones, 1.0).then_inc(*s_ones.tick(0))
        nc.gpsimd.memset(eps_c[:, 0:1], 4 * EPS)
        nc.gpsimd.memset(eps_c[:, 1:2], 4 * LN_EPS)
        nc.gpsimd.memset(small, 0.0).then_inc(*s_ones.tick(1))
        for l in range(LAYERS):
            for name, (r, m) in VEC.items():
                src = A[name][l]
                if name in ("sc_conv_w", "ssd_conv_w"):
                    src = src.rearrange("a (b p) -> (a b) p", p=P)
                else:
                    src = src.rearrange("(a p) -> a p", p=P)
                nc.gpsimd.dma_start(vrow[r:r + m, l, :], src).then_inc(rows_in, 16)
        for st in steps:
            kind, args = st[0], st[1:]
            pool.wait_ge(*so_far())
            if kind == "norm":
                l, which = args
                t = ALL if which == "mix" else t_of(l)
                sl = slice(t[0], t[1])
                pool.wait_ge(s_inv, s_inv.at(("n", l, which)))
                for k in range(1, KC, 2):
                    pool.wait_ge(*so_far())
                    if k >= 4:
                        pool.wait_ge(s_hh, s_hh.at((l, which, k - 4)))
                        pool.wait_ge(s_h32, s_h32.at((l, which, k - 4)))
                    nc.gpsimd.tensor_tensor(XN[k % 4][:, sl], XT[:, k, sl], RS[:, sl], ALU.mult)\
                        .then_inc(*s_xn_pool.tick((l, "n", which, k)))
                if which == "mix":
                    if l > 0:
                        pool.wait_ge(s_x_new, s_x_new.at((l - 1, "ffn", KC - 1)))
                    nc.gpsimd.memset(CST[0:48].bitcast(F32), 0.0)
                    nc.gpsimd.memset(XP0, 0.0)
                    nc.gpsimd.memset(XP1, 0.0)
                    nc.gpsimd.memset(TP, 0.0).then_inc(*s_pads.tick(l))
            elif kind == "post":
                l, which = args
                t = t_of(l)
                sl = slice(t[0], t[1])
                pool.wait_ge(s_inv, s_inv.at(("p", l, which)))
                for k in range(1, KC, 2):
                    pool.wait_ge(*so_far())
                    if k >= 4:
                        pool.wait_ge(s_x_new, s_x_new.at((l, which, k - 4)))
                    nc.gpsimd.tensor_tensor(XN[k % 4][:, sl], YM[:, k, sl], RS[:, sl], ALU.mult)\
                        .then_inc(*s_xn_pool.tick((l, "p", which, k)))
            elif kind == "ssd_rec":
                l = args[0]
                pool.wait_ge(s_dec, s_dec.at(l))
                pool.wait_ge(s_rec0, s_rec0.at(l))
                r = slice(64, 128)
                for a, b in ((0, 3), (3, 2)):
                    pool.wait_ge(*so_far())
                    nc.gpsimd.tensor_tensor(Sin[r, b, :].rearrange("p (h d) -> p h d", h=8), Sin[r, a, :].rearrange("p (h d) -> p h d", h=8),
                                            bc(DEC[r, a, :].unsqueeze(2), [64, 8, 64]), ALU.mult).then_inc(*s_rec_back.tick((l, "decayed", a)))
                    pool.wait_ge(s_rec_back, s_rec_back.at((l, "decayed", a)))
                    pool.wait_ge(s_st, s_st.at((l, a)))
                    nc.gpsimd.tensor_tensor(Sin[r, b, :], Sin[r, b, :], ST[r, a, :], ALU.add)\
                        .then_inc(*s_rec_back.tick((l, "added", a), *([l] if a == 3 else [])))
            elif kind == "ssd_g":
                l = args[0]
                pool.wait_ge(s_sc, s_sc.at((l, 1)))
                pool.wait_ge(s_mla_y, s_mla_y.at(mla_last[l]))
                nc.gpsimd.memset(Sin[0:64, 0, :], 0.0)
                nc.gpsimd.memset(Sin[64:128, 1, :], 0.0).then_inc(*s_sin0.tick(l))
            elif kind == "ssd_head":
                l, h = args
                t0 = t_of(l)[0]
                if 0 < h <= SSD_HEADS:
                    g = h - 1
                    m = MM_[g % 2]
                    pool.wait_ge(s_gt, s_gt.at((l, 1)))
                    pool.wait_ge(s_ssd_m, s_ssd_m.at((l, g)))
                    nc.gpsimd.tensor_tensor(m[:, t0:T], m[:, t0:T], GT[:, g // 4, t0:T], ALU.mult).then_inc(*s_mg.tick((l, g)))
                if h < SSD_HEADS:
                    pool.wait_ge(*so_far())
                    pool.wait_ge(s_ctd, s_ctd.at(l))
                    pool.wait_ge(s_ecs, s_ecs.at((l, h, 1)))
                    if h >= 2:
                        pool.wait_ge(s_ssd_y, s_ssd_y.at((l, h - 2)))
                    nc.gpsimd.tensor_tensor(Ce[h % 2][:, t0:T], CTd[:, h // 4, t0:T], ec[h % 2][:, t0:T], ALU.mult)\
                        .then_inc(*s_ce.tick((l, h)))

    block.__exit__(None, None, None)
    return {name: s.mine for name, s in signals.items()}


_INS = ['x', 'c', 'ctx', 'c_ctx', 'w_mod', 'b_mod', 'g_pre_mix', 'w_in', 'mla_q_norm', 'w_uq', 'mla_kv_norm', 'w_ukv',
        'sc_conv_w', 'ssd_conv_w', 'ssd_conv_b', 'ssd_a_log', 'ssd_dt_bias', 'ssd_d', 'ssd_norm', 'w_out',
        'g_post_mix', 'g_pre_ffn', 'w_ff1', 'w_ff2', 'g_post_ffn', 'p_2', 'a_w_in_2', 'a_w_out_2', 'b_w_in_2',
        'b_sinks_2', 'b_w_out_2', 'ln_g_2', 'ln_b_2', 'ple_w_proj_2', 'ple_w_gate_2']


def kernel(**inputs):
    import numpy as _np
    import concourse.bacc as _bacc
    from concourse import mybir as _mybir
    from concourse.bass_utils import run_bass_kernel_spmd as _run

    tables = constants()

    def program(counts):
        nc = _bacc.Bacc("TRN2", target_bir_lowering=False, num_devices=1)
        arrays, A = {}, {}
        for name in _INS:
            a = _np.ascontiguousarray(inputs[name])
            arrays[f"in_{name}_dram"] = a
            A[name] = nc.dram_tensor(f"in_{name}_dram", a.shape, _mybir.dt.from_np(a.dtype), kind="ExternalInput").ap()
        for name, a in tables.items():
            arrays[f"k_{name}_dram"] = a
            A["k_" + name] = nc.dram_tensor(f"k_{name}_dram", a.shape, _mybir.dt.from_np(a.dtype), kind="ExternalInput").ap()
        out = nc.dram_tensor("out_0_dram", (1, SEQ, D), F32, kind="ExternalOutput").ap()
        return nc, arrays, build(nc, A, out, counts)

    _, _, counts = program(None)
    nc, arrays, _ = program(counts)
    r = _run(nc, [arrays], core_ids=[0])
    return r.results[0]["out_0_dram"]
```
